# Optimizing a Trainium2 kernel written in Bass

```python
import math
import jax, jax.numpy as jnp
from jax import lax
import numpy as np

D_MODEL = 1024
BATCH = 1
SEQ = 1024
DEPTH = 1

RET_HEADS = 4
RET_HEAD_DIM = 128
RET_WIDTH = RET_HEADS * RET_HEAD_DIM
RET_CHUNK = 128
SWA_Q_HEADS = 8
SWA_KV_HEADS = 2
SWA_HEAD_DIM = 64
SWA_WIDTH = SWA_Q_HEADS * SWA_HEAD_DIM
SWA_KV_WIDTH = SWA_KV_HEADS * SWA_HEAD_DIM
WINDOW = 128
MIX_WIDTH = RET_WIDTH + SWA_WIDTH
IN_COLS = 4 * RET_WIDTH + SWA_WIDTH + 2 * SWA_KV_WIDTH
ROPE_THETA = 10000.0
PEER_HEADS = 8
PEER_N_KEYS = 128
PEER_N_EXPERTS = PEER_N_KEYS * PEER_N_KEYS
PEER_QUERY_DIM = 256
PEER_HALF = PEER_QUERY_DIM // 2
PEER_TOPK = 16
PEER_TOKEN_BLOCK = 128
LN_EPS = 1e-5
GN_EPS = 1e-6
ALPHA = (2.0 * DEPTH) ** 0.25
BETA = (8.0 * DEPTH) ** -0.25
NEG_INF = -1e30

kernel_name = "hymba_retnet_swa_peer_deepnorm"

def layer_norm(x, w, b):
    xf = x.astype(jnp.float32)
    mu = jnp.mean(xf, axis=-1, keepdims=True)
    var = jnp.mean(jnp.square(xf - mu), axis=-1, keepdims=True)
    return ((xf - mu) * lax.rsqrt(var + LN_EPS) * w.astype(jnp.float32) + b.astype(jnp.float32)).astype(x.dtype)

def head_group_norm(y):
    yf = y.astype(jnp.float32)
    mu = jnp.mean(yf, axis=-1, keepdims=True)
    var = jnp.mean(jnp.square(yf - mu), axis=-1, keepdims=True)
    return ((yf - mu) * lax.rsqrt(var + GN_EPS)).astype(y.dtype)

def rotary(x, pos):
    d = x.shape[-1]
    inv = 1.0 / (ROPE_THETA ** (jnp.arange(0, d, 2, dtype=jnp.float32) / d))
    ang = pos.astype(jnp.float32)[:, None] * inv[None, :]
    cos = jnp.cos(ang)[None, :, None, :]
    sin = jnp.sin(ang)[None, :, None, :]
    xf = x.astype(jnp.float32)
    x1, x2 = xf[..., : d // 2], xf[..., d // 2:]
    out = jnp.concatenate([x1 * cos - x2 * sin, x2 * cos + x1 * sin], axis=-1)
    return out.astype(x.dtype)

def retention(q, k, v):
    B, S, H, d = q.shape
    C = RET_CHUNK
    n = S // C
    dt = q.dtype
    log_g = jnp.log(1.0 - 2.0 ** (-5.0 - jnp.arange(H, dtype=jnp.float32)))
    k = k * (d ** -0.5)
    qc = q.reshape(B, n, C, H, d).transpose(0, 3, 1, 2, 4)
    kc = k.reshape(B, n, C, H, d).transpose(0, 3, 1, 2, 4)
    vc = v.reshape(B, n, C, H, d).transpose(0, 3, 1, 2, 4)
    idx = jnp.arange(C, dtype=jnp.float32)
    diff = idx[:, None] - idx[None, :]
    decay = jnp.where(diff[None] >= 0,
                      jnp.exp(jnp.maximum(diff, 0.0)[None] * log_g[:, None, None]), 0.0).astype(dt)
    zeta = jnp.exp((C - 1.0 - idx)[None] * log_g[:, None]).astype(dt)
    xi = jnp.exp((idx + 1.0)[None] * log_g[:, None]).astype(dt)
    g_chunk = jnp.exp(C * log_g)
    scores = jnp.einsum('bhncd,bhnmd->bhncm', qc, kc) * decay[None, :, None]
    y_intra = jnp.einsum('bhncm,bhnme->bhnce', scores, vc)
    chunk_kv = jnp.einsum('bhnmd,bhnme->bhnde', kc * zeta[None, :, None, :, None], vc)
    kv_seq = jnp.moveaxis(chunk_kv, 2, 0)
    gc = g_chunk.astype(kv_seq.dtype)[None, :, None, None]

    def step(state, kv):
        return state * gc + kv, state

    _, prev = lax.scan(step, jnp.zeros_like(kv_seq[0]), kv_seq)
    prev = jnp.moveaxis(prev, 0, 2)
    y_cross = jnp.einsum('bhncd,bhnde->bhnce', qc * xi[None, :, None, :, None], prev)
    y = (y_intra + y_cross).transpose(0, 2, 3, 1, 4).reshape(B, S, H, d)
    return y

def sliding_window_attention(q, k, v, sinks):
    B, S, Hq, d = q.shape
    Hkv = k.shape[2]
    G = Hq // Hkv
    W = WINDOW
    n = S // W
    qb = q.reshape(B, n, W, Hkv, G, d)
    kb = k.reshape(B, n, W, Hkv, d)
    vb = v.reshape(B, n, W, Hkv, d)
    zk = jnp.zeros_like(kb[:, :1])
    kk = jnp.concatenate([jnp.concatenate([zk, kb[:, :-1]], axis=1), kb], axis=2)
    vv = jnp.concatenate([jnp.concatenate([zk, vb[:, :-1]], axis=1), vb], axis=2)
    s = jnp.einsum('bnqhgd,bnkhd->bnhgqk', qb, kk).astype(jnp.float32) * (d ** -0.5)
    qi = jnp.arange(W)[:, None] + W
    kj = jnp.arange(2 * W)[None, :]
    rel = qi - kj
    blk = jnp.arange(n)
    valid = ((rel >= 0) & (rel < W))[None] & ((blk[:, None, None] > 0) | (kj[None] >= W))
    s = jnp.where(valid[None, :, None, None], s, NEG_INF)
    sink = jnp.broadcast_to(sinks.astype(jnp.float32).reshape(Hkv, G)[None, None, :, :, None, None],
                            s.shape[:-1] + (1,))
    p = jax.nn.softmax(jnp.concatenate([s, sink], axis=-1), axis=-1)[..., :-1]
    o = jnp.einsum('bnhgqk,bnkhd->bnqhgd', p.astype(v.dtype), vv)
    return o.reshape(B, S, Hq, d)

def peer_ffn(x, w_pq, sub_keys, u_tab, v_tab):
    B, S, D = x.shape
    T = B * S
    H, K = PEER_HEADS, PEER_TOPK
    xt = x.reshape(T, D)
    q = (xt @ w_pq).reshape(T, H, 2, PEER_HALF)
    s = jnp.einsum('thpd,hpkd->thpk', q, sub_keys)
    s1, i1 = lax.top_k(s[:, :, 0], K)
    s2, i2 = lax.top_k(s[:, :, 1], K)
    cand = (s1[..., :, None] + s2[..., None, :]).reshape(T, H, K * K)
    cand_idx = (i1[..., :, None] * PEER_N_KEYS + i2[..., None, :]).reshape(T, H, K * K)
    top_s, pos = lax.top_k(cand, K)
    idx = jnp.take_along_axis(cand_idx, pos, axis=-1)
    g = jax.nn.softmax(top_s.astype(jnp.float32), axis=-1).astype(x.dtype)
    c = PEER_TOKEN_BLOCK
    nb = T // c

    def block(args):
        xb, ib, gb = args
        ib = ib.reshape(c, H * K)
        gb = gb.reshape(c, H * K)
        u = jnp.take(u_tab, ib, axis=0)
        a = jax.nn.gelu(jnp.einsum('cd,ced->ce', xb, u), approximate=False) * gb
        vsel = jnp.take(v_tab, ib, axis=0)
        return jnp.einsum('ce,ced->cd', a, vsel)

    y = lax.map(block, (xt.reshape(nb, c, D), idx.reshape(nb, c, H, K), g.reshape(nb, c, H, K)))
    return y.reshape(B, S, D)

def setup_inputs(seed: int = 0) -> dict:
    key = jax.random.key(seed)
    ks = jax.random.split(key, 13)
    f32 = jnp.float32
    col_scale = jnp.concatenate([
        jnp.ones((2 * RET_WIDTH,), f32),
        jnp.full((RET_WIDTH,), BETA, f32),
        jnp.ones((RET_WIDTH,), f32),
        jnp.ones((SWA_WIDTH + SWA_KV_WIDTH,), f32),
        jnp.full((SWA_KV_WIDTH,), BETA, f32),
    ])
    x = jax.random.normal(ks[0], (BATCH, SEQ, D_MODEL), f32)
    w_in = jax.random.normal(ks[1], (DEPTH, D_MODEL, IN_COLS), f32) * (D_MODEL ** -0.5) * col_scale
    ret_gn_w = 1.0 + 0.02 * jax.random.normal(ks[2], (DEPTH, RET_WIDTH), f32)
    swa_sinks = 0.5 * jax.random.normal(ks[3], (DEPTH, SWA_Q_HEADS), f32)
    w_out = jax.random.normal(ks[4], (DEPTH, MIX_WIDTH, D_MODEL), f32) * (MIX_WIDTH ** -0.5) * BETA
    ln1_w = 1.0 + 0.02 * jax.random.normal(ks[5], (DEPTH, D_MODEL), f32)
    ln1_b = 0.02 * jax.random.normal(ks[6], (DEPTH, D_MODEL), f32)
    w_pq = jax.random.normal(ks[7], (DEPTH, D_MODEL, PEER_HEADS * PEER_QUERY_DIM), f32) * (D_MODEL ** -0.5)
    peer_sub_keys = jax.random.normal(ks[8], (DEPTH, PEER_HEADS, 2, PEER_N_KEYS, PEER_HALF), f32) * (PEER_HALF ** -0.5)
    peer_u = jax.random.normal(ks[9], (DEPTH, PEER_N_EXPERTS, D_MODEL), f32) * (D_MODEL ** -0.5) * BETA
    peer_v = jax.random.normal(ks[10], (DEPTH, PEER_N_EXPERTS, D_MODEL), f32) * BETA
    ln2_w = 1.0 + 0.02 * jax.random.normal(ks[11], (DEPTH, D_MODEL), f32)
    ln2_b = 0.02 * jax.random.normal(ks[12], (DEPTH, D_MODEL), f32)
    return {"x": x, "w_in": w_in, "ret_gn_w": ret_gn_w, "swa_sinks": swa_sinks, "w_out": w_out,
            "ln1_w": ln1_w, "ln1_b": ln1_b, "w_pq": w_pq, "peer_sub_keys": peer_sub_keys,
            "peer_u": peer_u, "peer_v": peer_v, "ln2_w": ln2_w, "ln2_b": ln2_b}

def reference(x, w_in, ret_gn_w, swa_sinks, w_out, ln1_w, ln1_b, w_pq, peer_sub_keys,
              peer_u, peer_v, ln2_w, ln2_b):
    B, S, D = x.shape
    pos = jnp.arange(S)
    o1 = RET_WIDTH
    splits = [o1, 2 * o1, 3 * o1, 4 * o1, 4 * o1 + SWA_WIDTH, 4 * o1 + SWA_WIDTH + SWA_KV_WIDTH]
    h = x
    for l in range(DEPTH):
        proj = h @ w_in[l]
        rq, rk, rv, rg, sq, sk, sv = jnp.split(proj, splits, axis=-1)
        rq = rotary(rq.reshape(B, S, RET_HEADS, RET_HEAD_DIM), pos)
        rk = rotary(rk.reshape(B, S, RET_HEADS, RET_HEAD_DIM), pos)
        rv = rv.reshape(B, S, RET_HEADS, RET_HEAD_DIM)
        y_ret = head_group_norm(retention(rq, rk, rv)).reshape(B, S, RET_WIDTH) * ret_gn_w[l]
        y_ret = jax.nn.silu(rg) * y_ret
        sq = rotary(sq.reshape(B, S, SWA_Q_HEADS, SWA_HEAD_DIM), pos)
        sk = rotary(sk.reshape(B, S, SWA_KV_HEADS, SWA_HEAD_DIM), pos)
        sv = sv.reshape(B, S, SWA_KV_HEADS, SWA_HEAD_DIM)
        y_swa = sliding_window_attention(sq, sk, sv, swa_sinks[l]).reshape(B, S, SWA_WIDTH)
        mix = jnp.concatenate([y_ret, y_swa], axis=-1) @ w_out[l]
        h = layer_norm(ALPHA * h + mix, ln1_w[l], ln1_b[l])
        ffn = peer_ffn(h, w_pq[l], peer_sub_keys[l], peer_u[l], peer_v[l])
        h = layer_norm(ALPHA * h + ffn, ln2_w[l], ln2_b[l])
    return h


_drawn_inputs = setup_inputs


def setup_inputs(seed=0):
    import zlib

    import numpy as np

    out = dict(_drawn_inputs(seed))
    spreads = {}
    factors = {'ret_gn_w': 5.7, 'swa_sinks': 8.0, 'ln2_w': 2.829, 'ln2_b': 2.887}
    for name, (base, spread) in spreads.items():
        noise = np.random.default_rng([zlib.crc32(name.encode()), seed]).standard_normal(out[name].shape)
        drawn = base * np.exp(spread * noise) if base else spread * noise
        out[name] = __import__('jax').numpy.asarray(drawn.astype(out[name].dtype))
    for name, factor in factors.items():
        out[name] = (out[name] * factor).astype(out[name].dtype)
    return out
```

```python
from contextlib import ExitStack

import numpy as np
import concourse.bass as bass
from concourse import mybir

F32 = mybir.dt.float32
F32R = mybir.dt.float32r
U32 = mybir.dt.uint32
ACT = mybir.ActivationFunctionType
ALU = mybir.AluOpType
AX = mybir.AxisListType

P = 128
D = 1024
T = 1024
KT = D // P
TB = T // P
RH, RD = 4, 128
RW = RH * RD
QH, KVH, SD = 8, 2, 64
G = QH // KVH
SW, SKV = QH * SD, KVH * SD
COLS = 4 * RW + SW + 2 * SKV
ALPHA = 2.0 ** 0.25
LN_EPS, GN_EPS = 1e-5, 1e-6
PH, NK, TOPK = 8, 128, 16
PAIRS = 2 * PH
NEG = -1e30
LOWEST = -3.0e38
GROUP = 4
GT = 32
NG = NK // GROUP


def bc(ap, axis, n):
    v = ap.unsqueeze(axis)
    shape = list(v.shape)
    shape[axis] = n
    return v.to_broadcast(shape)


class Chain:

    def __init__(self, eng, sem):
        self.eng, self.sem, self.n = eng, sem, 0

    def link(self, ins):
        self.n += 1
        ins.then_inc(self.sem, 1)
        self.eng.wait_ge(self.sem, self.n)

    def restart(self):
        self.eng.wait_ge(self.sem, self.n)
        self.eng.sem_clear(self.sem)
        self.n = 0


def memory(nc, ctx):
    def sb(name, shape, dt=F32):
        return ctx.enter_context(nc.sbuf_tensor(name, shape, dt))

    def bank(name):
        return ctx.enter_context(nc.psum_tensor(name, [P, 512], F32))

    def sem(name):
        return ctx.enter_context(nc.semaphore(name))

    return sb, bank, sem


def project(nc, d):
    chunks = [("rot", 0, 512), ("rot", 512, 512), ("copy", 1024, 512), ("silu", 1536, 512),
              ("rot64", 2048, 512), ("kv", 2560, 256)]
    NB = 4
    OUT = 3
    with ExitStack() as ctx:
        sb, bank, sem = memory(nc, ctx)
        x_raw = sb("x_raw", [P, KT, T])
        x_hi = sb("x_hi", [P, KT, T], F32R)
        x_lo = sb("x_lo", [P, KT, T], F32R)
        w_raw = sb("w_raw", [P, KT, 512])
        w_hi = sb("w_hi", [P, 2, KT, 512], F32R)
        w_lo = sb("w_lo", [P, 2, KT, 512], F32R)
        rope = sb("rope", [P, TB, 2, RD // 2])
        rope64 = sb("rope64", [P, TB, 2, SD // 2])
        t_cos = sb("t_cos", [P, 512])
        t_sin = sb("t_sin", [P, 512])
        res = sb("res", [P, OUT, 512])
        ps = [bank(f"pp{i}") for i in range(NB)]
        x_here = [sem(f"x_here{k}") for k in range(KT)]
        w_here = [sem(f"w_here{k}") for k in range(KT)]
        rope_here = sem("rope_here")
        x_his, x_los = sem("x_his"), sem("x_los")
        w_his, w_los = sem("w_his"), sem("w_los")
        tile_done = sem("tile_done")
        res_act, res_dve = sem("res_act"), sem("res_dve")
        stored = [sem(f"stored{i}") for i in range(OUT)]
        own = sem("own_dve1")
        tiles = [(c, tb) for c in range(len(chunks)) for tb in range(TB)]
        by_act = [chunks[c][0] in ("copy", "silu") for c, _ in tiles]

        def finished(n):
            return (res_act, sum(by_act[:n + 1])) if by_act[n] else (res_dve, n + 1 - sum(by_act[:n + 1]))

        with nc.Block() as block:

            @block.sync
            def _(sp):
                sp.dma_start(rope[:], d["rope"]).then_inc(rope_here, 16)
                sp.dma_start(rope64[:], d["rope64"]).then_inc(rope_here, 16)
                for k in range(KT):
                    sp.dma_start(x_raw[:, k], d["xT"][:, k]).then_inc(x_here[k], 16)
                    sp.dma_start(w_raw[:, k], d["w_in"][:, k, 0:512]).then_inc(w_here[k], 16)
                for n, (c, tb) in enumerate(tiles):
                    if c + 1 < len(chunks):
                        _, c0, w = chunks[c + 1]
                        k = tb
                        sp.wait_ge(w_his, c * KT + k + 1)
                        sp.wait_ge(w_los, c * KT + k + 1)
                        sp.dma_start(w_raw[:, k, 0:w], d["w_in"][:, k, c0:c0 + w]).then_inc(w_here[k], 16)
                    _, c0, w = chunks[c]
                    sp.wait_ge(*finished(n))
                    sp.dma_start(d["proj"][tb * P:(tb + 1) * P, c0:c0 + w],
                                 res[:, n % OUT, 0:w]).then_inc(stored[n % OUT], 16)
                for i in range(OUT):
                    sp.wait_ge(stored[i], 16 * len(range(i, len(tiles), OUT)))

            @block.tensor
            def _(pe):
                for n, (c, tb) in enumerate(tiles):
                    w = chunks[c][2]
                    if n >= NB:
                        pe.wait_ge(*finished(n - NB))
                    for k in range(KT):
                        if tb == 0:
                            if c == 0:
                                pe.wait_ge(x_los, k + 1)
                            pe.wait_ge(w_los, c * KT + k + 1)
                        xh = x_hi[:, k, tb * P:(tb + 1) * P]
                        xl = x_lo[:, k, tb * P:(tb + 1) * P]
                        wh, wl = w_hi[:, c % 2, k, 0:w], w_lo[:, c % 2, k, 0:w]
                        o = ps[n % NB][:, 0:w]
                        nc.tensor.matmul(o, xh, wh, start=(k == 0), stop=False)
                        nc.tensor.matmul(o, xh, wl, start=False, stop=False)
                        last = nc.tensor.matmul(o, xl, wh, start=False, stop=(k == KT - 1))
                    last.then_inc(tile_done, 1)

            @block.scalar
            def _(act):
                def split_w(c, k):
                    w = chunks[c][2]
                    act.wait_ge(w_here[k], 16 * (c + 1))
                    if c >= 2:
                        act.wait_ge(tile_done, TB * (c - 1))
                    nc.scalar.activation(w_hi[:, c % 2, k, 0:w], w_raw[:, k, 0:w], ACT.Copy).then_inc(w_his, 1)

                for k in range(KT):
                    act.wait_ge(x_here[k], 16)
                    nc.scalar.activation(x_hi[:, k], x_raw[:, k], ACT.Copy).then_inc(x_his, 1)
                    split_w(0, k)
                for n, (c, tb) in enumerate(tiles):
                    if c + 1 < len(chunks):
                        split_w(c + 1, tb)
                    if by_act[n]:
                        act.wait_ge(tile_done, n + 1)
                        if n >= OUT:
                            act.wait_ge(stored[n % OUT], 16 * (n // OUT))
                        f = ACT.Silu if chunks[c][0] == "silu" else ACT.Copy
                        nc.scalar.activation(res[:, n % OUT, :], ps[n % NB][:], f).then_inc(res_act, 1)

            @block.vector
            def _(v):
                chain = Chain(v, own)

                def split_w(c, k):
                    w = chunks[c][2]
                    v.wait_ge(w_his, c * KT + k + 1)
                    nc.vector.tensor_tensor(w_lo[:, c % 2, k, 0:w], w_raw[:, k, 0:w],
                                            w_hi[:, c % 2, k, 0:w].bitcast(F32), ALU.subtract).then_inc(w_los, 1)

                def rotate(src, out, cos, sin, heads, half):
                    n = heads * 2 * half
                    s4 = src.rearrange("p (h a f) -> p h a f", h=heads, a=2)
                    c4 = t_cos[:, 0:n].rearrange("p (h a f) -> p h a f", h=heads, a=2)
                    n4 = t_sin[:, 0:n].rearrange("p (h a f) -> p h a f", h=heads, a=2)
                    o4 = out.rearrange("p (h a f) -> p h a f", h=heads, a=2)
                    cosb = bc(bc(cos, 1, 2), 1, heads)
                    sinb = bc(bc(sin, 1, 2), 1, heads)
                    nc.vector.tensor_tensor(c4, s4, cosb, ALU.mult)
                    chain.link(nc.vector.tensor_tensor(n4, s4, sinb, ALU.mult))
                    chain.link(nc.vector.tensor_tensor(o4[:, :, 0], c4[:, :, 0], n4[:, :, 1], ALU.subtract))
                    return nc.vector.tensor_tensor(o4[:, :, 1], c4[:, :, 1], n4[:, :, 0], ALU.add)

                for k in range(KT):
                    v.wait_ge(x_his, k + 1)
                    nc.vector.tensor_tensor(x_lo[:, k], x_raw[:, k], x_hi[:, k].bitcast(F32),
                                            ALU.subtract).then_inc(x_los, 1)
                    split_w(0, k)
                v.wait_ge(rope_here, 32)
                for n, (c, tb) in enumerate(tiles):
                    if c + 1 < len(chunks):
                        split_w(c + 1, tb)
                    if by_act[n]:
                        continue
                    kind = chunks[c][0]
                    v.wait_ge(tile_done, n + 1)
                    if n >= OUT:
                        v.wait_ge(stored[n % OUT], 16 * (n // OUT))
                    if finished(n)[1] > 1:
                        v.wait_ge(res_dve, finished(n)[1] - 1)
                    o = res[:, n % OUT]
                    if kind == "rot":
                        last = rotate(ps[n % NB][:], o, rope[:, tb, 0], rope[:, tb, 1], RH, RD // 2)
                    elif kind == "rot64":
                        last = rotate(ps[n % NB][:], o, rope64[:, tb, 0], rope64[:, tb, 1], QH, SD // 2)
                    else:
                        nc.vector.tensor_copy(o[:, SKV:2 * SKV], ps[n % NB][:, SKV:2 * SKV])
                        last = rotate(ps[n % NB][:, 0:SKV], o[:, 0:SKV], rope64[:, tb, 0], rope64[:, tb, 1],
                                      KVH, SD // 2)
                    last.then_inc(res_dve, 1)


def attend(nc, d, hT_hi, hT_lo):
    with ExitStack() as ctx:
        sb, bank, sem = memory(nc, ctx)
        ident = sb("ident", [P, P])
        decayT = sb("decayT", [P, RH, P])
        zeta, xi = sb("zeta", [P, RH]), sb("xi", [P, RH])
        masks = sb("masks", [P, 2, 2 * P])
        gn_w, sinks = sb("gn_w", [P, RW]), sb("sinks", [P, QH])
        ln_w, ln_b = sb("ln_w", [P, D]), sb("ln_b", [P, D])
        wo_hi, wo_lo = sb("wo_hi", [P, KT, D], F32R), sb("wo_lo", [P, KT, D], F32R)
        minus_half = sb("minus_half", [P, RH])
        pj = sb("pj", [P, COLS])
        rqT, rkT = sb("rqT", [P, RH, P]), sb("rkT", [P, RH, P])
        sqT = sb("sqT", [P, QH // 2, P])
        skT = sb("skT", [P, 2, P])
        v_prev = sb("v_prev", [P, SKV])
        kz = sb("kz", [P, RH, P])
        retT = sb("retT", [P, RH, P])
        state = sb("state", [P, RH, P])
        yr = sb("yr", [P, RH, P])
        stats, mv = sb("stats", [P, RH, 6]), sb("mv", [P, RH, 2])
        gn_var, gn_rstd = sb("gn_var", [P, RH]), sb("gn_rstd", [P, RH])
        sm = sb("sm", [P, QH, 2 * P])
        wo_raw = sm[:].rearrange("p (a h) k -> p a (h k)", a=2)
        mx, neg, sd = sb("mx", [P, QH]), sb("neg", [P, QH]), sb("sd", [P, QH])
        sums, sink_e, den, rden = (sb(n, [P, QH]) for n in ("sums", "sink_e", "den", "rden"))
        pT = sb("pT", [P, QH, 2, P])
        ycat = sb("ycat", [P, D])
        yT_hi, yT_lo = sb("yT_hi", [P, KT, P], F32R), sb("yT_lo", [P, KT, P], F32R)
        hr = sb("hr", [P, D])
        lstats, lmv = sb("lstats", [P, 2, 6]), sb("lmv", [P, 2])
        l_var, l_rstd = sb("l_var", [P, 1]), sb("l_rstd", [P, 1])
        b = [bank(f"pa{i}") for i in range(8)]
        const_here, wo_here = sem("const_here"), [sem("wo_here0"), sem("wo_here1")]
        pj_here, x_here, h_out = sem("pj_here"), sem("x_here"), sem("h_out")
        wo_his, wo_los = sem("wo_his"), sem("wo_los")
        ready = sem("ready")
        qkT, q_evac_a, q_evac_v = sem("qkT"), sem("q_evac_a"), sem("q_evac_v")
        ret_s, swa_s, ret_sT = sem("ret_s"), sem("swa_s"), sem("ret_sT")
        ret_y, ret_used = sem("ret_y"), sem("ret_used")
        masked, negs, exps = sem("masked"), sem("negs"), sem("exps")
        pTs, pT_a, pT_v = sem("pTs"), sem("pT_a"), sem("pT_v")
        pv, y_ready = sem("pv"), sem("y_ready")
        var_here, rstd_here = sem("var_here"), sem("rstd_here")
        yTs, yT_his, yT_los = sem("yTs"), sem("yT_his"), sem("yT_los")
        mixed, mix_read = sem("mixed"), sem("mix_read")
        lvar_here, lrstd_here = sem("lvar_here"), sem("lrstd_here")
        h_ready, hTs, hT_his, hT_los = sem("h_ready"), sem("hTs"), sem("hT_his"), sem("hT_los")
        kept = sem("kept")
        own, own_pool = sem("own_dve2"), sem("own_pool2")

        with nc.Block() as block:

            @block.sync
            def _(sp):
                for t, n in ((ident, "ident"), (decayT, "decayT"), (zeta, "zeta"), (xi, "xi"), (masks, "masks"),
                             (gn_w, "gn_w"), (sinks, "sinks"), (ln_w, "ln1_w"), (ln_b, "ln1_b")):
                    sp.dma_start(t[:], d[n]).then_inc(const_here, 16)

            @block.tensor
            def _(pe):
                def products(out, pairs, start=True):
                    for n, (l, r) in enumerate(pairs):
                        last = nc.tensor.matmul(out, l, r, start=(n == 0), stop=(n == len(pairs) - 1))
                    return last

                pe.wait_ge(const_here, 16 * 9)
                pe.wait_ge(ready, 1)
                with pe.Fori(0, TB) as i:
                    pe.wait_ge(pj_here, (i + 1) * 16)
                    pe.wait_ge(hT_los, i * 2)
                    for h in range(RH):
                        last = nc.tensor.transpose(b[0][:, h * P:(h + 1) * P], pj[:, h * RD:(h + 1) * RD], ident[:])
                    last.then_inc(qkT, 1)
                    for h in range(RH):
                        last = nc.tensor.transpose(b[1][:, h * P:(h + 1) * P],
                                                   pj[:, RW + h * RD:RW + (h + 1) * RD], ident[:])
                    last.then_inc(qkT, 1)
                    for h in range(QH // 2):
                        last = nc.tensor.transpose(b[2][:, h * P:(h + 1) * P],
                                                   pj[:, 4 * RW + h * P:4 * RW + (h + 1) * P], ident[:])
                    last.then_inc(qkT, 1)
                    nc.tensor.transpose(b[3][:, 0:P], pj[:, 4 * RW + SW:4 * RW + SW + SKV], ident[:]).then_inc(qkT, 1)
                    pe.wait_ge(q_evac_a, 2 * i + 1)
                    pe.wait_ge(q_evac_v, 3 * i + 1)
                    for h in range(RH):
                        last = nc.tensor.matmul(b[4][:, h * P:(h + 1) * P], rkT[:, h], rqT[:, h], start=True, stop=True)
                    last.then_inc(ret_s, 1)
                    pe.wait_ge(q_evac_a, 2 * i + 2)
                    pe.wait_ge(q_evac_v, 3 * i + 2)
                    for h in (0, 4, 1, 5, 2, 6, 3, 7):
                        lo = (h // G) * SD
                        last = nc.tensor.matmul(b[h // 2][:, (h % 2) * 256:(h % 2) * 256 + 256],
                                                sqT[lo:lo + SD, h % G], skT[lo:lo + SD].rearrange("p a k -> p (a k)"),
                                                start=True, stop=True)
                        if h % 2:
                            last.then_inc(swa_s, 1)
                    pe.wait_ge(ret_sT, i + 1)
                    pe.wait_ge(q_evac_v, 3 * i + 3)
                    pe.wait_ge(yT_los, i * 2)
                    for h in range(RH):
                        vh = pj[:, 2 * RW + h * RD:2 * RW + (h + 1) * RD]
                        nc.tensor.matmul(b[5][:, h * P:(h + 1) * P], retT[:, h], vh, start=True, stop=True)
                        nc.tensor.matmul(b[6][:, h * P:(h + 1) * P], rqT[:, h], state[:, h], start=True, stop=True)
                        last = nc.tensor.matmul(b[7][:, h * P:(h + 1) * P], kz[:, h], vh, start=True, stop=True)
                    last.then_inc(ret_y, 1)
                    pe.wait_ge(exps, i + 1)
                    for h in range(QH):
                        for a in range(2):
                            n = 2 * h + a
                            last = nc.tensor.transpose(b[n // 4][:, (n % 4) * P:(n % 4 + 1) * P],
                                                       sm[:, h, a * P:(a + 1) * P], ident[:])
                        if h % 2:
                            last.then_inc(pTs, 1)
                    for h in range(QH):
                        if h % 2 == 0:
                            pe.wait_ge(*((pT_a, 2 * i + h // 4 + 1) if h % 4 == 0 else (pT_v, 2 * i + h // 4 + 1)))
                        g = h // G
                        nc.tensor.matmul(b[4][:, h * SD:(h + 1) * SD], pT[:, h, 0], v_prev[:, g * SD:(g + 1) * SD],
                                         start=True, stop=False)
                        last = nc.tensor.matmul(b[4][:, h * SD:(h + 1) * SD], pT[:, h, 1],
                                                pj[:, COLS - SKV + g * SD:COLS - SKV + (g + 1) * SD],
                                                start=False, stop=True)
                    last.then_inc(pv, 1)
                    pe.wait_ge(y_ready, i + 1)
                    for k in range(KT):
                        last = nc.tensor.transpose(b[5 + k // 4][:, (k % 4) * P:(k % 4 + 1) * P],
                                                   ycat[:, k * P:(k + 1) * P], ident[:])
                        if k % 4 == 3:
                            last.then_inc(yTs, 1)
                    pe.wait_ge(yT_los, 2 * i + 2)
                    pe.wait_ge(wo_los, KT)
                    for a in range(2):
                        c = slice(a * 512, (a + 1) * 512)
                        pairs = []
                        for k in range(KT):
                            pairs += [(yT_hi[:, k], wo_hi[:, k, c]), (yT_hi[:, k], wo_lo[:, k, c]),
                                      (yT_lo[:, k], wo_hi[:, k, c])]
                        products(b[a][:], pairs).then_inc(mixed, 1)
                    pe.wait_ge(h_ready, i + 1)
                    for k in range(KT):
                        last = nc.tensor.transpose(b[2 + k // 4][:, (k % 4) * P:(k % 4 + 1) * P],
                                                   hr[:, k * P:(k + 1) * P], ident[:])
                        if k % 4 == 3:
                            last.then_inc(hTs, 1)

            @block.scalar
            def _(act):
                for k in range(KT):
                    if k >= 2:
                        act.wait_ge(wo_los, k - 1)
                    act.dma_start(wo_raw[:, k % 2], d["w_out"][:, k]).then_inc(wo_here[k % 2], 16)
                    act.wait_ge(wo_here[k % 2], 16 * (k // 2 + 1))
                    nc.scalar.activation(wo_hi[:, k], wo_raw[:, k % 2], ACT.Copy).then_inc(wo_his, 1)
                act.wait_ge(const_here, 16 * 9)
                proj = d["proj"].rearrange("(n p) c -> n p c", p=P)
                with act.Fori(0, TB) as i:
                    act.wait_ge(kept, i)
                    act.dma_start(pj[:], proj[i]).then_inc(pj_here, 16)
                    act.wait_ge(h_out, i * 16)
                    act.wait_ge(hTs, i * 2)
                    act.dma_start(hr[:], d["x"].rearrange("(n p) c -> n p c", p=P)[i]).then_inc(x_here, 16)
                    act.wait_ge(qkT, 4 * i + 1)
                    nc.scalar.activation(rqT[:].rearrange("p h t -> p (h t)"), b[0][:], ACT.Copy).then_inc(q_evac_a, 1)
                    act.wait_ge(qkT, 4 * i + 3)
                    nc.scalar.activation(sqT[:].rearrange("p h t -> p (h t)"), b[2][:], ACT.Copy).then_inc(q_evac_a, 1)
                    act.wait_ge(negs, i + 1)
                    for h in range(QH):
                        nc.scalar.activation(sm[:, h], sm[:, h], ACT.Exp, bias=neg[:, h:h + 1],
                                             accum_out=sums[:, h:h + 1])
                    nc.scalar.activation(sink_e[:], sd[:], ACT.Exp).then_inc(exps, 1)
                    for n in (0, 2):
                        act.wait_ge(pTs, 4 * i + n + 1)
                        nc.scalar.activation(pT[:, n * 2:n * 2 + 2].rearrange("p h a q -> p (h a q)"), b[n][:],
                                             ACT.Copy).then_inc(pT_a, 1)
                    for n in range(2):
                        act.wait_ge(yTs, 2 * i + n + 1)
                        nc.scalar.activation(yT_hi[:, 4 * n:4 * n + 4].rearrange("p k t -> p (k t)"), b[5 + n][:],
                                             ACT.Copy).then_inc(yT_his, 1)
                    act.wait_ge(h_ready, i + 1)
                    act.dma_start(d["h"][i], hr[:]).then_inc(h_out, 16)
                    act.wait_ge(hTs, 2 * i + 1)
                    nc.scalar.activation(hT_hi[:, 0:4, bass.ts(i, P)], b[2][:].rearrange("p (k t) -> p k t", k=4),
                                         ACT.Copy).then_inc(hT_his, 1)
                    act.wait_ge(hTs, 2 * i + 2)
                    nc.scalar.activation(hT_hi[:, 4:8, bass.ts(i, P)], b[3][:].rearrange("p (k t) -> p k t", k=4),
                                         ACT.Copy).then_inc(hT_his, 1)
                act.wait_ge(h_out, 16 * TB)

            @block.gpsimd
            def _(pool):
                nc.gpsimd.memset(minus_half[:], -0.5).then_inc(own_pool, 1)
                pool.wait_ge(own_pool, 1)
                with pool.Fori(0, TB) as i:
                    pool.wait_ge(var_here, i + 1)
                    nc.gpsimd.tensor_tensor(gn_rstd[:], gn_var[:], minus_half[:], ALU.pow).then_inc(rstd_here, 1)
                    pool.wait_ge(lvar_here, i + 1)
                    nc.gpsimd.tensor_tensor(l_rstd[:], l_var[:], minus_half[:, 0:1], ALU.pow).then_inc(lrstd_here, 1)

            @block.vector
            def _(v):
                nc.vector.memset(state[:], 0.0)
                nc.vector.memset(v_prev[:], 0.0)
                nc.vector.memset(skT[:], 0.0).then_inc(ready, 1)
                v.wait_ge(ready, 1)
                for k in range(KT):
                    v.wait_ge(wo_his, k + 1)
                    nc.vector.tensor_tensor(wo_lo[:, k], wo_raw[:, k % 2], wo_hi[:, k].bitcast(F32),
                                            ALU.subtract).then_inc(wo_los, 1)
                v.wait_ge(const_here, 16 * 9)
                chain = Chain(v, own)
                link = chain.link
                with v.Fori(0, TB) as i:
                    v.wait_ge(qkT, 4 * i + 2)
                    nc.vector.tensor_copy(rkT[:].rearrange("p h t -> p (h t)"), b[1][:]).then_inc(q_evac_v, 1)
                    v.wait_ge(qkT, 4 * i + 4)
                    nc.vector.tensor_copy(skT[:, 1], b[3][:, 0:P]).then_inc(q_evac_v, 1)
                    nc.vector.tensor_tensor(kz[:], pj[:, RW:2 * RW].rearrange("p (h c) -> p h c", h=RH),
                                            bc(zeta[:], 2, P), ALU.mult).then_inc(q_evac_v, 1)
                    v.wait_ge(ret_s, i + 1)
                    nc.vector.tensor_tensor(retT[:], b[4][:].rearrange("p (h t) -> p h t", h=RH), decayT[:],
                                            ALU.mult).then_inc(ret_sT, 1)
                    for done, n in enumerate((0, 2, 1, 3)):
                        v.wait_ge(swa_s, 4 * i + done + 1)
                        link(nc.vector.scalar_tensor_tensor(
                            sm[:, 2 * n:2 * n + 2], b[n][:].rearrange("p (a k) -> p a k", a=2), SD ** -0.5,
                            bc(masks[:, 0], 1, 2), ALU.mult, ALU.add))
                    link(nc.vector.tensor_reduce(mx[:], sm[:], AX.X, ALU.max))
                    link(nc.vector.tensor_tensor(mx[:], mx[:], sinks[:], ALU.max))
                    nc.vector.tensor_tensor(sd[:], sinks[:], mx[:], ALU.subtract)
                    nc.vector.tensor_scalar(neg[:], mx[:], -1.0, None, ALU.mult).then_inc(negs, 1)
                    v.wait_ge(ret_y, i + 1)
                    link(nc.vector.tensor_tensor(yr[:], b[6][:].rearrange("p (h t) -> p h t", h=RH),
                                                 bc(xi[:], 2, P), ALU.mult))
                    link(nc.vector.tensor_tensor(yr[:].rearrange("p h t -> p (h t)"), b[5][:],
                                                 yr[:].rearrange("p h t -> p (h t)"), ALU.add))
                    for h in range(RH):
                        g = float((1.0 - 2.0 ** (-5.0 - h)) ** P)
                        link(nc.vector.scalar_tensor_tensor(state[:, h], state[:, h], g,
                                                            b[7][:, h * P:(h + 1) * P], ALU.mult, ALU.add))
                    for h in range(RH):
                        link(nc.vector.bn_stats(stats[:, h], yr[:, h]))
                    for h in range(RH):
                        link(nc.vector.bn_aggr(mv[:, h], stats[:, h]))
                    nc.vector.tensor_scalar(gn_var[:], mv[:, :, 1], GN_EPS, None, ALU.add).then_inc(var_here, 1)
                    link(nc.vector.tensor_tensor(yr[:], yr[:], bc(mv[:, :, 0], 2, P), ALU.subtract))
                    v.wait_ge(rstd_here, i + 1)
                    link(nc.vector.tensor_tensor(yr[:], yr[:], bc(gn_rstd[:], 2, P), ALU.mult))
                    link(nc.vector.tensor_tensor(yr[:], yr[:], gn_w[:].rearrange("p (h t) -> p h t", h=RH), ALU.mult))
                    v.wait_ge(exps, i + 1)
                    link(nc.vector.tensor_tensor(ycat[:, 0:RW], yr[:].rearrange("p h t -> p (h t)"),
                                                 pj[:, 3 * RW:4 * RW], ALU.mult))
                    link(nc.vector.tensor_tensor(den[:], sums[:], sink_e[:], ALU.add))
                    link(nc.vector.reciprocal(rden[:], den[:]))
                    for n in (1, 3):
                        v.wait_ge(pTs, 4 * i + n + 1)
                        nc.vector.tensor_copy(pT[:, n * 2:n * 2 + 2].rearrange("p h a q -> p (h a q)"),
                                              b[n][:]).then_inc(pT_v, 1)
                    v.wait_ge(pv, i + 1)
                    nc.vector.tensor_tensor(ycat[:, RW:D].rearrange("p (h c) -> p h c", h=QH),
                                            b[4][:].rearrange("p (h c) -> p h c", h=QH),
                                            bc(rden[:], 2, SD), ALU.mult).then_inc(y_ready, 1)
                    nc.vector.tensor_copy(v_prev[:], pj[:, COLS - SKV:COLS])
                    nc.vector.tensor_copy(masks[:, 0], masks[:, 1])
                    nc.vector.tensor_copy(skT[:, 0], skT[:, 1]).then_inc(kept, 1)
                    for n in range(2):
                        v.wait_ge(yT_his, 2 * i + n + 1)
                        nc.vector.tensor_tensor(yT_lo[:, 4 * n:4 * n + 4].rearrange("p k t -> p (k t)"), b[5 + n][:],
                                                yT_hi[:, 4 * n:4 * n + 4].rearrange("p k t -> p (k t)").bitcast(F32),
                                                ALU.subtract).then_inc(yT_los, 1)
                    v.wait_ge(x_here, 16 * (i + 1))
                    for a in range(2):
                        c = slice(a * 512, (a + 1) * 512)
                        v.wait_ge(mixed, 2 * i + a + 1)
                        ins = nc.vector.scalar_tensor_tensor(hr[:, c], hr[:, c], ALPHA, b[a][:], ALU.mult, ALU.add)
                        ins.then_inc(mix_read, 1)
                        v.wait_ge(mix_read, 2 * i + a + 1)
                        link(nc.vector.bn_stats(lstats[:, a], hr[:, c]))
                    link(nc.vector.bn_aggr(lmv[:], lstats[:]))
                    nc.vector.tensor_scalar(l_var[:], lmv[:, 1:2], LN_EPS, None, ALU.add).then_inc(lvar_here, 1)
                    v.wait_ge(lrstd_here, i + 1)
                    link(nc.vector.tensor_scalar(hr[:], hr[:], lmv[:, 0:1], l_rstd[:], ALU.subtract, ALU.mult))
                    link(nc.vector.tensor_tensor(hr[:], hr[:], ln_w[:], ALU.mult))
                    nc.vector.tensor_tensor(hr[:], hr[:], ln_b[:], ALU.add).then_inc(h_ready, 1)
                    v.wait_ge(hT_his, 2 * i + 1)
                    nc.vector.tensor_tensor(hT_lo[:, 0:4, bass.ts(i, P)], b[2][:].rearrange("p (k t) -> p k t", k=4),
                                            hT_hi[:, 0:4, bass.ts(i, P)].bitcast(F32), ALU.subtract).then_inc(hT_los, 1)
                    v.wait_ge(hT_his, 2 * i + 2)
                    nc.vector.tensor_tensor(hT_lo[:, 4:8, bass.ts(i, P)], b[3][:].rearrange("p (k t) -> p k t", k=4),
                                            hT_hi[:, 4:8, bass.ts(i, P)].bitcast(F32), ALU.subtract).then_inc(hT_los, 1)
                    chain.restart()


def score(nc, d, hT_hi, hT_lo):
    HT = T // 2
    with ExitStack() as ctx:
        sb, bank, sem = memory(nc, ctx)
        keysT = sb("keysT", [P, PAIRS, NK])
        w_raw = [sb(f"wq_raw{p}", [P, KT, P]) for p in range(2)]
        w_hi = [sb(f"wq_hi{p}", [P, KT, P], F32R) for p in range(2)]
        w_lo = [sb(f"wq_lo{p}", [P, KT, P], F32R) for p in range(2)]
        qT = [sb(f"qT{p}", [P, T]) for p in range(2)]
        s_out = sb("s_out", [P, TB, 2, NK])
        q_ps = [[bank(f"q_ps{p}{a}") for a in range(2)] for p in range(2)]
        s_ps = [[bank(f"s_ps{p}{a}") for a in range(2)] for p in range(2)]
        keys_here = sem("keys_here")
        w_here = [sem(f"wq_here{p}") for p in range(2)]
        w_his, w_los = sem("wq_his"), sem("wq_los")
        q_done, q_act, q_dve = sem("q_done"), sem("q_act"), sem("q_dve")
        s_done, s_act, s_dve = sem("s_done"), sem("s_act"), sem("s_dve")
        s_stored = sem("s_stored")

        with nc.Block() as block:

            @block.sync
            def _(sp):
                sp.dma_start(keysT[:], d["keysT"]).then_inc(keys_here, 16)
                with sp.Fori(0, PH) as h:
                    for p in range(2):
                        sp.wait_ge(w_los, 2 * h)
                        sp.dma_start(w_raw[p][:], d["w_pq"][2 * h + p]).then_inc(w_here[p], 16)

            @block.tensor
            def _(pe):
                pe.wait_ge(keys_here, 16)
                with pe.Fori(0, PH) as h:
                    for p in range(2):
                        pe.wait_ge(w_los, 2 * h + p + 1)
                        for a in range(2):
                            c = slice(a * HT, (a + 1) * HT)
                            for k in range(KT):
                                nc.tensor.matmul(q_ps[p][a][:], w_hi[p][:, k], hT_hi[:, k, c],
                                                 start=(k == 0), stop=False)
                                nc.tensor.matmul(q_ps[p][a][:], w_hi[p][:, k], hT_lo[:, k, c],
                                                 start=False, stop=False)
                                last = nc.tensor.matmul(q_ps[p][a][:], w_lo[p][:, k], hT_hi[:, k, c],
                                                        start=False, stop=(k == KT - 1))
                            last.then_inc(q_done, 1)
                    for p in range(2):
                        for a in range(2):
                            pe.wait_ge((q_act, q_dve)[a], 2 * h + p + 1)
                            pe.wait_ge((s_act, s_dve)[a], 2 * h)
                            for n in range(4):
                                tb = 4 * a + n
                                last = nc.tensor.matmul(s_ps[p][a][:, n * P:(n + 1) * P], qT[p][:, tb * P:(tb + 1) * P],
                                                        keysT[:, bass.ds(2 * h + p, 1), :].rearrange("p a k -> p (a k)"),
                                                        start=True, stop=True)
                            last.then_inc(s_done, 1)

            @block.scalar
            def _(act):
                with act.Fori(0, PH) as h:
                    for p in range(2):
                        act.wait_ge(w_here[p], (h + 1) * 16)
                        act.wait_ge(q_done, 4 * h)
                        nc.scalar.activation(w_hi[p][:], w_raw[p][:], ACT.Copy).then_inc(w_his, 1)
                    for p in range(2):
                        act.wait_ge(q_done, 4 * h + 2 * p + 1)
                        nc.scalar.activation(qT[p][:, 0:HT], q_ps[p][0][:], ACT.Copy).then_inc(q_act, 1)
                    for p in range(2):
                        act.wait_ge(s_done, 4 * h + 2 * p + 1)
                        act.wait_ge(s_stored, 16 * h)
                        nc.scalar.activation(s_out[:, 0:4, p], s_ps[p][0][:].rearrange("p (t k) -> p t k", k=NK),
                                             ACT.Copy).then_inc(s_act, 1)
                    act.wait_ge(s_act, 2 * h + 2)
                    act.wait_ge(s_dve, 2 * h + 2)
                    act.dma_start(d["scores"].rearrange("n h p k -> h p n k")[h],
                                  s_out[:].rearrange("p t a k -> p t (a k)")).then_inc(s_stored, 16)
                act.wait_ge(s_stored, 16 * PH)

            @block.vector
            def _(v):
                with v.Fori(0, PH) as h:
                    for p in range(2):
                        v.wait_ge(w_his, 2 * h + p + 1)
                        nc.vector.tensor_tensor(w_lo[p][:], w_raw[p][:], w_hi[p][:].bitcast(F32),
                                                ALU.subtract).then_inc(w_los, 1)
                    for p in range(2):
                        v.wait_ge(q_done, 4 * h + 2 * p + 2)
                        nc.vector.tensor_copy(qT[p][:, HT:T], q_ps[p][1][:]).then_inc(q_dve, 1)
                    for p in range(2):
                        v.wait_ge(s_done, 4 * h + 2 * p + 2)
                        v.wait_ge(s_stored, 16 * h)
                        nc.vector.tensor_copy(s_out[:, 4:8, p],
                                              s_ps[p][1][:].rearrange("p (t k) -> p t k", k=NK)).then_inc(s_dve, 1)


def experts_in(nc, d, hT_hi, hT_lo):
    HT = T // 2
    BODIES = TB * PH // 2
    A_BLOCK = PH // 2
    with ExitStack() as ctx:
        sb, bank, sem = memory(nc, ctx)
        ident, iota = sb("ident4", [P, P]), sb("iota", [P, P])
        u_raw = [sb(f"u_raw{e}", [P, KT, P]) for e in range(2)]
        u_hi = [sb(f"u_hi{e}", [P, KT, P], F32R) for e in range(2)]
        u_lo = [sb(f"u_lo{e}", [P, KT, P], F32R) for e in range(2)]
        z_sb = [sb(f"z_sb{e}", [P, T]) for e in range(2)]
        s_in = [sb(f"s_in{j}", [P, 2, NK]) for j in range(2)]
        s_cp, s_left = sb("s_cp", [P, 2, NK]), sb("s_left", [P, 2, NK])
        top, top_i, top_f = sb("top", [P, 2, TOPK]), sb("top_i", [P, 2, TOPK], U32), sb("top_f", [P, 2, TOPK])
        cand, cand_left = sb("cand", [P, TOPK, TOPK]), sb("cand_left", [P, TOPK * TOPK])
        best, pos = sb("best", [P, TOPK]), sb("pos", [P, TOPK], U32)
        ab, ab_f = sb("ab", [P, 2, TOPK], U32), sb("ab_f", [P, 2, TOPK])
        pick = sb("pick", [P, 2, TOPK, TOPK])
        gap, gap_e = sb("gap", [P, TOPK]), sb("gap_e", [P, TOPK])
        gap_sum, gap_r = sb("gap_sum", [P, 1]), sb("gap_r", [P, 1])
        found = sb("found", [P, 3, PH, TOPK])
        iT = sb("iT", [P, 2, P])
        gT_hi, gT_lo = sb("gT_hi", [P, P], F32R), sb("gT_lo", [P, P])
        cur = sb("cur", [P, 4, GT])
        hot2 = [sb(f"hot2_{g}", [P, 4, NK], F32R) for g in range(2)]
        hot1_hi = [sb(f"hot1_hi{g}", [P, 4, NK], F32R) for g in range(2)]
        hot1_lo = [sb(f"hot1_lo{g}", [P, 4, NK], F32R) for g in range(2)]
        g_sb = sb("g_sb", [P, NK, GT])
        z_ps = [[bank(f"z_ps{e}{a}") for a in range(2)] for e in range(2)]
        g_ps = [bank(f"g_ps{g}") for g in range(2)]
        t_ps = bank("t_ps")
        const_here = sem("const4")
        u_here = [sem(f"u_here{e}") for e in range(2)]
        u_hi_in = [sem(f"u_hi_in{e}") for e in range(2)]
        u_lo_in = [sem(f"u_lo_in{e}") for e in range(2)]
        z_done = [sem(f"z_done{e}") for e in range(2)]
        z_read = [sem(f"z_read{e}") for e in range(2)]
        z_stored = [sem(f"z_stored{e}") for e in range(2)]
        s_here = [sem(f"s_here{j}") for j in range(2)]
        s_taken = [sem(f"s_taken{j}") for j in range(2)]
        gaps, exps = sem("gaps"), sem("exps4")
        found_in, found_T = sem("found_in"), sem("found_T")
        hot_in = [sem(f"hot_in{g}") for g in range(2)]
        g_done = [sem(f"g_done{g}") for g in range(2)]
        g_read = [sem(f"g_read{g}") for g in range(2)]
        g_stored = sem("g_stored")
        own = sem("own_dve4")

        def bodies(eng, body, block_end=lambda tb: None):
            with eng.Fori(0, A_BLOCK) as m:
                body(m, True, False)
            block_end(0)
            with eng.Fori(1, TB) as tb:
                with eng.Fori(0, A_BLOCK) as q:
                    body(tb * A_BLOCK + q, True, True, q)
                block_end(tb)
            with eng.Fori(0, A_BLOCK) as q:
                body(q + BODIES, False, True, q)

        with nc.Block() as block:

            @block.sync
            def _(sp):
                sp.dma_start(ident[:], d["ident"]).then_inc(const_here, 16)
                sp.dma_start(iota[:], d["iota"]).then_inc(const_here, 16)
                scores = d["scores"].rearrange("n h p k -> (n h) p k")
                with sp.Fori(0, BODIES) as m:
                    for j in range(2):
                        sp.wait_ge(s_taken[j], m)
                        sp.dma_start(s_in[j][:], scores[2 * m + j].rearrange("p (a k) -> p a k", a=2)).then_inc(
                            s_here[j], 16)
                        for e in range(2):
                            sp.wait_ge(u_lo_in[e], 2 * m + j)
                            sp.dma_start(u_raw[e][:], d["uT"][4 * m + 2 * j + e]).then_inc(u_here[e], 16)

            @block.tensor
            def _(pe):
                pe.wait_ge(const_here, 32)

                def body(m, heads, gates, q=None):
                    c = m - A_BLOCK
                    for n in range(8):
                        j, e, a = n // 4, n // 2 % 2, n % 2
                        if heads:
                            if a == 0:
                                pe.wait_ge(u_lo_in[e], 2 * m + j + 1)
                                pe.wait_ge(z_read[e], 2 * (2 * m + j))
                            cols = slice(a * HT, (a + 1) * HT)
                            for k in range(KT):
                                nc.tensor.matmul(z_ps[e][a][:], u_hi[e][:, k], hT_hi[:, k, cols],
                                                 start=(k == 0), stop=False)
                                nc.tensor.matmul(z_ps[e][a][:], u_hi[e][:, k], hT_lo[:, k, cols],
                                                 start=False, stop=False)
                                last = nc.tensor.matmul(z_ps[e][a][:], u_lo[e][:, k], hT_hi[:, k, cols],
                                                        start=False, stop=(k == KT - 1))
                            last.then_inc(z_done[e], 1)
                        if gates:
                            g = n % 2
                            pe.wait_ge(hot_in[g], 4 * c + n // 2 + 1)
                            pe.wait_ge(g_read[g], 4 * c + n // 2)
                            for t in range(4):
                                o = g_ps[g][:, t * P:(t + 1) * P]
                                nc.tensor.matmul(o, hot2[g][:, t], hot1_hi[g][:, t], start=True, stop=False)
                                last = nc.tensor.matmul(o, hot2[g][:, t], hot1_lo[g][:, t], start=False, stop=True)
                            last.then_inc(g_done[g], 1)

                def block_end(tb):
                    pe.wait_ge(found_in, tb + 1)
                    for n in range(3):
                        last = nc.tensor.transpose(t_ps[:, n * P:(n + 1) * P],
                                                   found[:, n].rearrange("p h k -> p (h k)"), ident[:])
                    last.then_inc(found_T, 1)

                bodies(pe, body, block_end)

            @block.scalar
            def _(act):
                def body(m, heads, gates, q=None):
                    c = m - A_BLOCK
                    if gates:
                        act.wait_ge(g_stored, 16 * c)
                    for n in range(8):
                        j, e, a = n // 4, n // 2 % 2, n % 2
                        if heads and a == 0:
                            act.wait_ge(u_here[e], 16 * (2 * m + j + 1))
                            act.wait_ge(z_done[e], 2 * (2 * m + j))
                            nc.scalar.activation(u_hi[e][:], u_raw[e][:], ACT.Copy).then_inc(u_hi_in[e], 1)
                            act.wait_ge(z_stored[e], 16 * (2 * m + j))
                        if heads and n % 4 == 3:
                            act.wait_ge(gaps, 2 * m + j + 1)
                            nc.scalar.activation(gap_e[:], gap[:], ACT.Exp, accum_out=gap_sum[:]).then_inc(exps, 1)
                        if heads:
                            act.wait_ge(z_done[e], 2 * (2 * m + j) + a + 1)
                            nc.scalar.activation(z_sb[e][:, a * HT:(a + 1) * HT], z_ps[e][a][:],
                                                 ACT.Copy).then_inc(z_read[e], 1)
                        if heads and a == 1:
                            act.wait_ge(z_read[e], 2 * (2 * m + j) + 2)
                            act.dma_start(d["z"][4 * m + 2 * j + e], z_sb[e][:]).then_inc(z_stored[e], 16)
                        if gates:
                            act.wait_ge(g_done[n % 2], 4 * c + n // 2 + 1)
                            nc.scalar.activation(g_sb[:, :, 4 * n:4 * n + 4].rearrange("p i t -> p t i"),
                                                 g_ps[n % 2][:].rearrange("p (t i) -> p t i", t=4),
                                                 ACT.Copy).then_inc(g_read[n % 2], 1)
                    if gates:
                        act.wait_ge(g_read[0], 4 * c + 4)
                        act.wait_ge(g_read[1], 4 * c + 4)
                        act.dma_start(d["gates"][c], g_sb[:]).then_inc(g_stored, 16)

                bodies(act, body)
                for e in range(2):
                    act.wait_ge(z_stored[e], 16 * NK // 2)
                act.wait_ge(g_stored, 16 * BODIES)

            @block.gpsimd
            def _(pool):
                with pool.Fori(0, BODIES) as m:
                    for n in range(4):
                        j, e = n // 2, n % 2
                        pool.wait_ge(u_hi_in[e], 2 * m + j + 1)
                        nc.gpsimd.tensor_tensor(u_lo[e][:], u_raw[e][:], u_hi[e][:].bitcast(F32),
                                                ALU.subtract).then_inc(u_lo_in[e], 1)

            @block.vector
            def _(v):
                chain = Chain(v, own)
                link = chain.link
                v.wait_ge(const_here, 32)

                def top16(values, left, out, index):
                    link(nc.vector.max(out[:, 0:8], values))
                    link(nc.vector.max_index(index[:, 0:8], out[:, 0:8], values))
                    link(nc.vector.match_replace(left, out[:, 0:8], values, LOWEST))
                    link(nc.vector.max(out[:, 8:16], left))
                    return nc.vector.max_index(index[:, 8:16], out[:, 8:16], left)

                def top_piece(piece, m, j, h):
                    if piece == 0:
                        v.wait_ge(s_here[j], 16 * (m + 1))
                        link(nc.vector.tensor_copy(s_cp[:], s_in[j][:]))
                        link(top16(s_cp[:, 0], s_left[:, 0], top[:, 0], top_i[:, 0]))
                    elif piece == 1:
                        top16(s_cp[:, 1], s_left[:, 1], top[:, 1], top_i[:, 1]).then_inc(s_taken[j], 1)
                    elif piece == 2:
                        v.wait_ge(s_taken[j], m + 1)
                        link(nc.vector.tensor_tensor(cand[:], bc(top[:, 0], 2, TOPK), bc(top[:, 1], 1, TOPK), ALU.add))
                        link(top16(cand[:].rearrange("p a b -> p (a b)"), cand_left[:], best, pos))
                        v.wait_ge(exps, 2 * m + j)
                        nc.vector.tensor_scalar(gap[:], best[:], best[:, 0:1], None, ALU.subtract).then_inc(gaps, 1)
                    else:
                        link(nc.vector.tensor_copy(top_f[:], top_i[:]))
                        link(nc.vector.tensor_scalar(ab[:, 0], pos[:], 4, None, ALU.logical_shift_right))
                        link(nc.vector.tensor_scalar(ab[:, 1], pos[:], 15, None, ALU.bitwise_and))
                        link(nc.vector.tensor_copy(ab_f[:], ab[:]))
                        link(nc.vector.tensor_tensor(pick[:], bc(ab_f[:], 3, TOPK),
                                                     bc(bc(iota[:, 0:TOPK], 1, TOPK), 1, 2), ALU.is_equal))
                        link(nc.vector.tensor_tensor(pick[:], pick[:], bc(top_f[:], 2, TOPK), ALU.mult))
                        link(nc.vector.tensor_reduce(found[:, 0:2, bass.ds(h, 1), :].rearrange("p a h k -> p a (h k)"),
                                                     pick[:], AX.X, ALU.add))
                        v.wait_ge(exps, 2 * m + j + 1)
                        link(nc.vector.reciprocal(gap_r[:], gap_sum[:]))
                        link(nc.vector.tensor_scalar(found[:, 2, bass.ds(h, 1), :].rearrange("p h k -> p (h k)"),
                                                     gap_e[:], gap_r[:], None, ALU.mult))

                def body(m, heads, gates, q=None):
                    c = m - A_BLOCK
                    if gates:
                        t0 = q * GT
                        for g in range(2):
                            v.wait_ge(hot_in[g], 4 * c)
                        nc.vector.tensor_scalar(cur[:, 0:2], iT[:, :, bass.ds(t0, GT)], 1.0, None, ALU.mult)
                        nc.vector.tensor_scalar(cur[:, 2], gT_hi[:, bass.ds(t0, GT)].bitcast(F32), 1.0, None, ALU.mult)
                        link(nc.vector.tensor_scalar(cur[:, 3], gT_lo[:, bass.ds(t0, GT)], 1.0, None, ALU.mult))
                    for n in range(8):
                        j = n // 4
                        if gates:
                            g = n % 2
                            v.wait_ge(g_done[g], 4 * c + n // 2)
                            for t in range(4):
                                w = 4 * n + t
                                nc.vector.tensor_scalar(hot2[g][:, t], iota[:], cur[:, 1, w:w + 1], None,
                                                        ALU.is_equal)
                                nc.vector.tensor_scalar(hot1_hi[g][:, t], iota[:], cur[:, 0, w:w + 1],
                                                        cur[:, 2, w:w + 1], ALU.is_equal, ALU.mult)
                                last = nc.vector.tensor_scalar(hot1_lo[g][:, t], iota[:], cur[:, 0, w:w + 1],
                                                               cur[:, 3, w:w + 1], ALU.is_equal, ALU.mult)
                            last.then_inc(hot_in[g], 1)
                        if heads:
                            h = (q if q is not None else m) * 2 + j
                            top_piece(n % 4, m, j, h)
                    chain.restart()

                def block_end(tb):
                    nc.vector.engine_nop().then_inc(found_in, 1)
                    v.wait_ge(found_T, tb + 1)
                    nc.vector.tensor_copy(iT[:].rearrange("p a t -> p (a t)"), t_ps[:, 0:2 * P])
                    link(nc.vector.tensor_copy(gT_hi[:], t_ps[:, 2 * P:3 * P]))
                    link(nc.vector.tensor_tensor(gT_lo[:], t_ps[:, 2 * P:3 * P], gT_hi[:].bitcast(F32), ALU.subtract))
                    chain.restart()

                bodies(v, body, block_end)


def experts_out(nc, d):
    with ExitStack() as ctx:
        sb, bank, sem = memory(nc, ctx)
        z_in = [sb(f"z_in{p}", [P, GROUP, T]) for p in range(2)]
        g_in = [sb(f"g_in{p}", [P, T // GT, GROUP * GT]) for p in range(2)]
        v_raw = [sb(f"v_raw{e}", [P, D]) for e in range(2)]
        v_hi = [sb(f"v_hi{p}", [P, GROUP, D], F32R) for p in range(2)]
        v_lo = [sb(f"v_lo{p}", [P, GROUP, D], F32R) for p in range(2)]
        a_hi, a_lo = sb("a_hi", [P, GROUP, T], F32R), sb("a_lo", [P, GROUP, T], F32R)
        y = sb("y", [P, TB, D])
        st, mv = sb("st5", [P, TB, 2, 6]), sb("mv5", [P, TB, 2])
        var, rstd, minus_half = sb("var5", [P, TB]), sb("rstd5", [P, TB]), sb("minus_half5", [P, TB])
        ln = z_in[0]
        y_ps = [bank(f"y_ps{n}") for n in range(8)]
        z_here = [sem(f"z_here{p}") for p in range(2)]
        v_here = [sem(f"v_here{e}") for e in range(2)]
        v_hi_in = [sem(f"v_hi_in{e}") for e in range(2)]
        v_lo_in = [sem(f"v_lo_in{e}") for e in range(2)]
        h_here, h_scaled, ln_here = sem("h_here"), sem("h_scaled"), sem("ln_here")
        gelu_in, prod_in, a_hi_in, a_lo_in = sem("gelu_in"), sem("prod_in"), sem("a_hi_in"), sem("a_lo_in")
        y_done = sem("y_done")
        y_read = [sem(f"y_read{n}") for n in range(8)]
        var_in, rstd_in, y_in, stored = sem("var_in"), sem("rstd_in"), sem("y_in"), sem("stored5")
        own, own_pool = sem("own_dve5"), sem("own_pool5")

        def groups(step):
            def all_of(eng):
                step(0, 0, 0, True, False)
                with eng.Fori(0, NG // 2 - 1) as n:
                    step(2 * n + 1, 1, n, True, True)
                    step(2 * n + 2, 0, n + 1, True, True)
                step(NG - 1, 1, NG // 2 - 1, True, True)
                step(NG, 0, NG // 2, False, True)
            return all_of

        def tokens(s):
            return slice(s * P, (s + 1) * P)

        with nc.Block() as block:

            @block.sync
            def _(sp):
                def load_z(r, p):
                    sp.dma_start(z_in[p][:], d["z"].rearrange("(r i) e t -> r e i t", i=GROUP)[r]).then_inc(z_here[p], 16)
                    sp.dma_start(g_in[p][:], d["gates"].rearrange("c e (r i) t -> r e c (i t)", i=GROUP)[r]).then_inc(
                        z_here[p], 16)

                def load_v(r):
                    for i in range(GROUP):
                        sp.wait_ge(v_lo_in[i % 2], 2 * r + i // 2)
                        sp.dma_start(v_raw[i % 2][:], d["v"][GROUP * r + i]).then_inc(v_here[i % 2], 16)

                load_z(0, 0)
                load_v(0)
                load_z(1, 1)
                load_v(1)
                with sp.Fori(0, NG // 2 - 1) as n:
                    for p in range(2):
                        sp.wait_ge(a_lo_in, TB * (2 * n + p + 1))
                        load_z(2 * n + 2 + p, p)
                        load_v(2 * n + 2 + p)
                sp.wait_ge(a_lo_in, TB * (NG - 1))
                sp.dma_start(ln[:, 0], d["ln2_w"]).then_inc(ln_here, 16)
                sp.dma_start(ln[:, 1], d["ln2_b"]).then_inc(ln_here, 16)
                for tb in range(TB):
                    sp.wait_ge(y_in, tb + 1)
                    sp.dma_start(d["out"][tokens(tb)], y[:, tb]).then_inc(stored, 16)
                sp.wait_ge(stored, 16 * TB)

            @block.tensor
            def _(pe):
                with pe.Fori(0, NG // 2) as n:
                    for p in range(2):
                        r = 2 * n + p
                        for e in range(2):
                            pe.wait_ge(v_lo_in[e], 2 * r + 2)
                        for s in range(TB):
                            pe.wait_ge(a_lo_in, TB * r + s + 1)
                            for a in range(2):
                                bk = (2 * s + a) % 8
                                c = slice(a * 512, (a + 1) * 512)
                                pe.wait_ge(y_read[bk], 2 * r + s // 4)
                                for i in range(GROUP):
                                    ah, al = a_hi[:, i, tokens(s)], a_lo[:, i, tokens(s)]
                                    nc.tensor.matmul(y_ps[bk][:], ah, v_hi[p][:, i, c], start=(i == 0), stop=False)
                                    nc.tensor.matmul(y_ps[bk][:], ah, v_lo[p][:, i, c], start=False, stop=False)
                                    last = nc.tensor.matmul(y_ps[bk][:], al, v_hi[p][:, i, c],
                                                            start=False, stop=(i == GROUP - 1))
                                last.then_inc(y_done, 1)

            @block.scalar
            def _(act):
                def step(r, p, use, prepare, add):
                    if not prepare:
                        return

                    def hi(s):
                        act.wait_ge(prod_in, TB * r + s + 1)
                        if add:
                            act.wait_ge(y_done, 16 * (r - 1) + 2 * s + 2)
                        nc.scalar.activation(a_hi[:, :, tokens(s)], z_in[p][:, :, tokens(s)],
                                             ACT.Copy).then_inc(a_hi_in, 1)

                    act.wait_ge(z_here[p], 32 * (use + 1))
                    if add:
                        act.wait_ge(y_done, 16 * (r - 1))
                    for s in range(TB):
                        nc.scalar.activation(z_in[p][:, :, tokens(s)], z_in[p][:, :, tokens(s)],
                                             ACT.Gelu).then_inc(gelu_in, 1)
                        if s % 2 == 0:
                            i = s // 2
                            act.wait_ge(v_here[i % 2], 16 * (2 * r + i // 2 + 1))
                            nc.scalar.activation(v_hi[p][:, i], v_raw[i % 2][:], ACT.Copy).then_inc(v_hi_in[i % 2], 1)
                        if s:
                            hi(s - 1)
                    hi(TB - 1)

                groups(step)(act)

            @block.gpsimd
            def _(pool):
                pool.dma_start(y[:], d["h"].rearrange("n p c -> p n c")).then_inc(h_here, 16)
                nc.gpsimd.memset(minus_half[:], -0.5).then_inc(own_pool, 1)
                with pool.Fori(0, NG // 2) as n:
                    for p in range(2):
                        r = 2 * n + p
                        for i in range(GROUP):
                            pool.wait_ge(v_hi_in[i % 2], 2 * r + i // 2 + 1)
                            nc.gpsimd.tensor_tensor(v_lo[p][:, i], v_raw[i % 2][:], v_hi[p][:, i].bitcast(F32),
                                                    ALU.subtract).then_inc(v_lo_in[i % 2], 1)
                pool.wait_ge(own_pool, 1)
                pool.wait_ge(var_in, 1)
                nc.gpsimd.tensor_tensor(rstd[:], var[:], minus_half[:], ALU.pow).then_inc(rstd_in, 1)

            @block.vector
            def _(v):
                chain = Chain(v, own)
                link = chain.link

                def step(r, p, use, prepare, add):
                    def lo(s):
                        v.wait_ge(a_hi_in, TB * r + s + 1)
                        nc.vector.tensor_tensor(a_lo[:, :, tokens(s)], z_in[p][:, :, tokens(s)],
                                                a_hi[:, :, tokens(s)].bitcast(F32), ALU.subtract).then_inc(a_lo_in, 1)

                    for s in range(TB):
                        if prepare:
                            v.wait_ge(gelu_in, TB * r + s + 1)
                            zs = z_in[p][:, :, tokens(s)].rearrange("p i (c t) -> p i c t", t=GT)
                            gs = g_in[p][:, 4 * s:4 * s + 4].rearrange("p c (i t) -> p i c t", t=GT)
                            nc.vector.tensor_tensor(zs, zs, gs, ALU.mult).then_inc(prod_in, 1)
                        if add:
                            for a in range(2):
                                bk = (2 * s + a) % 8
                                c = slice(a * 512, (a + 1) * 512)
                                v.wait_ge(y_done, 16 * (r - 1) + 2 * s + a + 1)
                                nc.vector.tensor_tensor(y[:, s, c], y_ps[bk][:], y[:, s, c], ALU.add).then_inc(
                                    y_read[bk], 1)
                        if prepare and s:
                            lo(s - 1)
                    if prepare:
                        lo(TB - 1)
                    if not add:
                        v.wait_ge(h_here, 16)
                        nc.vector.tensor_scalar(y[:], y[:], ALPHA, None, ALU.mult).then_inc(h_scaled, 1)
                        v.wait_ge(h_scaled, 1)

                groups(step)(v)
                for bk in range(8):
                    v.wait_ge(y_read[bk], 2 * NG)
                for s in range(TB):
                    for a in range(2):
                        link(nc.vector.bn_stats(st[:, s, a], y[:, s, a * 512:(a + 1) * 512]))
                for s in range(TB):
                    link(nc.vector.bn_aggr(mv[:, s], st[:, s]))
                nc.vector.tensor_scalar(var[:], mv[:, :, 1], LN_EPS, None, ALU.add).then_inc(var_in, 1)
                v.wait_ge(rstd_in, 1)
                v.wait_ge(ln_here, 32)
                for s in range(TB):
                    link(nc.vector.tensor_scalar(y[:, s], y[:, s], mv[:, s, 0:1], rstd[:, s:s + 1],
                                                 ALU.subtract, ALU.mult))
                    link(nc.vector.tensor_tensor(y[:, s], y[:, s], ln[:, 0], ALU.mult))
                    nc.vector.tensor_tensor(y[:, s], y[:, s], ln[:, 1], ALU.add).then_inc(y_in, 1)


PHASES = [1, 2, 3, 4, 5]


def build(nc, d):
    project(nc, d)
    if 2 not in PHASES:
        return
    with ExitStack() as ctx:
        hT_hi = ctx.enter_context(nc.sbuf_tensor("hT_hi", [P, KT, T], F32R))
        hT_lo = ctx.enter_context(nc.sbuf_tensor("hT_lo", [P, KT, T], F32R))
        attend(nc, d, hT_hi, hT_lo)
        if 3 not in PHASES:
            return
        score(nc, d, hT_hi, hT_lo)
        if 4 not in PHASES:
            return
        experts_in(nc, d, hT_hi, hT_lo)
    if 5 in PHASES:
        experts_out(nc, d)


def tables():
    f = np.float32
    pos = np.arange(T, dtype=f)

    def rope(dim):
        inv = f(1.0) / (f(10000.0) ** (np.arange(0, dim, 2, dtype=f) / f(dim)))
        ang = pos[:, None] * inv[None, :]
        both = np.stack([np.cos(ang), np.sin(ang)], axis=1).astype(f)
        return np.ascontiguousarray(both.reshape(TB, P, 2, dim // 2).transpose(1, 0, 2, 3))

    idx = np.arange(P)
    log_g = np.log(1.0 - 2.0 ** (-5.0 - np.arange(RH)))
    diff = idx[:, None] - idx[None, :]
    decay = np.where(diff[None] >= 0, np.exp(np.maximum(diff, 0)[None] * log_g[:, None, None]), 0.0)
    scale = RD ** -0.5
    q, k = np.arange(P)[:, None] + P, np.arange(2 * P)[None, :]
    seen = (q - k >= 0) & (q - k < P)
    return {
        "rope": rope(RD), "rope64": rope(SD),
        "decayT": np.ascontiguousarray(decay.transpose(2, 0, 1) * scale).astype(f),
        "zeta": (np.exp((P - 1.0 - idx)[:, None] * log_g[None]) * scale).astype(f),
        "xi": np.exp((idx + 1.0)[:, None] * log_g[None]).astype(f),
        "masks": np.stack([np.where(seen & (k >= P), 0.0, NEG), np.where(seen, 0.0, NEG)], axis=1).astype(f),
        "ident": np.eye(P, dtype=f),
        "iota": np.broadcast_to(np.arange(P, dtype=f), (P, P)).copy(),
    }


def rows(a):
    return np.ascontiguousarray(np.broadcast_to(a, (P,) + a.shape))


def kernel(x, w_in, ret_gn_w, swa_sinks, w_out, ln1_w, ln1_b, w_pq, peer_sub_keys,
           peer_u, peer_v, ln2_w, ln2_b):
    import concourse.bacc as bacc
    from concourse.bass_utils import run_bass_kernel_spmd

    a = {k: np.asarray(v) for k, v in dict(
        x=x, w_in=w_in, ret_gn_w=ret_gn_w, swa_sinks=swa_sinks, w_out=w_out, ln1_w=ln1_w, ln1_b=ln1_b,
        w_pq=w_pq, keys=peer_sub_keys, u=peer_u, v=peer_v, ln2_w=ln2_w, ln2_b=ln2_b).items()}
    assert a["x"].shape == (1, T, D) and a["w_in"].shape == (1, D, COLS)

    def slices(w):
        return np.ascontiguousarray(w.reshape(KT, P, -1).transpose(1, 0, 2))

    heads = [g * G + n for n in range(G) for g in range(KVH)]
    cols = np.concatenate([np.arange(4 * RW)] + [4 * RW + h * SD + np.arange(SD) for h in heads]
                          + [np.arange(4 * RW + SW, COLS)])
    arrays = {
        "x": a["x"][0],
        "xT": slices(a["x"][0].T),
        "w_in": slices(a["w_in"][0][:, cols]),
        "w_out": slices(a["w_out"][0]),
        "w_pq": np.ascontiguousarray(a["w_pq"][0].reshape(KT, P, PAIRS, P).transpose(2, 1, 0, 3)),
        "keysT": np.ascontiguousarray(a["keys"][0].reshape(PAIRS, NK, P).transpose(2, 0, 1)),
        "uT": np.ascontiguousarray(a["u"][0].reshape(NK, NK, KT, P).transpose(0, 3, 2, 1)),
        "v": a["v"][0].reshape(NK, NK, D),
        "gn_w": rows(a["ret_gn_w"][0]), "sinks": rows(a["swa_sinks"][0]),
        "ln1_w": rows(a["ln1_w"][0]), "ln1_b": rows(a["ln1_b"][0]),
        "ln2_w": rows(a["ln2_w"][0]), "ln2_b": rows(a["ln2_b"][0]),
        **tables(),
    }
    nc = bacc.Bacc("TRN2", target_bir_lowering=False, num_devices=1)
    d = {n: nc.dram_tensor(f"in_{n}", t.shape, F32, kind="ExternalInput").ap() for n, t in arrays.items()}
    for n, shape in (("proj", (T, COLS)), ("h", (TB, P, D)), ("scores", (TB, PH, P, 2 * NK)),
                     ("z", (NK, P, T)), ("gates", (T // GT, P, NK, GT))):
        d[n] = nc.dram_tensor(n, shape, F32, kind="Internal").ap()
    d["out"] = nc.dram_tensor("out", (T, D), F32, kind="ExternalOutput").ap()
    build(nc, d)
    r = run_bass_kernel_spmd(nc, [{f"in_{n}": t for n, t in arrays.items()}], core_ids=[0])
    return r.results[0]["out"].reshape(1, T, D)
```

```python
from contextlib import ExitStack

import numpy as np
import concourse.bass as bass
from concourse import mybir

F32 = mybir.dt.float32
F32R = mybir.dt.float32r
U32 = mybir.dt.uint32
ACT = mybir.ActivationFunctionType
ALU = mybir.AluOpType
AX = mybir.AxisListType

P = 128
D = 1024
T = 1024
KT = D // P
TB = T // P
RH, RD = 4, 128
RW = RH * RD
QH, KVH, SD = 8, 2, 64
G = QH // KVH
SW, SKV = QH * SD, KVH * SD
COLS = 4 * RW + SW + 2 * SKV
ALPHA = 2.0 ** 0.25
LN_EPS, GN_EPS = 1e-5, 1e-6
PH, NK, TOPK = 8, 128, 16
PAIRS = 2 * PH
NEG = -1e30
LOWEST = -3.0e38
GROUP = 4
GT = 32
NG = NK // GROUP


def bc(ap, axis, n):
    v = ap.unsqueeze(axis)
    shape = list(v.shape)
    shape[axis] = n
    return v.to_broadcast(shape)


def wait(eng, sem, value):
    if not isinstance(value, int) or value > 0:
        eng.wait_ge(sem, value)


def turns(eng, n, turn, last=1):
    turn(0)
    with eng.Fori(1, n - last) as i:
        turn(i)
    for i in range(n - last, n):
        turn(i)


class Chain:

    def __init__(self, eng, sem):
        self.eng, self.sem, self.n = eng, sem, 0

    def link(self, ins):
        self.n += 1
        ins.then_inc(self.sem, 1)
        self.eng.wait_ge(self.sem, self.n)

    def restart(self):
        self.eng.wait_ge(self.sem, self.n)
        self.eng.sem_clear(self.sem)
        self.n = 0


def memory(nc, ctx):
    def sb(name, shape, dt=F32):
        return ctx.enter_context(nc.sbuf_tensor(name, shape, dt))

    def bank(name):
        return ctx.enter_context(nc.psum_tensor(name, [P, 512], F32))

    def sem(name):
        return ctx.enter_context(nc.semaphore(name))

    return sb, bank, sem


def project(nc, d):
    chunks = [("rot", 0, 512), ("rot", 512, 512), ("copy", 1024, 512), ("silu", 1536, 512),
              ("rot64", 2048, 512), ("kv", 2560, 256)]
    NB = 4
    OUT = 3
    with ExitStack() as ctx:
        sb, bank, sem = memory(nc, ctx)
        x_raw = sb("x_raw", [P, KT, T])
        x_hi = sb("x_hi", [P, KT, T], F32R)
        x_lo = sb("x_lo", [P, KT, T], F32R)
        w_raw = sb("w_raw", [P, KT, 512])
        w_hi = sb("w_hi", [P, 2, KT, 512], F32R)
        w_lo = sb("w_lo", [P, 2, KT, 512], F32R)
        rope = sb("rope", [P, TB, 2, RD // 2])
        rope64 = sb("rope64", [P, TB, 2, SD // 2])
        t_cos = sb("t_cos", [P, 512])
        t_sin = sb("t_sin", [P, 512])
        res = sb("res", [P, OUT, 512])
        ps = [bank(f"pp{i}") for i in range(NB)]
        x_here = [sem(f"x_here{k}") for k in range(KT)]
        w_here = [sem(f"w_here{k}") for k in range(KT)]
        rope_here = sem("rope_here")
        x_his, x_los = sem("x_his"), sem("x_los")
        w_his, w_los = sem("w_his"), sem("w_los")
        tile_done = sem("tile_done")
        res_act, res_dve = sem("res_act"), sem("res_dve")
        stored = [sem(f"stored{i}") for i in range(OUT)]
        own = sem("own_dve1")
        tiles = [(c, tb) for c in range(len(chunks)) for tb in range(TB)]
        by_act = [chunks[c][0] in ("copy", "silu") for c, _ in tiles]

        def finished(n):
            return (res_act, sum(by_act[:n + 1])) if by_act[n] else (res_dve, n + 1 - sum(by_act[:n + 1]))

        with nc.Block() as block:

            @block.sync
            def _(sp):
                sp.dma_start(rope[:], d["rope"]).then_inc(rope_here, 16)
                sp.dma_start(rope64[:], d["rope64"]).then_inc(rope_here, 16)
                for k in range(KT):
                    sp.dma_start(x_raw[:, k], d["xT"][:, k]).then_inc(x_here[k], 16)
                    sp.dma_start(w_raw[:, k], d["w_in"][:, k, 0:512]).then_inc(w_here[k], 16)
                for n, (c, tb) in enumerate(tiles):
                    if c + 1 < len(chunks):
                        _, c0, w = chunks[c + 1]
                        k = tb
                        sp.wait_ge(w_his, c * KT + k + 1)
                        sp.wait_ge(w_los, c * KT + k + 1)
                        sp.dma_start(w_raw[:, k, 0:w], d["w_in"][:, k, c0:c0 + w]).then_inc(w_here[k], 16)
                    _, c0, w = chunks[c]
                    sp.wait_ge(*finished(n))
                    sp.dma_start(d["proj"][tb * P:(tb + 1) * P, c0:c0 + w],
                                 res[:, n % OUT, 0:w]).then_inc(stored[n % OUT], 16)
                for i in range(OUT):
                    sp.wait_ge(stored[i], 16 * len(range(i, len(tiles), OUT)))

            @block.tensor
            def _(pe):
                for n, (c, tb) in enumerate(tiles):
                    w = chunks[c][2]
                    if n >= NB:
                        pe.wait_ge(*finished(n - NB))
                    for k in range(KT):
                        if tb == 0:
                            if c == 0:
                                pe.wait_ge(x_los, k + 1)
                            pe.wait_ge(w_los, c * KT + k + 1)
                        xh = x_hi[:, k, tb * P:(tb + 1) * P]
                        xl = x_lo[:, k, tb * P:(tb + 1) * P]
                        wh, wl = w_hi[:, c % 2, k, 0:w], w_lo[:, c % 2, k, 0:w]
                        o = ps[n % NB][:, 0:w]
                        nc.tensor.matmul(o, xh, wh, start=(k == 0), stop=False)
                        nc.tensor.matmul(o, xh, wl, start=False, stop=False)
                        last = nc.tensor.matmul(o, xl, wh, start=False, stop=(k == KT - 1))
                    last.then_inc(tile_done, 1)

            @block.scalar
            def _(act):
                def split_w(c, k):
                    w = chunks[c][2]
                    act.wait_ge(w_here[k], 16 * (c + 1))
                    if c >= 2:
                        act.wait_ge(tile_done, TB * (c - 1))
                    nc.scalar.activation(w_hi[:, c % 2, k, 0:w], w_raw[:, k, 0:w], ACT.Copy).then_inc(w_his, 1)

                for k in range(KT):
                    act.wait_ge(x_here[k], 16)
                    nc.scalar.activation(x_hi[:, k], x_raw[:, k], ACT.Copy).then_inc(x_his, 1)
                    split_w(0, k)
                for n, (c, tb) in enumerate(tiles):
                    if c + 1 < len(chunks):
                        split_w(c + 1, tb)
                    if by_act[n]:
                        act.wait_ge(tile_done, n + 1)
                        if n >= OUT:
                            act.wait_ge(stored[n % OUT], 16 * (n // OUT))
                        f = ACT.Silu if chunks[c][0] == "silu" else ACT.Copy
                        nc.scalar.activation(res[:, n % OUT, :], ps[n % NB][:], f).then_inc(res_act, 1)

            @block.vector
            def _(v):
                chain = Chain(v, own)

                def split_w(c, k):
                    w = chunks[c][2]
                    v.wait_ge(w_his, c * KT + k + 1)
                    nc.vector.tensor_tensor(w_lo[:, c % 2, k, 0:w], w_raw[:, k, 0:w],
                                            w_hi[:, c % 2, k, 0:w].bitcast(F32), ALU.subtract).then_inc(w_los, 1)

                def rotate(src, out, cos, sin, heads, half):
                    n = heads * 2 * half
                    s4 = src.rearrange("p (h a f) -> p h a f", h=heads, a=2)
                    c4 = t_cos[:, 0:n].rearrange("p (h a f) -> p h a f", h=heads, a=2)
                    n4 = t_sin[:, 0:n].rearrange("p (h a f) -> p h a f", h=heads, a=2)
                    o4 = out.rearrange("p (h a f) -> p h a f", h=heads, a=2)
                    cosb = bc(bc(cos, 1, 2), 1, heads)
                    sinb = bc(bc(sin, 1, 2), 1, heads)
                    nc.vector.tensor_tensor(c4, s4, cosb, ALU.mult)
                    chain.link(nc.vector.tensor_tensor(n4, s4, sinb, ALU.mult))
                    chain.link(nc.vector.tensor_tensor(o4[:, :, 0], c4[:, :, 0], n4[:, :, 1], ALU.subtract))
                    return nc.vector.tensor_tensor(o4[:, :, 1], c4[:, :, 1], n4[:, :, 0], ALU.add)

                for k in range(KT):
                    v.wait_ge(x_his, k + 1)
                    nc.vector.tensor_tensor(x_lo[:, k], x_raw[:, k], x_hi[:, k].bitcast(F32),
                                            ALU.subtract).then_inc(x_los, 1)
                    split_w(0, k)
                v.wait_ge(rope_here, 32)
                for n, (c, tb) in enumerate(tiles):
                    if c + 1 < len(chunks):
                        split_w(c + 1, tb)
                    if by_act[n]:
                        continue
                    kind = chunks[c][0]
                    v.wait_ge(tile_done, n + 1)
                    if n >= OUT:
                        v.wait_ge(stored[n % OUT], 16 * (n // OUT))
                    if finished(n)[1] > 1:
                        v.wait_ge(res_dve, finished(n)[1] - 1)
                    o = res[:, n % OUT]
                    if kind == "rot":
                        last = rotate(ps[n % NB][:], o, rope[:, tb, 0], rope[:, tb, 1], RH, RD // 2)
                    elif kind == "rot64":
                        last = rotate(ps[n % NB][:], o, rope64[:, tb, 0], rope64[:, tb, 1], QH, SD // 2)
                    else:
                        nc.vector.tensor_copy(o[:, SKV:2 * SKV], ps[n % NB][:, SKV:2 * SKV])
                        last = rotate(ps[n % NB][:, 0:SKV], o[:, 0:SKV], rope64[:, tb, 0], rope64[:, tb, 1],
                                      KVH, SD // 2)
                    last.then_inc(res_dve, 1)


def attend(nc, d, hT_hi, hT_lo):
    with ExitStack() as ctx:
        sb, bank, sem = memory(nc, ctx)
        ident = sb("ident", [P, P])
        decayT = sb("decayT", [P, RH, P])
        zeta, xi = sb("zeta", [P, RH]), sb("xi", [P, RH])
        masks = sb("masks", [P, 2, 2 * P])
        gn_w, sinks = sb("gn_w", [P, RW]), sb("sinks", [P, QH])
        ln_w, ln_b = sb("ln_w", [P, D]), sb("ln_b", [P, D])
        wo_hi, wo_lo = sb("wo_hi", [P, KT, D], F32R), sb("wo_lo", [P, KT, D], F32R)
        minus_half = sb("minus_half", [P, RH])
        pj = sb("pj", [P, COLS])
        rqT, rkT = sb("rqT", [P, RH, P]), sb("rkT", [P, RH, P])
        sqT = sb("sqT", [P, QH // 2, P])
        skT = sb("skT", [P, 2, P])
        v_prev = sb("v_prev", [P, SKV])
        kz = sb("kz", [P, RH, P])
        retT = sb("retT", [P, RH, P])
        state = sb("state", [P, RH, P])
        yr = sb("yr", [P, RH, P])
        stats, mv = sb("stats", [P, RH, 6]), sb("mv", [P, RH, 2])
        gn_var, gn_rstd = sb("gn_var", [P, RH]), sb("gn_rstd", [P, RH])
        sm = sb("sm", [P, QH, 2 * P])
        wo_raw = sm[:].rearrange("p (a h) k -> p a (h k)", a=2)
        mx, neg, sd = sb("mx", [P, QH]), sb("neg", [P, QH]), sb("sd", [P, QH])
        sums, sink_e, den, rden = (sb(n, [P, QH]) for n in ("sums", "sink_e", "den", "rden"))
        pT = sb("pT", [P, QH, 2, P])
        ycat = sb("ycat", [P, D])
        yT_hi, yT_lo = sb("yT_hi", [P, KT, P], F32R), sb("yT_lo", [P, KT, P], F32R)
        hr = sb("hr", [P, D])
        lstats, lmv = sb("lstats", [P, 2, 6]), sb("lmv", [P, 2])
        l_var, l_rstd = sb("l_var", [P, 1]), sb("l_rstd", [P, 1])
        b = [bank(f"pa{i}") for i in range(8)]
        const_here, wo_here = sem("const_here"), [sem("wo_here0"), sem("wo_here1")]
        pj_here, x_here, h_out = sem("pj_here"), sem("x_here"), sem("h_out")
        wo_his, wo_los = sem("wo_his"), sem("wo_los")
        ready = sem("ready")
        qkT, q_evac_a, q_evac_v = sem("qkT"), sem("q_evac_a"), sem("q_evac_v")
        ret_s, swa_s, ret_sT = sem("ret_s"), sem("swa_s"), sem("ret_sT")
        ret_y, ret_used = sem("ret_y"), sem("ret_used")
        masked, negs, exps = sem("masked"), sem("negs"), sem("exps")
        pTs, pT_a, pT_v = sem("pTs"), sem("pT_a"), sem("pT_v")
        pv, y_ready = sem("pv"), sem("y_ready")
        var_here, rstd_here = sem("var_here"), sem("rstd_here")
        yTs, yT_his, yT_los = sem("yTs"), sem("yT_his"), sem("yT_los")
        mixed, mix_read = sem("mixed"), sem("mix_read")
        lvar_here, lrstd_here = sem("lvar_here"), sem("lrstd_here")
        h_ready, hTs, hT_his, hT_los = sem("h_ready"), sem("hTs"), sem("hT_his"), sem("hT_los")
        kept = sem("kept")
        own, own_pool = sem("own_dve2"), sem("own_pool2")

        with nc.Block() as block:

            @block.sync
            def _(sp):
                for t, n in ((ident, "ident"), (decayT, "decayT"), (zeta, "zeta"), (xi, "xi"), (masks, "masks"),
                             (gn_w, "gn_w"), (sinks, "sinks"), (ln_w, "ln1_w"), (ln_b, "ln1_b")):
                    sp.dma_start(t[:], d[n]).then_inc(const_here, 16)

            @block.tensor
            def _(pe):
                def products(out, pairs, start=True):
                    for n, (l, r) in enumerate(pairs):
                        last = nc.tensor.matmul(out, l, r, start=(n == 0), stop=(n == len(pairs) - 1))
                    return last

                pe.wait_ge(const_here, 16 * 9)
                pe.wait_ge(ready, 1)
                def turn(i):
                    pe.wait_ge(pj_here, (i + 1) * 16)
                    wait(pe, hT_los, i * 2)
                    for h in range(RH):
                        last = nc.tensor.transpose(b[0][:, h * P:(h + 1) * P], pj[:, h * RD:(h + 1) * RD], ident[:])
                    last.then_inc(qkT, 1)
                    for h in range(RH):
                        last = nc.tensor.transpose(b[1][:, h * P:(h + 1) * P],
                                                   pj[:, RW + h * RD:RW + (h + 1) * RD], ident[:])
                    last.then_inc(qkT, 1)
                    for h in range(QH // 2):
                        last = nc.tensor.transpose(b[2][:, h * P:(h + 1) * P],
                                                   pj[:, 4 * RW + h * P:4 * RW + (h + 1) * P], ident[:])
                    last.then_inc(qkT, 1)
                    nc.tensor.transpose(b[3][:, 0:P], pj[:, 4 * RW + SW:4 * RW + SW + SKV], ident[:]).then_inc(qkT, 1)
                    pe.wait_ge(q_evac_a, 2 * i + 1)
                    pe.wait_ge(q_evac_v, 3 * i + 1)
                    for h in range(RH):
                        last = nc.tensor.matmul(b[4][:, h * P:(h + 1) * P], rkT[:, h], rqT[:, h], start=True, stop=True)
                    last.then_inc(ret_s, 1)
                    pe.wait_ge(q_evac_a, 2 * i + 2)
                    pe.wait_ge(q_evac_v, 3 * i + 2)
                    for h in (0, 4, 1, 5, 2, 6, 3, 7):
                        lo = (h // G) * SD
                        last = nc.tensor.matmul(b[h // 2][:, (h % 2) * 256:(h % 2) * 256 + 256],
                                                sqT[lo:lo + SD, h % G], skT[lo:lo + SD].rearrange("p a k -> p (a k)"),
                                                start=True, stop=True)
                        if h % 2:
                            last.then_inc(swa_s, 1)
                    pe.wait_ge(ret_sT, i + 1)
                    pe.wait_ge(q_evac_v, 3 * i + 3)
                    wait(pe, yT_los, i * 2)
                    for h in range(RH):
                        vh = pj[:, 2 * RW + h * RD:2 * RW + (h + 1) * RD]
                        nc.tensor.matmul(b[5][:, h * P:(h + 1) * P], retT[:, h], vh, start=True, stop=True)
                        nc.tensor.matmul(b[6][:, h * P:(h + 1) * P], rqT[:, h], state[:, h], start=True, stop=True)
                        last = nc.tensor.matmul(b[7][:, h * P:(h + 1) * P], kz[:, h], vh, start=True, stop=True)
                    last.then_inc(ret_y, 1)
                    pe.wait_ge(exps, i + 1)
                    for h in range(QH):
                        for a in range(2):
                            n = 2 * h + a
                            last = nc.tensor.transpose(b[n // 4][:, (n % 4) * P:(n % 4 + 1) * P],
                                                       sm[:, h, a * P:(a + 1) * P], ident[:])
                        if h % 2:
                            last.then_inc(pTs, 1)
                    for h in range(QH):
                        if h % 2 == 0:
                            pe.wait_ge(*((pT_a, 2 * i + h // 4 + 1) if h % 4 == 0 else (pT_v, 2 * i + h // 4 + 1)))
                        g = h // G
                        nc.tensor.matmul(b[4][:, h * SD:(h + 1) * SD], pT[:, h, 0], v_prev[:, g * SD:(g + 1) * SD],
                                         start=True, stop=False)
                        last = nc.tensor.matmul(b[4][:, h * SD:(h + 1) * SD], pT[:, h, 1],
                                                pj[:, COLS - SKV + g * SD:COLS - SKV + (g + 1) * SD],
                                                start=False, stop=True)
                    last.then_inc(pv, 1)
                    pe.wait_ge(y_ready, i + 1)
                    for k in range(KT):
                        last = nc.tensor.transpose(b[5 + k // 4][:, (k % 4) * P:(k % 4 + 1) * P],
                                                   ycat[:, k * P:(k + 1) * P], ident[:])
                        if k % 4 == 3:
                            last.then_inc(yTs, 1)
                    pe.wait_ge(yT_los, 2 * i + 2)
                    pe.wait_ge(wo_los, KT)
                    for a in range(2):
                        c = slice(a * 512, (a + 1) * 512)
                        pairs = []
                        for k in range(KT):
                            pairs += [(yT_hi[:, k], wo_hi[:, k, c]), (yT_hi[:, k], wo_lo[:, k, c]),
                                      (yT_lo[:, k], wo_hi[:, k, c])]
                        products(b[a][:], pairs).then_inc(mixed, 1)
                    pe.wait_ge(h_ready, i + 1)
                    for k in range(KT):
                        last = nc.tensor.transpose(b[2 + k // 4][:, (k % 4) * P:(k % 4 + 1) * P],
                                                   hr[:, k * P:(k + 1) * P], ident[:])
                        if k % 4 == 3:
                            last.then_inc(hTs, 1)

                turns(pe, TB, turn, last=0)

            @block.scalar
            def _(act):
                for k in range(KT):
                    if k >= 2:
                        act.wait_ge(wo_los, k - 1)
                    act.dma_start(wo_raw[:, k % 2], d["w_out"][:, k]).then_inc(wo_here[k % 2], 16)
                    act.wait_ge(wo_here[k % 2], 16 * (k // 2 + 1))
                    nc.scalar.activation(wo_hi[:, k], wo_raw[:, k % 2], ACT.Copy).then_inc(wo_his, 1)
                act.wait_ge(const_here, 16 * 9)
                proj = d["proj"].rearrange("(n p) c -> n p c", p=P)
                def turn(i):
                    wait(act, kept, i)
                    act.dma_start(pj[:], proj[i]).then_inc(pj_here, 16)
                    wait(act, h_out, i * 16)
                    wait(act, hTs, i * 2)
                    act.dma_start(hr[:], d["x"].rearrange("(n p) c -> n p c", p=P)[i]).then_inc(x_here, 16)
                    act.wait_ge(qkT, 4 * i + 1)
                    nc.scalar.activation(rqT[:].rearrange("p h t -> p (h t)"), b[0][:], ACT.Copy).then_inc(q_evac_a, 1)
                    act.wait_ge(qkT, 4 * i + 3)
                    nc.scalar.activation(sqT[:].rearrange("p h t -> p (h t)"), b[2][:], ACT.Copy).then_inc(q_evac_a, 1)
                    act.wait_ge(negs, i + 1)
                    for h in range(QH):
                        nc.scalar.activation(sm[:, h], sm[:, h], ACT.Exp, bias=neg[:, h:h + 1],
                                             accum_out=sums[:, h:h + 1])
                    nc.scalar.activation(sink_e[:], sd[:], ACT.Exp).then_inc(exps, 1)
                    for n in (0, 2):
                        act.wait_ge(pTs, 4 * i + n + 1)
                        nc.scalar.activation(pT[:, n * 2:n * 2 + 2].rearrange("p h a q -> p (h a q)"), b[n][:],
                                             ACT.Copy).then_inc(pT_a, 1)
                    for n in range(2):
                        act.wait_ge(yTs, 2 * i + n + 1)
                        nc.scalar.activation(yT_hi[:, 4 * n:4 * n + 4].rearrange("p k t -> p (k t)"), b[5 + n][:],
                                             ACT.Copy).then_inc(yT_his, 1)
                    act.wait_ge(h_ready, i + 1)
                    act.dma_start(d["h"][i], hr[:]).then_inc(h_out, 16)
                    act.wait_ge(hTs, 2 * i + 1)
                    nc.scalar.activation(hT_hi[:, 0:4, bass.ts(i, P)], b[2][:].rearrange("p (k t) -> p k t", k=4),
                                         ACT.Copy).then_inc(hT_his, 1)
                    act.wait_ge(hTs, 2 * i + 2)
                    nc.scalar.activation(hT_hi[:, 4:8, bass.ts(i, P)], b[3][:].rearrange("p (k t) -> p k t", k=4),
                                         ACT.Copy).then_inc(hT_his, 1)

                turns(act, TB, turn, last=0)
                act.wait_ge(h_out, 16 * TB)

            @block.gpsimd
            def _(pool):
                nc.gpsimd.memset(minus_half[:], -0.5).then_inc(own_pool, 1)
                pool.wait_ge(own_pool, 1)
                def turn(i):
                    pool.wait_ge(var_here, i + 1)
                    nc.gpsimd.tensor_tensor(gn_rstd[:], gn_var[:], minus_half[:], ALU.pow).then_inc(rstd_here, 1)
                    pool.wait_ge(lvar_here, i + 1)
                    nc.gpsimd.tensor_tensor(l_rstd[:], l_var[:], minus_half[:, 0:1], ALU.pow).then_inc(lrstd_here, 1)

                turns(pool, TB, turn, last=0)

            @block.vector
            def _(v):
                nc.vector.memset(state[:], 0.0)
                nc.vector.memset(v_prev[:], 0.0)
                nc.vector.memset(skT[:], 0.0).then_inc(ready, 1)
                v.wait_ge(ready, 1)
                for k in range(KT):
                    v.wait_ge(wo_his, k + 1)
                    nc.vector.tensor_tensor(wo_lo[:, k], wo_raw[:, k % 2], wo_hi[:, k].bitcast(F32),
                                            ALU.subtract).then_inc(wo_los, 1)
                v.wait_ge(const_here, 16 * 9)
                chain = Chain(v, own)
                link = chain.link
                def turn(i):
                    v.wait_ge(qkT, 4 * i + 2)
                    nc.vector.tensor_copy(rkT[:].rearrange("p h t -> p (h t)"), b[1][:]).then_inc(q_evac_v, 1)
                    v.wait_ge(qkT, 4 * i + 4)
                    nc.vector.tensor_copy(skT[:, 1], b[3][:, 0:P]).then_inc(q_evac_v, 1)
                    nc.vector.tensor_tensor(kz[:], pj[:, RW:2 * RW].rearrange("p (h c) -> p h c", h=RH),
                                            bc(zeta[:], 2, P), ALU.mult).then_inc(q_evac_v, 1)
                    v.wait_ge(ret_s, i + 1)
                    nc.vector.tensor_tensor(retT[:], b[4][:].rearrange("p (h t) -> p h t", h=RH), decayT[:],
                                            ALU.mult).then_inc(ret_sT, 1)
                    for done, n in enumerate((0, 2, 1, 3)):
                        v.wait_ge(swa_s, 4 * i + done + 1)
                        link(nc.vector.scalar_tensor_tensor(
                            sm[:, 2 * n:2 * n + 2], b[n][:].rearrange("p (a k) -> p a k", a=2), SD ** -0.5,
                            bc(masks[:, 0], 1, 2), ALU.mult, ALU.add))
                    link(nc.vector.tensor_reduce(mx[:], sm[:], AX.X, ALU.max))
                    link(nc.vector.tensor_tensor(mx[:], mx[:], sinks[:], ALU.max))
                    nc.vector.tensor_tensor(sd[:], sinks[:], mx[:], ALU.subtract)
                    nc.vector.tensor_scalar(neg[:], mx[:], -1.0, None, ALU.mult).then_inc(negs, 1)
                    v.wait_ge(ret_y, i + 1)
                    link(nc.vector.tensor_tensor(yr[:], b[6][:].rearrange("p (h t) -> p h t", h=RH),
                                                 bc(xi[:], 2, P), ALU.mult))
                    link(nc.vector.tensor_tensor(yr[:].rearrange("p h t -> p (h t)"), b[5][:],
                                                 yr[:].rearrange("p h t -> p (h t)"), ALU.add))
                    for h in range(RH):
                        g = float((1.0 - 2.0 ** (-5.0 - h)) ** P)
                        link(nc.vector.scalar_tensor_tensor(state[:, h], state[:, h], g,
                                                            b[7][:, h * P:(h + 1) * P], ALU.mult, ALU.add))
                    for h in range(RH):
                        link(nc.vector.bn_stats(stats[:, h], yr[:, h]))
                    for h in range(RH):
                        link(nc.vector.bn_aggr(mv[:, h], stats[:, h]))
                    nc.vector.tensor_scalar(gn_var[:], mv[:, :, 1], GN_EPS, None, ALU.add).then_inc(var_here, 1)
                    link(nc.vector.tensor_tensor(yr[:], yr[:], bc(mv[:, :, 0], 2, P), ALU.subtract))
                    v.wait_ge(rstd_here, i + 1)
                    link(nc.vector.tensor_tensor(yr[:], yr[:], bc(gn_rstd[:], 2, P), ALU.mult))
                    link(nc.vector.tensor_tensor(yr[:], yr[:], gn_w[:].rearrange("p (h t) -> p h t", h=RH), ALU.mult))
                    v.wait_ge(exps, i + 1)
                    link(nc.vector.tensor_tensor(ycat[:, 0:RW], yr[:].rearrange("p h t -> p (h t)"),
                                                 pj[:, 3 * RW:4 * RW], ALU.mult))
                    link(nc.vector.tensor_tensor(den[:], sums[:], sink_e[:], ALU.add))
                    link(nc.vector.reciprocal(rden[:], den[:]))
                    for n in (1, 3):
                        v.wait_ge(pTs, 4 * i + n + 1)
                        nc.vector.tensor_copy(pT[:, n * 2:n * 2 + 2].rearrange("p h a q -> p (h a q)"),
                                              b[n][:]).then_inc(pT_v, 1)
                    v.wait_ge(pv, i + 1)
                    nc.vector.tensor_tensor(ycat[:, RW:D].rearrange("p (h c) -> p h c", h=QH),
                                            b[4][:].rearrange("p (h c) -> p h c", h=QH),
                                            bc(rden[:], 2, SD), ALU.mult).then_inc(y_ready, 1)
                    nc.vector.tensor_copy(v_prev[:], pj[:, COLS - SKV:COLS])
                    nc.vector.tensor_copy(masks[:, 0], masks[:, 1])
                    nc.vector.tensor_copy(skT[:, 0], skT[:, 1]).then_inc(kept, 1)
                    for n in range(2):
                        v.wait_ge(yT_his, 2 * i + n + 1)
                        nc.vector.tensor_tensor(yT_lo[:, 4 * n:4 * n + 4].rearrange("p k t -> p (k t)"), b[5 + n][:],
                                                yT_hi[:, 4 * n:4 * n + 4].rearrange("p k t -> p (k t)").bitcast(F32),
                                                ALU.subtract).then_inc(yT_los, 1)
                    v.wait_ge(x_here, 16 * (i + 1))
                    for a in range(2):
                        c = slice(a * 512, (a + 1) * 512)
                        v.wait_ge(mixed, 2 * i + a + 1)
                        ins = nc.vector.scalar_tensor_tensor(hr[:, c], hr[:, c], ALPHA, b[a][:], ALU.mult, ALU.add)
                        ins.then_inc(mix_read, 1)
                        v.wait_ge(mix_read, 2 * i + a + 1)
                        link(nc.vector.bn_stats(lstats[:, a], hr[:, c]))
                    link(nc.vector.bn_aggr(lmv[:], lstats[:]))
                    nc.vector.tensor_scalar(l_var[:], lmv[:, 1:2], LN_EPS, None, ALU.add).then_inc(lvar_here, 1)
                    v.wait_ge(lrstd_here, i + 1)
                    link(nc.vector.tensor_scalar(hr[:], hr[:], lmv[:, 0:1], l_rstd[:], ALU.subtract, ALU.mult))
                    link(nc.vector.tensor_tensor(hr[:], hr[:], ln_w[:], ALU.mult))
                    nc.vector.tensor_tensor(hr[:], hr[:], ln_b[:], ALU.add).then_inc(h_ready, 1)
                    v.wait_ge(hT_his, 2 * i + 1)
                    nc.vector.tensor_tensor(hT_lo[:, 0:4, bass.ts(i, P)], b[2][:].rearrange("p (k t) -> p k t", k=4),
                                            hT_hi[:, 0:4, bass.ts(i, P)].bitcast(F32), ALU.subtract).then_inc(hT_los, 1)
                    v.wait_ge(hT_his, 2 * i + 2)
                    nc.vector.tensor_tensor(hT_lo[:, 4:8, bass.ts(i, P)], b[3][:].rearrange("p (k t) -> p k t", k=4),
                                            hT_hi[:, 4:8, bass.ts(i, P)].bitcast(F32), ALU.subtract).then_inc(hT_los, 1)
                    chain.restart()

                turns(v, TB, turn, last=0)


class TopK:

    def __init__(self, nc, ctx):
        sb = memory(nc, ctx)[0]
        self.nc = nc
        self.places = sb("places", [P, TOPK])
        self.s_cp, self.s_left = sb("s_cp", [P, 2, NK]), sb("s_left", [P, 2, NK])
        self.top, self.top_f = sb("top", [P, 2, TOPK]), sb("top_f", [P, 2, TOPK])
        self.top_i = sb("top_i", [P, 2, TOPK], U32)
        self.cand, self.cand_left = sb("cand", [P, TOPK, TOPK]), sb("cand_left", [P, TOPK * TOPK])
        self.best, self.pos = sb("best", [P, TOPK]), sb("pos", [P, TOPK], U32)
        self.ab, self.ab_f = sb("ab", [P, 2, TOPK], U32), sb("ab_f", [P, 2, TOPK])
        self.pick = sb("pick", [P, 2, TOPK, TOPK])
        self.gap, self.gap_e = sb("gap", [P, TOPK]), sb("gap_e", [P, TOPK])
        self.gap_sum, self.gap_r = sb("gap_sum", [P, 1]), sb("gap_r", [P, 1])
        self.found = sb("found", [P, 3, PH, TOPK])

    def top16(self, link, values, left, out, index):
        nc = self.nc
        link(nc.vector.max(out[:, 0:8], values))
        nc.vector.max_index(index[:, 0:8], out[:, 0:8], values)
        link(nc.vector.match_replace(left, out[:, 0:8], values, LOWEST))
        link(nc.vector.max(out[:, 8:16], left))
        link(nc.vector.max_index(index[:, 8:16], out[:, 8:16], left))

    def side(self, link, p):
        self.top16(link, self.s_cp[:, p], self.s_left[:, p], self.top[:, p], self.top_i[:, p])

    def pairs(self, link):
        nc = self.nc
        link(nc.vector.tensor_tensor(self.cand[:], bc(self.top[:, 0], 2, TOPK), bc(self.top[:, 1], 1, TOPK), ALU.add))
        self.top16(link, self.cand[:].rearrange("p a b -> p (a b)"), self.cand_left[:], self.best, self.pos)

    def gaps(self):
        return self.nc.vector.tensor_scalar(self.gap[:], self.best[:], self.best[:, 0:1], None, ALU.subtract)

    def names(self, link, h):
        nc = self.nc
        nc.vector.tensor_copy(self.top_f[:], self.top_i[:])
        nc.vector.tensor_scalar(self.ab[:, 0], self.pos[:], 4, None, ALU.logical_shift_right)
        link(nc.vector.tensor_scalar(self.ab[:, 1], self.pos[:], 15, None, ALU.bitwise_and))
        link(nc.vector.tensor_copy(self.ab_f[:], self.ab[:]))
        link(nc.vector.tensor_tensor(self.pick[:], bc(self.ab_f[:], 3, TOPK),
                                     bc(bc(self.places[:], 1, TOPK), 1, 2), ALU.is_equal))
        link(nc.vector.tensor_tensor(self.pick[:], self.pick[:], bc(self.top_f[:], 2, TOPK), ALU.mult))
        link(nc.vector.tensor_reduce(self.found[:, 0:2, bass.ds(h, 1), :].rearrange("p a h k -> p a (h k)"),
                                     self.pick[:], AX.X, ALU.add))

    def exp(self):
        return self.nc.scalar.activation(self.gap_e[:], self.gap[:], ACT.Exp, accum_out=self.gap_sum[:])

    def gates(self, link, h):
        nc = self.nc
        link(nc.vector.reciprocal(self.gap_r[:], self.gap_sum[:]))
        link(nc.vector.tensor_scalar(self.found[:, 2, bass.ds(h, 1), :].rearrange("p h k -> p (h k)"),
                                     self.gap_e[:], self.gap_r[:], None, ALU.mult))


def score(nc, d, hT_hi, hT_lo, tk):
    HT = T // 2
    with ExitStack() as ctx:
        sb, bank, sem = memory(nc, ctx)
        keysT = sb("keysT", [P, PAIRS, NK])
        w_raw = [sb(f"wq_raw{p}", [P, KT, P]) for p in range(2)]
        w_hi = [sb(f"wq_hi{p}", [P, KT, P], F32R) for p in range(2)]
        w_lo = [sb(f"wq_lo{p}", [P, KT, P], F32R) for p in range(2)]
        qT = [sb(f"qT{p}", [P, T]) for p in range(2)]
        s_out = sb("s_out", [P, TB, 2, NK])
        q_ps = [[bank(f"q_ps{p}{a}") for a in range(2)] for p in range(2)]
        s_ps = [[bank(f"s_ps{p}{a}") for a in range(2)] for p in range(2)]
        keys_here, places_here = sem("keys_here"), sem("places_here")
        w_here = [sem(f"wq_here{p}") for p in range(2)]
        w_his, w_los = sem("wq_his"), sem("wq_los")
        q_done, q_act, q_dve = sem("q_done"), sem("q_act"), sem("q_dve")
        s_done, s_act, s_dve = sem("s_done"), sem("s_act"), sem("s_dve")
        s_taken, s_stored = sem("s_taken3"), sem("s_stored")
        gaps, exps = sem("gaps3"), sem("exps3")
        own = sem("own_dve3")

        with nc.Block() as block:

            @block.sync
            def _(sp):
                def load(h):
                    for p in range(2):
                        wait(sp, w_los, 2 * h - 1 + p)
                        sp.dma_start(w_raw[p][:], d["w_pq"][2 * h + p]).then_inc(w_here[p], 16)

                load(0)
                sp.dma_start(keysT[:], d["keysT"]).then_inc(keys_here, 16)
                sp.dma_start(tk.places[:], d["iota"][:, 0:TOPK]).then_inc(places_here, 16)
                with sp.Fori(1, PH) as h:
                    load(h)

            @block.tensor
            def _(pe):
                def query(h, p, a):
                    if a == 0:
                        pe.wait_ge(w_los, 2 * h + p + 1)
                    c = slice(a * HT, (a + 1) * HT)
                    for k in range(KT):
                        nc.tensor.matmul(q_ps[p][a][:], w_hi[p][:, k], hT_hi[:, k, c], start=(k == 0), stop=False)
                        nc.tensor.matmul(q_ps[p][a][:], w_hi[p][:, k], hT_lo[:, k, c], start=False, stop=False)
                        last = nc.tensor.matmul(q_ps[p][a][:], w_lo[p][:, k], hT_hi[:, k, c],
                                                start=False, stop=(k == KT - 1))
                    last.then_inc(q_done, 1)

                def scores(h, p):
                    for a in range(2):
                        pe.wait_ge((q_act, q_dve)[a], 2 * h + p + 1)
                        wait(pe, (s_act, s_dve)[a], 2 * h)
                        for n in range(4):
                            tb = 4 * a + n
                            last = nc.tensor.matmul(s_ps[p][a][:, n * P:(n + 1) * P], qT[p][:, tb * P:(tb + 1) * P],
                                                    keysT[:, bass.ds(2 * h + p, 1), :].rearrange("p a k -> p (a k)"),
                                                    start=True, stop=True)
                        last.then_inc(s_done, 1)

                def turn(h):
                    query(h, 0, 0)
                    query(h, 0, 1)
                    query(h, 1, 0)
                    scores(h, 0)
                    query(h, 1, 1)
                    scores(h, 1)

                pe.wait_ge(keys_here, 16)
                turns(pe, PH, turn)

            @block.scalar
            def _(act):
                def split_w(h, p):
                    act.wait_ge(w_here[p], 16 * h + 16)
                    wait(act, q_done, 4 * h - 2 + 2 * p)
                    nc.scalar.activation(w_hi[p][:], w_raw[p][:], ACT.Copy).then_inc(w_his, 1)

                def query(h, p):
                    act.wait_ge(q_done, 4 * h + 2 * p + 1)
                    nc.scalar.activation(qT[p][:, 0:HT], q_ps[p][0][:], ACT.Copy).then_inc(q_act, 1)

                def scores(h, p):
                    act.wait_ge(s_done, 4 * h + 2 * p + 1)
                    wait(act, s_stored, 16 * h)
                    wait(act, s_taken, h)
                    nc.scalar.activation(s_out[:, 0:4, p], s_ps[p][0][:].rearrange("p (t k) -> p t k", k=NK),
                                         ACT.Copy).then_inc(s_act, 1)

                def turn(h):
                    last = isinstance(h, int) and h == PH - 1
                    query(h, 0)
                    if not (isinstance(h, int) and h == 0):
                        act.wait_ge(gaps, h)
                        tk.exp().then_inc(exps, 1)
                    if not last:
                        split_w(h + 1, 0)
                    query(h, 1)
                    scores(h, 0)
                    if not last:
                        split_w(h + 1, 1)
                    scores(h, 1)
                    act.wait_ge(s_act, 2 * h + 2)
                    act.wait_ge(s_dve, 2 * h + 2)
                    act.dma_start(d["scores"].rearrange("n h p k -> h p n k")[h][:, 1:TB],
                                  s_out[:, 1:TB].rearrange("p t a k -> p t (a k)")).then_inc(s_stored, 16)

                for p in range(2):
                    split_w(0, p)
                turns(act, PH, turn)
                act.wait_ge(gaps, PH)
                tk.exp().then_inc(exps, 1)
                act.wait_ge(s_stored, 16 * PH)

            @block.vector
            def _(v):
                chain = Chain(v, own)
                link = chain.link

                def split_w(h, p):
                    v.wait_ge(w_his, 2 * h + p + 1)
                    nc.vector.tensor_tensor(w_lo[p][:], w_raw[p][:], w_hi[p][:].bitcast(F32),
                                            ALU.subtract).then_inc(w_los, 1)

                def query(h, p):
                    v.wait_ge(q_done, 4 * h + 2 * p + 2)
                    nc.vector.tensor_copy(qT[p][:, HT:T], q_ps[p][1][:]).then_inc(q_dve, 1)

                def scores(h, p):
                    v.wait_ge(s_done, 4 * h + 2 * p + 2)
                    wait(v, s_stored, 16 * h)
                    nc.vector.tensor_copy(s_out[:, 4:8, p],
                                          s_ps[p][1][:].rearrange("p (t k) -> p t k", k=NK)).then_inc(s_dve, 1)

                def finish_top(h):
                    tk.names(link, h)
                    v.wait_ge(exps, h + 1)
                    tk.gates(link, h)

                def turn(h):
                    last = isinstance(h, int) and h == PH - 1
                    query(h, 0)
                    if not last:
                        split_w(h + 1, 0)
                    if not (isinstance(h, int) and h == 0):
                        finish_top(h - 1)
                    scores(h, 0)
                    query(h, 1)
                    if not last:
                        split_w(h + 1, 1)
                    scores(h, 1)
                    v.wait_ge(s_act, 2 * h + 2)
                    link(nc.vector.tensor_scalar(tk.s_cp[:], s_out[:, 0], 1.0, None, ALU.mult))
                    nc.vector.engine_nop().then_inc(s_taken, 1)
                    tk.side(link, 0)
                    tk.side(link, 1)
                    tk.pairs(link)
                    tk.gaps().then_inc(gaps, 1)
                    chain.restart()

                for p in range(2):
                    split_w(0, p)
                v.wait_ge(places_here, 16)
                turns(v, PH, turn)
                finish_top(PH - 1)


def experts_in(nc, d, hT_hi, hT_lo, tk):
    HT = T // 2
    Q = PH // 2
    with ExitStack() as ctx:
        sb, bank, sem = memory(nc, ctx)
        ident, iota = sb("ident4", [P, P]), sb("iota", [P, P])
        u_raw = [sb(f"u_raw{e}", [P, KT, P]) for e in range(2)]
        u_hi = [sb(f"u_hi{e}", [P, KT, P], F32R) for e in range(2)]
        u_lo = [sb(f"u_lo{e}", [P, KT, P], F32R) for e in range(2)]
        z_sb = [sb(f"z_sb{e}", [P, T]) for e in range(2)]
        s_in = [sb(f"s_in{j}", [P, 2, NK]) for j in range(2)]
        iT = sb("iT", [P, 2, P])
        gT_hi, gT_lo = sb("gT_hi", [P, P], F32R), sb("gT_lo", [P, P])
        cur = [sb(f"cur{b}", [P, 4, GT]) for b in range(2)]
        hot2 = [sb(f"hot2_{g}", [P, 4, NK], F32R) for g in range(2)]
        hot1 = [sb(f"hot1_{g}", [P, 4, NK]) for g in range(2)]
        hot1_g = [sb(f"hot1_g{g}", [P, 4, 2, NK], F32R) for g in range(2)]
        g_lo = [sb(f"g_lo{g}", [P, 4, NK]) for g in range(2)]
        g_sb = [sb(f"g_sb{b}", [P, NK, GT]) for b in range(2)]
        z_ps = [[bank(f"z_ps{e}{a}") for a in range(2)] for e in range(2)]
        g_ps = [ctx.enter_context(nc.psum_tensor(f"g_ps{g}", [P, 4, 2, NK], F32)) for g in range(2)]
        const_here = sem("const4")
        u_here = [sem(f"u_here{e}") for e in range(2)]
        u_hi_in = [sem(f"u_hi_in{e}") for e in range(2)]
        u_lo_in = [sem(f"u_lo_in{e}") for e in range(2)]
        z_done = [sem(f"z_done{e}") for e in range(2)]
        z_read = [sem(f"z_read{e}") for e in range(2)]
        z_stored = [sem(f"z_stored{e}") for e in range(2)]
        s_here = [sem(f"s_here{j}") for j in range(2)]
        s_taken = [sem(f"s_taken{j}") for j in range(2)]
        gaps, exps = sem("gaps"), sem("exps4")
        found_in, found_T = sem("found_in"), sem("found_T")
        hot_in = [sem(f"hot_in{g}") for g in range(2)]
        hot_g_in = [sem(f"hot_g_in{g}") for g in range(2)]
        g_done = [sem(f"g_done{g}") for g in range(2)]
        g_lo_in = [sem(f"g_lo_in{g}") for g in range(2)]
        g_read = [sem(f"g_read{g}") for g in range(2)]
        g_stored = [sem(f"g_stored{b}") for b in range(2)]
        own = sem("own_dve4")

        def is_(n, value):
            return isinstance(n, int) and n == value

        with nc.Block() as block:

            @block.sync
            def _(sp):
                scores = d["scores"].rearrange("n h p k -> (n h) p k")

                def load(m, heads):
                    for j in range(2):
                        if heads:
                            wait(sp, s_taken[j], m)
                            sp.dma_start(s_in[j][:], scores[2 * m + j + PH].rearrange(
                                "p (a k) -> p a k", a=2)).then_inc(s_here[j], 16)
                        for e in range(2):
                            wait(sp, u_lo_in[e], 2 * m + j)
                            sp.dma_start(u_raw[e][:], d["uT"][4 * m + 2 * j + e]).then_inc(u_here[e], 16)

                sp.dma_start(ident[:], d["ident"]).then_inc(const_here, 16)
                sp.dma_start(iota[:], d["iota"]).then_inc(const_here, 16)
                load(0, True)
                with sp.Fori(1, Q * (TB - 1)) as m:
                    load(m, True)
                with sp.Fori(Q * (TB - 1), Q * TB) as m:
                    load(m, False)

            @block.tensor
            def _(pe):
                pe.wait_ge(const_here, 32)

                def z_half(m, n):
                    j, e, a = n // 4, n // 2 % 2, n % 2
                    if a == 0:
                        pe.wait_ge(u_lo_in[e], 2 * m + j + 1)
                        wait(pe, z_read[e], 2 * (2 * m + j))
                    cols = slice(a * HT, (a + 1) * HT)
                    for k in range(KT):
                        nc.tensor.matmul(z_ps[e][a][:], u_hi[e][:, k], hT_hi[:, k, cols], start=(k == 0), stop=False)
                        nc.tensor.matmul(z_ps[e][a][:], u_hi[e][:, k], hT_lo[:, k, cols], start=False, stop=False)
                        last = nc.tensor.matmul(z_ps[e][a][:], u_lo[e][:, k], hT_hi[:, k, cols],
                                                start=False, stop=(k == KT - 1))
                    last.then_inc(z_done[e], 1)

                def gates(m, n):
                    g = n % 2
                    pe.wait_ge(hot_g_in[g], 4 * m + n // 2 + 1)
                    wait(pe, g_read[g], 4 * m + n // 2)
                    for t in range(4):
                        last = nc.tensor.matmul(g_ps[g][:, t].rearrange("p w i -> p (w i)"), hot2[g][:, t],
                                                hot1_g[g][:, t].rearrange("p w i -> p (w i)"), start=True, stop=True)
                    last.then_inc(g_done[g], 1)

                def turn(tb):
                    for q in range(Q):
                        m = tb * Q + q
                        z_half(m, 0)
                        if q == 0:
                            wait(pe, found_in, tb)
                            wait(pe, g_read[0], 4 * m)
                            for n in range(3):
                                last = nc.tensor.transpose(g_ps[0][:, n, 0], tk.found[:, n].rearrange("p h k -> p (h k)"),
                                                           ident[:])
                            last.then_inc(found_T, 1)
                        for n in range(1, 8):
                            z_half(m, n)
                            gates(m, n - 1)
                        gates(m, 7)

                turns(pe, TB, turn)

            @block.scalar
            def _(act):
                def split_u(m, i):
                    e, j = i % 2, i // 2
                    act.wait_ge(u_here[e], 16 * (2 * m + j + 1))
                    wait(act, z_done[e], 2 * (2 * m + j))
                    nc.scalar.activation(u_hi[e][:], u_raw[e][:], ACT.Copy).then_inc(u_hi_in[e], 1)

                def store_gates(m, b):
                    act.wait_ge(g_read[0], 4 * m + 4)
                    act.wait_ge(g_read[1], 4 * m + 4)
                    act.dma_start(d["gates"][m], g_sb[b][:]).then_inc(g_stored[b], 16)

                def take_gates_lo(m, n):
                    g = n % 2
                    act.wait_ge(g_done[g], 4 * m + n // 2 + 1)
                    nc.scalar.activation(g_lo[g][:], g_ps[g][:, :, 1], ACT.Copy).then_inc(g_lo_in[g], 1)

                def turn(tb):
                    heads = not is_(tb, TB - 1)
                    for q in range(Q):
                        m = tb * Q + q
                        for n in range(8):
                            j, e, a = n // 4, n // 2 % 2, n % 2
                            if a == 0 and not is_(4 * m + n // 2, NK - 1):
                                split_u(m, n // 2 + 1)
                            if heads and n % 4 == 3:
                                act.wait_ge(gaps, 2 * m + j + 1)
                                tk.exp().then_inc(exps, 1)
                            act.wait_ge(z_done[e], 2 * (2 * m + j) + a + 1)
                            if a == 0:
                                wait(act, z_stored[e], 16 * (2 * m + j))
                            nc.scalar.activation(z_sb[e][:, a * HT:(a + 1) * HT], z_ps[e][a][:],
                                                 ACT.Copy).then_inc(z_read[e], 1)
                            if a == 1:
                                act.wait_ge(z_read[e], 2 * (2 * m + j) + 2)
                                act.dma_start(d["z"][4 * m + 2 * j + e], z_sb[e][:]).then_inc(z_stored[e], 16)
                            if n:
                                take_gates_lo(m, n - 1)
                            if n == 1 and not is_(m, 0):
                                store_gates(m - 1, (q + 1) % 2)
                        take_gates_lo(m, 7)

                split_u(0, 0)
                turns(act, TB, turn)
                store_gates(Q * TB - 1, 1)
                for e in range(2):
                    act.wait_ge(z_stored[e], 16 * NK // 2)
                    act.wait_ge(g_stored[e], 16 * Q * TB // 2)

            @block.gpsimd
            def _(pool):
                def split_u(m, i):
                    e, j = i % 2, i // 2
                    pool.wait_ge(u_hi_in[e], 2 * m + j + 1)
                    nc.gpsimd.tensor_tensor(u_lo[e][:], u_raw[e][:], u_hi[e][:].bitcast(F32),
                                            ALU.subtract).then_inc(u_lo_in[e], 1)

                def turn(tb):
                    for q in range(Q):
                        m = tb * Q + q
                        for n in range(8):
                            if n % 2 == 0 and not is_(4 * m + n // 2, NK - 1):
                                split_u(m, n // 2 + 1)
                            g = n % 2
                            pool.wait_ge(hot_in[g], 4 * m + n // 2 + 1)
                            for w in range(2):
                                last = nc.gpsimd.tensor_tensor(hot1_g[g][:, :, w], hot1[g][:],
                                                               bc(cur[q % 2][:, 2 + w, 4 * n:4 * n + 4], 2, NK), ALU.mult)
                            last.then_inc(hot_g_in[g], 1)

                split_u(0, 0)
                turns(pool, TB, turn)

            @block.vector
            def _(v):
                chain = Chain(v, own)
                link = chain.link
                v.wait_ge(const_here, 32)

                def top_piece(piece, m, j, h):
                    if piece == 0:
                        v.wait_ge(s_here[j], 16 * (m + 1))
                        link(nc.vector.tensor_copy(tk.s_cp[:], s_in[j][:]))
                        nc.vector.engine_nop().then_inc(s_taken[j], 1)
                        tk.side(link, 0)
                    elif piece == 1:
                        tk.side(link, 1)
                    elif piece == 2:
                        tk.pairs(link)
                        tk.gaps().then_inc(gaps, 1)
                    else:
                        tk.names(link, h)
                        v.wait_ge(exps, 2 * m + j + 1)
                        tk.gates(link, h)

                def add_gates(m, b, n):
                    g = n % 2
                    v.wait_ge(g_lo_in[g], 4 * m + n // 2 + 1)
                    nc.vector.tensor_tensor(g_sb[b][:, :, 4 * n:4 * n + 4].rearrange("p i t -> p t i"),
                                            g_ps[g][:, :, 0], g_lo[g][:], ALU.add).then_inc(g_read[g], 1)

                def turn(tb):
                    heads = not is_(tb, TB - 1)
                    v.wait_ge(found_T, tb + 1)
                    nc.vector.tensor_copy(iT[:], g_ps[0][:, 0:2, 0])
                    link(nc.vector.tensor_copy(gT_hi[:], g_ps[0][:, 2, 0]))
                    link(nc.vector.tensor_tensor(gT_lo[:], g_ps[0][:, 2, 0], gT_hi[:].bitcast(F32), ALU.subtract))
                    for q in range(Q):
                        m, b, t0 = tb * Q + q, q % 2, q * GT
                        for g in range(2):
                            wait(v, hot_g_in[g], 4 * (m - 1))
                        nc.vector.tensor_copy(cur[b][:, 0:2], iT[:, :, t0:t0 + GT])
                        nc.vector.tensor_copy(cur[b][:, 2], gT_hi[:, t0:t0 + GT].bitcast(F32))
                        link(nc.vector.tensor_copy(cur[b][:, 3], gT_lo[:, t0:t0 + GT]))
                        for n in range(8):
                            g = n % 2
                            wait(v, g_done[g], 4 * m + n // 2)
                            for hot, side in ((hot2, 1), (hot1, 0)):
                                last = nc.vector.tensor_tensor(hot[g][:], bc(iota[:], 1, 4),
                                                               bc(cur[b][:, side, 4 * n:4 * n + 4], 2, NK),
                                                               ALU.is_equal)
                            last.then_inc(hot_in[g], 1)
                            if heads:
                                top_piece(n % 4, m, n // 4, q * 2 + n // 4)
                            if n == 0:
                                wait(v, g_stored[b], 16 * (2 * tb + q // 2))
                            else:
                                add_gates(m, b, n - 1)
                        add_gates(m, b, 7)
                        chain.restart()
                    if heads:
                        nc.vector.engine_nop().then_inc(found_in, 1)

                turns(v, TB, turn)


def experts_out(nc, d):
    with ExitStack() as ctx:
        sb, bank, sem = memory(nc, ctx)
        z_in = [sb(f"z_in{p}", [P, GROUP, T]) for p in range(2)]
        g_in = [sb(f"g_in{p}", [P, T // GT, GROUP * GT]) for p in range(2)]
        v_raw = [sb(f"v_raw{e}", [P, D]) for e in range(2)]
        v_hi = [sb(f"v_hi{p}", [P, GROUP, D], F32R) for p in range(2)]
        v_lo = [sb(f"v_lo{p}", [P, GROUP, D], F32R) for p in range(2)]
        a_hi, a_lo = sb("a_hi", [P, GROUP, T], F32R), sb("a_lo", [P, GROUP, T], F32R)
        y = sb("y", [P, TB, D])
        st, mv = sb("st5", [P, TB, 2, 6]), sb("mv5", [P, TB, 2])
        var, rstd, minus_half = sb("var5", [P, TB]), sb("rstd5", [P, TB]), sb("minus_half5", [P, TB])
        ln = z_in[0]
        y_ps = [bank(f"y_ps{n}") for n in range(8)]
        z_here = [sem(f"z_here{p}") for p in range(2)]
        v_here = [sem(f"v_here{e}") for e in range(2)]
        v_hi_in = [sem(f"v_hi_in{e}") for e in range(2)]
        v_lo_in = [sem(f"v_lo_in{e}") for e in range(2)]
        h_here, h_scaled, ln_here = sem("h_here"), sem("h_scaled"), sem("ln_here")
        gelu_in, prod_in, a_hi_in, a_lo_in = sem("gelu_in"), sem("prod_in"), sem("a_hi_in"), sem("a_lo_in")
        y_done = sem("y_done")
        y_read = [sem(f"y_read{n}") for n in range(8)]
        var_in, rstd_in, y_in, stored = sem("var_in"), sem("rstd_in"), sem("y_in"), sem("stored5")
        own, own_pool = sem("own_dve5"), sem("own_pool5")

        def groups(step):
            def all_of(eng):
                step(0, 0, 0, True, False)
                step(1, 1, 0, True, True)
                step(2, 0, 1, True, True)
                with eng.Fori(1, NG // 2 - 1) as n:
                    step(2 * n + 1, 1, n, True, True)
                    step(2 * n + 2, 0, n + 1, True, True)
                step(NG - 1, 1, NG // 2 - 1, True, True)
                step(NG, 0, NG // 2, False, True)
            return all_of

        def tokens(s):
            return slice(s * P, (s + 1) * P)

        with nc.Block() as block:

            @block.sync
            def _(sp):
                def load_z(r, p):
                    sp.dma_start(z_in[p][:], d["z"].rearrange("(r i) e t -> r e i t", i=GROUP)[r]).then_inc(z_here[p], 16)
                    sp.dma_start(g_in[p][:], d["gates"].rearrange("c e (r i) t -> r e c (i t)", i=GROUP)[r]).then_inc(
                        z_here[p], 16)

                def load_v(r):
                    for i in range(GROUP):
                        wait(sp, v_lo_in[i % 2], 2 * r + i // 2)
                        sp.dma_start(v_raw[i % 2][:], d["v"][GROUP * r + i]).then_inc(v_here[i % 2], 16)

                load_z(0, 0)
                load_v(0)
                load_z(1, 1)
                load_v(1)
                with sp.Fori(0, NG // 2 - 1) as n:
                    for p in range(2):
                        sp.wait_ge(a_lo_in, TB * (2 * n + p + 1))
                        load_z(2 * n + 2 + p, p)
                        load_v(2 * n + 2 + p)
                sp.wait_ge(a_lo_in, TB * (NG - 1))
                sp.dma_start(ln[:, 0], d["ln2_w"]).then_inc(ln_here, 16)
                sp.dma_start(ln[:, 1], d["ln2_b"]).then_inc(ln_here, 16)
                for tb in range(TB):
                    sp.wait_ge(y_in, tb + 1)
                    sp.dma_start(d["out"][tokens(tb)], y[:, tb]).then_inc(stored, 16)
                sp.wait_ge(stored, 16 * TB)

            @block.tensor
            def _(pe):
                def turn(n):
                    for p in range(2):
                        r = 2 * n + p
                        for e in range(2):
                            pe.wait_ge(v_lo_in[e], 2 * r + 2)
                        for s in range(TB):
                            pe.wait_ge(a_lo_in, TB * r + s + 1)
                            for a in range(2):
                                bk = (2 * s + a) % 8
                                c = slice(a * 512, (a + 1) * 512)
                                wait(pe, y_read[bk], 2 * r + s // 4)
                                for i in range(GROUP):
                                    ah, al = a_hi[:, i, tokens(s)], a_lo[:, i, tokens(s)]
                                    nc.tensor.matmul(y_ps[bk][:], ah, v_hi[p][:, i, c], start=(i == 0), stop=False)
                                    nc.tensor.matmul(y_ps[bk][:], ah, v_lo[p][:, i, c], start=False, stop=False)
                                    last = nc.tensor.matmul(y_ps[bk][:], al, v_hi[p][:, i, c],
                                                            start=False, stop=(i == GROUP - 1))
                                last.then_inc(y_done, 1)

                turns(pe, NG // 2, turn)

            @block.scalar
            def _(act):
                def step(r, p, use, prepare, add):
                    if not prepare:
                        return

                    def hi(s):
                        act.wait_ge(prod_in, TB * r + s + 1)
                        if add:
                            act.wait_ge(y_done, 16 * (r - 1) + 2 * s + 2)
                        nc.scalar.activation(a_hi[:, :, tokens(s)], z_in[p][:, :, tokens(s)],
                                             ACT.Copy).then_inc(a_hi_in, 1)

                    act.wait_ge(z_here[p], 32 * (use + 1))
                    if add:
                        wait(act, y_done, 16 * (r - 1))
                    for s in range(TB):
                        nc.scalar.activation(z_in[p][:, :, tokens(s)], z_in[p][:, :, tokens(s)],
                                             ACT.Gelu).then_inc(gelu_in, 1)
                        if s % 2 == 0:
                            i = s // 2
                            act.wait_ge(v_here[i % 2], 16 * (2 * r + i // 2 + 1))
                            nc.scalar.activation(v_hi[p][:, i], v_raw[i % 2][:], ACT.Copy).then_inc(v_hi_in[i % 2], 1)
                        if s:
                            hi(s - 1)
                    hi(TB - 1)

                groups(step)(act)

            @block.gpsimd
            def _(pool):
                pool.dma_start(y[:], d["h"].rearrange("n p c -> p n c")).then_inc(h_here, 16)
                nc.gpsimd.memset(minus_half[:], -0.5).then_inc(own_pool, 1)
                with pool.Fori(0, NG // 2) as n:
                    for p in range(2):
                        r = 2 * n + p
                        for i in range(GROUP):
                            pool.wait_ge(v_hi_in[i % 2], 2 * r + i // 2 + 1)
                            nc.gpsimd.tensor_tensor(v_lo[p][:, i], v_raw[i % 2][:], v_hi[p][:, i].bitcast(F32),
                                                    ALU.subtract).then_inc(v_lo_in[i % 2], 1)
                pool.wait_ge(own_pool, 1)
                pool.wait_ge(var_in, 1)
                nc.gpsimd.tensor_tensor(rstd[:], var[:], minus_half[:], ALU.pow).then_inc(rstd_in, 1)

            @block.vector
            def _(v):
                chain = Chain(v, own)
                link = chain.link

                def step(r, p, use, prepare, add):
                    def lo(s):
                        v.wait_ge(a_hi_in, TB * r + s + 1)
                        nc.vector.tensor_tensor(a_lo[:, :, tokens(s)], z_in[p][:, :, tokens(s)],
                                                a_hi[:, :, tokens(s)].bitcast(F32), ALU.subtract).then_inc(a_lo_in, 1)

                    for s in range(TB):
                        if prepare:
                            v.wait_ge(gelu_in, TB * r + s + 1)
                            zs = z_in[p][:, :, tokens(s)].rearrange("p i (c t) -> p i c t", t=GT)
                            gs = g_in[p][:, 4 * s:4 * s + 4].rearrange("p c (i t) -> p i c t", t=GT)
                            nc.vector.tensor_tensor(zs, zs, gs, ALU.mult).then_inc(prod_in, 1)
                        if add:
                            for a in range(2):
                                bk = (2 * s + a) % 8
                                c = slice(a * 512, (a + 1) * 512)
                                v.wait_ge(y_done, 16 * (r - 1) + 2 * s + a + 1)
                                nc.vector.tensor_tensor(y[:, s, c], y_ps[bk][:], y[:, s, c], ALU.add).then_inc(
                                    y_read[bk], 1)
                        if prepare and s:
                            lo(s - 1)
                    if prepare:
                        lo(TB - 1)
                    if not add:
                        v.wait_ge(h_here, 16)
                        nc.vector.tensor_scalar(y[:], y[:], ALPHA, None, ALU.mult).then_inc(h_scaled, 1)
                        v.wait_ge(h_scaled, 1)

                groups(step)(v)
                for bk in range(8):
                    v.wait_ge(y_read[bk], 2 * NG)
                for s in range(TB):
                    for a in range(2):
                        link(nc.vector.bn_stats(st[:, s, a], y[:, s, a * 512:(a + 1) * 512]))
                for s in range(TB):
                    link(nc.vector.bn_aggr(mv[:, s], st[:, s]))
                nc.vector.tensor_scalar(var[:], mv[:, :, 1], LN_EPS, None, ALU.add).then_inc(var_in, 1)
                v.wait_ge(rstd_in, 1)
                v.wait_ge(ln_here, 32)
                for s in range(TB):
                    link(nc.vector.tensor_scalar(y[:, s], y[:, s], mv[:, s, 0:1], rstd[:, s:s + 1],
                                                 ALU.subtract, ALU.mult))
                    link(nc.vector.tensor_tensor(y[:, s], y[:, s], ln[:, 0], ALU.mult))
                    nc.vector.tensor_tensor(y[:, s], y[:, s], ln[:, 1], ALU.add).then_inc(y_in, 1)


PHASES = [1, 2, 3, 4, 5]


def build(nc, d):
    project(nc, d)
    if 2 not in PHASES:
        return
    with ExitStack() as ctx:
        hT_hi = ctx.enter_context(nc.sbuf_tensor("hT_hi", [P, KT, T], F32R))
        hT_lo = ctx.enter_context(nc.sbuf_tensor("hT_lo", [P, KT, T], F32R))
        attend(nc, d, hT_hi, hT_lo)
        if 3 not in PHASES:
            return
        tk = TopK(nc, ctx)
        score(nc, d, hT_hi, hT_lo, tk)
        if 4 not in PHASES:
            return
        experts_in(nc, d, hT_hi, hT_lo, tk)
    if 5 in PHASES:
        experts_out(nc, d)


def tables():
    f = np.float32
    pos = np.arange(T, dtype=f)

    def rope(dim):
        inv = f(1.0) / (f(10000.0) ** (np.arange(0, dim, 2, dtype=f) / f(dim)))
        ang = pos[:, None] * inv[None, :]
        both = np.stack([np.cos(ang), np.sin(ang)], axis=1).astype(f)
        return np.ascontiguousarray(both.reshape(TB, P, 2, dim // 2).transpose(1, 0, 2, 3))

    idx = np.arange(P)
    log_g = np.log(1.0 - 2.0 ** (-5.0 - np.arange(RH)))
    diff = idx[:, None] - idx[None, :]
    decay = np.where(diff[None] >= 0, np.exp(np.maximum(diff, 0)[None] * log_g[:, None, None]), 0.0)
    scale = RD ** -0.5
    q, k = np.arange(P)[:, None] + P, np.arange(2 * P)[None, :]
    seen = (q - k >= 0) & (q - k < P)
    return {
        "rope": rope(RD), "rope64": rope(SD),
        "decayT": np.ascontiguousarray(decay.transpose(2, 0, 1) * scale).astype(f),
        "zeta": (np.exp((P - 1.0 - idx)[:, None] * log_g[None]) * scale).astype(f),
        "xi": np.exp((idx + 1.0)[:, None] * log_g[None]).astype(f),
        "masks": np.stack([np.where(seen & (k >= P), 0.0, NEG), np.where(seen, 0.0, NEG)], axis=1).astype(f),
        "ident": np.eye(P, dtype=f),
        "iota": np.broadcast_to(np.arange(P, dtype=f), (P, P)).copy(),
    }


def rows(a):
    return np.ascontiguousarray(np.broadcast_to(a, (P,) + a.shape))


def kernel(x, w_in, ret_gn_w, swa_sinks, w_out, ln1_w, ln1_b, w_pq, peer_sub_keys,
           peer_u, peer_v, ln2_w, ln2_b):
    import concourse.bacc as bacc
    from concourse.bass_utils import run_bass_kernel_spmd

    a = {k: np.asarray(v) for k, v in dict(
        x=x, w_in=w_in, ret_gn_w=ret_gn_w, swa_sinks=swa_sinks, w_out=w_out, ln1_w=ln1_w, ln1_b=ln1_b,
        w_pq=w_pq, keys=peer_sub_keys, u=peer_u, v=peer_v, ln2_w=ln2_w, ln2_b=ln2_b).items()}
    assert a["x"].shape == (1, T, D) and a["w_in"].shape == (1, D, COLS)

    def slices(w):
        return np.ascontiguousarray(w.reshape(KT, P, -1).transpose(1, 0, 2))

    heads = [g * G + n for n in range(G) for g in range(KVH)]
    cols = np.concatenate([np.arange(4 * RW)] + [4 * RW + h * SD + np.arange(SD) for h in heads]
                          + [np.arange(4 * RW + SW, COLS)])
    arrays = {
        "x": a["x"][0],
        "xT": slices(a["x"][0].T),
        "w_in": slices(a["w_in"][0][:, cols]),
        "w_out": slices(a["w_out"][0]),
        "w_pq": np.ascontiguousarray(a["w_pq"][0].reshape(KT, P, PAIRS, P).transpose(2, 1, 0, 3)),
        "keysT": np.ascontiguousarray(a["keys"][0].reshape(PAIRS, NK, P).transpose(2, 0, 1)),
        "uT": np.ascontiguousarray(a["u"][0].reshape(NK, NK, KT, P).transpose(0, 3, 2, 1)),
        "v": a["v"][0].reshape(NK, NK, D),
        "gn_w": rows(a["ret_gn_w"][0]), "sinks": rows(a["swa_sinks"][0]),
        "ln1_w": rows(a["ln1_w"][0]), "ln1_b": rows(a["ln1_b"][0]),
        "ln2_w": rows(a["ln2_w"][0]), "ln2_b": rows(a["ln2_b"][0]),
        **tables(),
    }
    nc = bacc.Bacc("TRN2", target_bir_lowering=False, num_devices=1)
    d = {n: nc.dram_tensor(f"in_{n}", t.shape, F32, kind="ExternalInput").ap() for n, t in arrays.items()}
    for n, shape in (("proj", (T, COLS)), ("h", (TB, P, D)), ("scores", (TB, PH, P, 2 * NK)),
                     ("z", (NK, P, T)), ("gates", (T // GT, P, NK, GT))):
        d[n] = nc.dram_tensor(n, shape, F32, kind="Internal").ap()
    d["out"] = nc.dram_tensor("out", (T, D), F32, kind="ExternalOutput").ap()
    build(nc, d)
    r = run_bass_kernel_spmd(nc, [{f"in_{n}": t for n, t in arrays.items()}], core_ids=[0])
    return r.results[0]["out"].reshape(1, T, D)
```

```python
from contextlib import ExitStack

import numpy as np
import concourse.bass as bass
from concourse import mybir

F32 = mybir.dt.float32
F32R = mybir.dt.float32r
U32 = mybir.dt.uint32
ACT = mybir.ActivationFunctionType
ALU = mybir.AluOpType
AX = mybir.AxisListType

P = 128
D = 1024
T = 1024
KT = D // P
TB = T // P
RH, RD = 4, 128
RW = RH * RD
QH, KVH, SD = 8, 2, 64
G = QH // KVH
SW, SKV = QH * SD, KVH * SD
COLS = 4 * RW + SW + 2 * SKV
ALPHA = 2.0 ** 0.25
LN_EPS, GN_EPS = 1e-5, 1e-6
PH, NK, TOPK = 8, 128, 16
PAIRS = 2 * PH
NEG = -1e30
LOWEST = -3.0e38
GROUP = 4
GT = 32
NG = NK // GROUP


def bc(ap, axis, n):
    v = ap.unsqueeze(axis)
    shape = list(v.shape)
    shape[axis] = n
    return v.to_broadcast(shape)


def wait(eng, sem, value):
    if not isinstance(value, int) or value > 0:
        eng.wait_ge(sem, value)


def turns(eng, n, turn, last=1):
    turn(0)
    with eng.Fori(1, n - last) as i:
        turn(i)
    for i in range(n - last, n):
        turn(i)


class Chain:

    def __init__(self, eng, sem):
        self.eng, self.sem, self.n = eng, sem, 0

    def link(self, ins):
        self.n += 1
        ins.then_inc(self.sem, 1)
        self.eng.wait_ge(self.sem, self.n)

    def restart(self):
        self.eng.wait_ge(self.sem, self.n)
        self.eng.sem_clear(self.sem)
        self.n = 0


def memory(nc, ctx):
    def sb(name, shape, dt=F32):
        return ctx.enter_context(nc.sbuf_tensor(name, shape, dt))

    def bank(name):
        return ctx.enter_context(nc.psum_tensor(name, [P, 512], F32))

    def sem(name):
        return ctx.enter_context(nc.semaphore(name))

    return sb, bank, sem


def project(nc, d):
    chunks = [("rot", 0, 512), ("rot", 512, 512), ("copy", 1024, 512), ("silu", 1536, 512),
              ("rot64", 2048, 512), ("kv", 2560, 256)]
    NB = 4
    OUT = 3
    with ExitStack() as ctx:
        sb, bank, sem = memory(nc, ctx)
        x_raw = sb("x_raw", [P, KT, T])
        x_hi = sb("x_hi", [P, KT, T], F32R)
        x_lo = sb("x_lo", [P, KT, T], F32R)
        w_raw = sb("w_raw", [P, KT, 512])
        w_hi = sb("w_hi", [P, 2, KT, 512], F32R)
        w_lo = sb("w_lo", [P, 2, KT, 512], F32R)
        rope = sb("rope", [P, TB, 2, RD // 2])
        rope64 = sb("rope64", [P, TB, 2, SD // 2])
        t_cos = sb("t_cos", [P, 512])
        t_sin = sb("t_sin", [P, 512])
        res = sb("res", [P, OUT, 512])
        ps = [bank(f"pp{i}") for i in range(NB)]
        x_here = [sem(f"x_here{k}") for k in range(KT)]
        w_here = [sem(f"w_here{k}") for k in range(KT)]
        rope_here = sem("rope_here")
        x_his, x_los = sem("x_his"), sem("x_los")
        w_his, w_los = sem("w_his"), sem("w_los")
        tile_done = sem("tile_done")
        res_act, res_dve = sem("res_act"), sem("res_dve")
        stored = [sem(f"stored{i}") for i in range(OUT)]
        own = sem("own_dve1")
        tiles = [(c, tb) for c in range(len(chunks)) for tb in range(TB)]
        by_act = [chunks[c][0] in ("copy", "silu") for c, _ in tiles]

        def finished(n):
            return (res_act, sum(by_act[:n + 1])) if by_act[n] else (res_dve, n + 1 - sum(by_act[:n + 1]))

        with nc.Block() as block:

            @block.sync
            def _(sp):
                sp.dma_start(rope[:], d["rope"]).then_inc(rope_here, 16)
                sp.dma_start(rope64[:], d["rope64"]).then_inc(rope_here, 16)
                for k in range(KT):
                    sp.dma_start(x_raw[:, k], d["xT"][:, k]).then_inc(x_here[k], 16)
                    sp.dma_start(w_raw[:, k], d["w_in"][:, k, 0:512]).then_inc(w_here[k], 16)
                for n, (c, tb) in enumerate(tiles):
                    if tb == 0 and c + 1 < len(chunks):
                        _, c0, w = chunks[c + 1]
                        for k in range(KT):
                            sp.wait_ge(w_los, c * KT + k + 1)
                            sp.dma_start(w_raw[:, k, 0:w], d["w_in"][:, k, c0:c0 + w]).then_inc(w_here[k], 16)
                    _, c0, w = chunks[c]
                    sp.wait_ge(*finished(n))
                    sp.dma_start(d["proj"][tb * P:(tb + 1) * P, c0:c0 + w],
                                 res[:, n % OUT, 0:w]).then_inc(stored[n % OUT], 16)
                for i in range(OUT):
                    sp.wait_ge(stored[i], 16 * len(range(i, len(tiles), OUT)))

            @block.tensor
            def _(pe):
                for n, (c, tb) in enumerate(tiles):
                    w = chunks[c][2]
                    if n >= NB:
                        pe.wait_ge(*finished(n - NB))
                    for k in range(KT):
                        if tb == 0:
                            if c == 0:
                                pe.wait_ge(x_los, k + 1)
                            pe.wait_ge(w_los, c * KT + k + 1)
                        xh = x_hi[:, k, tb * P:(tb + 1) * P]
                        xl = x_lo[:, k, tb * P:(tb + 1) * P]
                        wh, wl = w_hi[:, c % 2, k, 0:w], w_lo[:, c % 2, k, 0:w]
                        o = ps[n % NB][:, 0:w]
                        nc.tensor.matmul(o, xh, wh, start=(k == 0), stop=False)
                        nc.tensor.matmul(o, xh, wl, start=False, stop=False)
                        last = nc.tensor.matmul(o, xl, wh, start=False, stop=(k == KT - 1))
                    last.then_inc(tile_done, 1)

            @block.scalar
            def _(act):
                def split_w(c, k):
                    w = chunks[c][2]
                    act.wait_ge(w_here[k], 16 * (c + 1))
                    if c >= 2:
                        act.wait_ge(tile_done, TB * (c - 1))
                    nc.scalar.activation(w_hi[:, c % 2, k, 0:w], w_raw[:, k, 0:w], ACT.Copy).then_inc(w_his, 1)

                for k in range(KT):
                    act.wait_ge(x_here[k], 16)
                    nc.scalar.activation(x_hi[:, k], x_raw[:, k], ACT.Copy).then_inc(x_his, 1)
                    split_w(0, k)
                for n, (c, tb) in enumerate(tiles):
                    if c + 1 < len(chunks):
                        split_w(c + 1, tb)
                    if by_act[n]:
                        act.wait_ge(tile_done, n + 1)
                        if n >= OUT:
                            act.wait_ge(stored[n % OUT], 16 * (n // OUT))
                        f = ACT.Silu if chunks[c][0] == "silu" else ACT.Copy
                        nc.scalar.activation(res[:, n % OUT, :], ps[n % NB][:], f).then_inc(res_act, 1)

            @block.gpsimd
            def _(pool):
                for c, (_, _, w) in enumerate(chunks):
                    for k in range(KT):
                        pool.wait_ge(w_his, c * KT + k + 1)
                        nc.gpsimd.tensor_tensor(w_lo[:, c % 2, k, 0:w], w_raw[:, k, 0:w],
                                                w_hi[:, c % 2, k, 0:w].bitcast(F32), ALU.subtract).then_inc(w_los, 1)

            @block.vector
            def _(v):
                chain = Chain(v, own)

                def rotate(src, out, cos, sin, heads, half):
                    n = heads * 2 * half
                    s4 = src.rearrange("p (h a f) -> p h a f", h=heads, a=2)
                    c4 = t_cos[:, 0:n].rearrange("p (h a f) -> p h a f", h=heads, a=2)
                    n4 = t_sin[:, 0:n].rearrange("p (h a f) -> p h a f", h=heads, a=2)
                    o4 = out.rearrange("p (h a f) -> p h a f", h=heads, a=2)
                    cosb = bc(bc(cos, 1, 2), 1, heads)
                    sinb = bc(bc(sin, 1, 2), 1, heads)
                    nc.vector.tensor_tensor(c4, s4, cosb, ALU.mult)
                    chain.link(nc.vector.tensor_tensor(n4, s4, sinb, ALU.mult))
                    chain.link(nc.vector.tensor_tensor(o4[:, :, 0], c4[:, :, 0], n4[:, :, 1], ALU.subtract))
                    return nc.vector.tensor_tensor(o4[:, :, 1], c4[:, :, 1], n4[:, :, 0], ALU.add)

                for k in range(KT):
                    v.wait_ge(x_his, k + 1)
                    nc.vector.tensor_tensor(x_lo[:, k], x_raw[:, k], x_hi[:, k].bitcast(F32),
                                            ALU.subtract).then_inc(x_los, 1)
                v.wait_ge(rope_here, 32)
                for n, (c, tb) in enumerate(tiles):
                    if by_act[n]:
                        continue
                    kind = chunks[c][0]
                    v.wait_ge(tile_done, n + 1)
                    if n >= OUT:
                        v.wait_ge(stored[n % OUT], 16 * (n // OUT))
                    if finished(n)[1] > 1:
                        v.wait_ge(res_dve, finished(n)[1] - 1)
                    o = res[:, n % OUT]
                    if kind == "rot":
                        last = rotate(ps[n % NB][:], o, rope[:, tb, 0], rope[:, tb, 1], RH, RD // 2)
                    elif kind == "rot64":
                        last = rotate(ps[n % NB][:], o, rope64[:, tb, 0], rope64[:, tb, 1], QH, SD // 2)
                    else:
                        nc.vector.tensor_copy(o[:, SKV:2 * SKV], ps[n % NB][:, SKV:2 * SKV])
                        last = rotate(ps[n % NB][:, 0:SKV], o[:, 0:SKV], rope64[:, tb, 0], rope64[:, tb, 1],
                                      KVH, SD // 2)
                    last.then_inc(res_dve, 1)


class Ahead:

    GATES_AHEAD = T - P

    def __init__(self, nc, ctx):
        sb, _, sem = memory(nc, ctx)
        self.room = sb("room", [P, 2 * GROUP * T + 2 * D])
        self.taken = 0
        self.z_in = self.carve(GROUP, T)
        self.g_in = self.carve(T // GT, GROUP * GT)
        self.v_raw = [self.carve(D) for _ in range(2)]
        self.taken = 0
        self.wq_raw = [self.carve(KT, P) for _ in range(2)]
        self.wq_here = [sem(f"wq_here{p}") for p in range(2)]
        self.taken = 0
        self.z_here, self.v_here = sem("ahead_here"), [sem(f"v_here{e}") for e in range(2)]
        self.Z_LOADS = 4

    def carve(self, *shape):
        n = int(np.prod(shape))
        piece = self.room[:, self.taken:self.taken + n]
        self.taken += n
        names = "abc"[:len(shape)]
        return piece.rearrange(f"p ({' '.join(names)}) -> p {' '.join(names)}", **dict(zip(names, shape)))


def attend(nc, d, hT_hi, hT_lo, room):
    with ExitStack() as ctx:
        sb, bank, sem = memory(nc, ctx)
        ident = sb("ident", [P, P])
        decayT, xi = sb("decayT", [P, RH, P]), sb("xi", [P, RH, P])
        zeta = sb("zeta", [P, RH])
        masks = sb("masks", [P, 2, 2 * P])
        gn_w, sinks = sb("gn_w", [P, RW]), sb("sinks", [P, QH])
        ln_w, ln_b = sb("ln_w", [P, D]), sb("ln_b", [P, D])
        wo_hi, wo_lo = sb("wo_hi", [P, KT, D], F32R), sb("wo_lo", [P, KT, D], F32R)
        wo_stage = room.carve(D)
        minus_half = sb("minus_half", [P, RH])
        pj = room.carve(COLS)
        rqT, rqxT, rkT = sb("rqT", [P, RH, P]), sb("rqxT", [P, RH, P]), sb("rkT", [P, RH, P])
        sqT = sb("sqT", [P, QH // 2, P])
        skT = sb("skT", [P, 2, P])
        v_prev = room.carve(SKV)
        kz = sb("kz", [P, RH, P])
        retT = sb("retT", [P, RH, P])
        state = sb("state", [P, RH, P])
        stats, mv = room.carve(RH, 6), room.carve(RH, 2)
        gn_var, gn_rstd = sb("gn_var", [P, RH]), sb("gn_rstd", [P, RH])
        sm = room.carve(QH, 2 * P)
        mx, neg, sd = (room.carve(QH) for _ in range(3))
        sums, sink_e, den, rden = (room.carve(QH) for _ in range(4))
        pT = room.carve(QH, 2, P)
        ycat = room.carve(D)
        yT_hi, yT_lo = sb("yT_hi", [P, KT, P], F32R), sb("yT_lo", [P, KT, P], F32R)
        hr = room.carve(D)
        wo_raw = [wo_stage, hr, ln_w, ln_b]
        lstats, lmv = room.carve(2, 6), sb("lmv", [P, 2])
        l_var, l_rstd = sb("l_var", [P, 1]), sb("l_rstd", [P, 1])
        b = [bank(f"pa{i}") for i in range(8)]
        RQ, RK, SQ, SK = b[3], b[4], b[5], b[0]
        RS, Y, KV = b[4], b[5], b[4]
        PV, YT, MIX, HT = b[0], b[1:3], b[6:8], b[6:8]
        ident_here, const_here, norm_here = sem("ident_here"), sem("const_here"), sem("norm_here")
        wo_here = [sem(f"wo_here{j}") for j in range(4)]
        qk_here, v_here, x_here, h_out = sem("qk_here"), sem("v_here"), sem("x_here"), sem("h_out")
        wo_his, wo_los = sem("wo_his"), sem("wo_los")
        ready = sem("ready")
        qkT, q_evac_a, q_evac_v = sem("qkT"), sem("q_evac_a"), sem("q_evac_v")
        kz_in, rqx_in, gate_in = sem("kz_in"), sem("rqx_in"), sem("gate_in")
        ret_s, swa_s, ret_sT = sem("ret_s"), sem("swa_s"), sem("ret_sT")
        ret_y, ret_kv = sem("ret_y"), sem("ret_kv")
        negs, exps = sem("negs"), sem("exps")
        pTs, pT_in = sem("pTs"), sem("pT_in")
        pv, y_ready = sem("pv"), sem("y_ready")
        var_here, rstd_here = sem("var_here"), sem("rstd_here")
        yTs, yT_his, yT_los = sem("yTs"), sem("yT_his"), sem("yT_los")
        mixed = sem("mixed")
        lvar_here, lrstd_here = sem("lvar_here"), sem("lrstd_here")
        h_ready, hTs, hT_his, hT_los = sem("h_ready"), sem("hTs"), sem("hT_his"), sem("hT_los")
        kept = sem("kept")
        own, own_pool = sem("own_dve2"), sem("own_pool2")

        def parts(i):
            return not (isinstance(i, int) and i == TB), not (isinstance(i, int) and i == 0)

        with nc.Block() as block:

            @block.sync
            def _(sp):
                proj = d["proj"].rearrange("(n p) c -> n p c", p=P)
                x = d["x"].rearrange("(n p) c -> n p c", p=P)

                def load_qk(i):
                    for c in (slice(0, 2 * RW), slice(4 * RW, COLS - SKV)):
                        sp.dma_start(pj[:, c], proj[i][:, c]).then_inc(qk_here, 16)

                def load_v(i):
                    for c in (slice(2 * RW, 4 * RW), slice(COLS - SKV, COLS)):
                        sp.dma_start(pj[:, c], proj[i][:, c]).then_inc(v_here, 16)

                def load_wo(k):
                    sp.dma_start(wo_raw[k % 4][:], d["w_out"][:, k]).then_inc(wo_here[k % 4], 16)

                def turn(i):
                    front, back = parts(i)
                    more = front and not (isinstance(i, int) and i == TB - 1)
                    if more:
                        sp.wait_ge(ret_s, i + 1)
                        sp.wait_ge(kz_in, i + 1)
                        load_qk(i + 1)
                    if not back:
                        for k in range(4, KT):
                            sp.wait_ge(wo_los, k - 3)
                            load_wo(k)
                        sp.wait_ge(wo_los, KT)
                        sp.dma_start(ln_w[:], d["ln1_w"]).then_inc(norm_here, 16)
                        sp.dma_start(ln_b[:], d["ln1_b"]).then_inc(norm_here, 16)
                    if not front:
                        sp.wait_ge(kept, TB)
                        for p in range(2):
                            sp.dma_start(room.wq_raw[p], d["w_pq"][p]).then_inc(room.wq_here[p], 16)
                    if back:
                        sp.wait_ge(hTs, 2 * i)
                        sp.dma_start(d["h"][i - 1], hr[:]).then_inc(h_out, 16)
                    if front:
                        if back:
                            sp.wait_ge(h_out, 16 * i)
                        sp.dma_start(hr[:], x[i]).then_inc(x_here, 16)
                    if more:
                        sp.wait_ge(kept, i + 1)
                        load_v(i + 1)

                sp.dma_start(ident[:], d["ident"]).then_inc(ident_here, 16)
                load_qk(0)
                for t, n in ((zeta, "zeta"), (xi, "xi"), (decayT, "decayT"), (masks, "masks"), (sinks, "sinks")):
                    sp.dma_start(t[:], d[n]).then_inc(const_here, 16)
                load_v(0)
                sp.dma_start(gn_w[:], d["gn_w"]).then_inc(norm_here, 16)
                for k in range(4):
                    load_wo(k)
                turns(sp, TB + 1, turn, last=2)
                sp.wait_ge(h_out, 16 * TB)

            @block.tensor
            def _(pe):
                def project_out(i, a):
                    c = slice(a * 512, (a + 1) * 512)
                    for k in range(KT):
                        nc.tensor.matmul(MIX[a][:], yT_hi[:, k], wo_hi[:, k, c], start=(k == 0), stop=False)
                        nc.tensor.matmul(MIX[a][:], yT_hi[:, k], wo_lo[:, k, c], start=False, stop=False)
                        last = nc.tensor.matmul(MIX[a][:], yT_lo[:, k], wo_hi[:, k, c],
                                                start=False, stop=(k == KT - 1))
                    last.then_inc(mixed, 1)

                def turn(i):
                    front, back = parts(i)
                    if front:
                        pe.wait_ge(qk_here, 32 * i + 32)
                        for out, c0 in ((RQ, 0), (RK, RW), (SQ, 4 * RW)):
                            for h in range(RH):
                                last = nc.tensor.transpose(out[:, h * P:(h + 1) * P],
                                                           pj[:, c0 + h * P:c0 + (h + 1) * P], ident[:])
                            last.then_inc(qkT, 1)
                        nc.tensor.transpose(SK[:, 0:P], pj[:, 4 * RW + SW:4 * RW + SW + SKV], ident[:]).then_inc(qkT, 1)
                    if back:
                        pe.wait_ge(yT_los, 2 * i)
                        pe.wait_ge(wo_los, KT)
                        wait(pe, hT_los, 2 * (i - 1))
                        project_out(i, 0)
                    if front:
                        pe.wait_ge(q_evac_a, 2 * i + 1)
                        pe.wait_ge(q_evac_v, 2 * i + 1)
                        for h in range(RH):
                            last = nc.tensor.matmul(RS[:, h * P:(h + 1) * P], rkT[:, h], rqT[:, h],
                                                    start=True, stop=True)
                        last.then_inc(ret_s, 1)
                        pe.wait_ge(q_evac_a, 2 * i + 2)
                        pe.wait_ge(q_evac_v, 2 * i + 2)
                        for h in (0, 4, 1, 5, 2, 6, 3, 7):
                            lo = (h // G) * SD
                            last = nc.tensor.matmul(b[h // 2][:, (h % 2) * 256:(h % 2) * 256 + 256],
                                                    sqT[lo:lo + SD, h % G],
                                                    skT[lo:lo + SD].rearrange("p a k -> p (a k)"),
                                                    start=True, stop=True)
                            if h % 2:
                                last.then_inc(swa_s, 1)
                    if back:
                        project_out(i, 1)
                    if front:
                        pe.wait_ge(ret_sT, i + 1)
                        pe.wait_ge(rqx_in, i + 1)
                        pe.wait_ge(v_here, 32 * i + 32)
                        for h in range(RH):
                            vh = pj[:, 2 * RW + h * RD:2 * RW + (h + 1) * RD]
                            nc.tensor.matmul(Y[:, h * P:(h + 1) * P], retT[:, h], vh, start=True, stop=False)
                            last = nc.tensor.matmul(Y[:, h * P:(h + 1) * P], rqxT[:, h], state[:, h],
                                                    start=False, stop=True)
                        last.then_inc(ret_y, 1)
                        pe.wait_ge(kz_in, i + 1)
                        for h in range(RH):
                            vh = pj[:, 2 * RW + h * RD:2 * RW + (h + 1) * RD]
                            last = nc.tensor.matmul(KV[:, h * P:(h + 1) * P], kz[:, h], vh, start=True, stop=True)
                        last.then_inc(ret_kv, 1)
                        pe.wait_ge(exps, i + 1)
                        for h in range(QH):
                            for a in range(2):
                                n = 2 * h + a
                                last = nc.tensor.transpose(b[n // 4][:, (n % 4) * P:(n % 4 + 1) * P],
                                                           sm[:, h, a * P:(a + 1) * P], ident[:])
                            if h % 2:
                                last.then_inc(pTs, 1)
                        for h in range(QH):
                            if h % 2 == 0:
                                pe.wait_ge(pT_in, 4 * i + h // 2 + 1)
                            g = h // G
                            nc.tensor.matmul(PV[:, h * SD:(h + 1) * SD], pT[:, h, 0], v_prev[:, g * SD:(g + 1) * SD],
                                             start=True, stop=False)
                            last = nc.tensor.matmul(PV[:, h * SD:(h + 1) * SD], pT[:, h, 1],
                                                    pj[:, COLS - SKV + g * SD:COLS - SKV + (g + 1) * SD],
                                                    start=False, stop=True)
                        last.then_inc(pv, 1)
                    if back:
                        pe.wait_ge(h_ready, i)
                        for k in range(KT):
                            last = nc.tensor.transpose(HT[k // 4][:, (k % 4) * P:(k % 4 + 1) * P],
                                                       hr[:, k * P:(k + 1) * P], ident[:])
                            if k % 4 == 3:
                                last.then_inc(hTs, 1)
                    if front:
                        pe.wait_ge(y_ready, i + 1)
                        for k in range(KT):
                            last = nc.tensor.transpose(YT[k // 4][:, (k % 4) * P:(k % 4 + 1) * P],
                                                       ycat[:, k * P:(k + 1) * P], ident[:])
                            if k % 4 == 3:
                                last.then_inc(yTs, 1)

                pe.wait_ge(ident_here, 16)
                pe.wait_ge(ready, 1)
                turns(pe, TB + 1, turn)

            @block.scalar
            def _(act):
                def split_wo(ks):
                    for k in ks:
                        act.wait_ge(wo_here[k % 4], 16 * (k // 4 + 1))
                        nc.scalar.activation(wo_hi[:, k], wo_raw[k % 4][:], ACT.Copy).then_inc(wo_his, 1)

                def turn(i):
                    front, back = parts(i)
                    if front:
                        act.wait_ge(qkT, 4 * i + 1)
                        nc.scalar.activation(rqT[:].rearrange("p h t -> p (h t)"), RQ[:], ACT.Copy).then_inc(q_evac_a, 1)
                        act.wait_ge(qkT, 4 * i + 3)
                        nc.scalar.activation(sqT[:].rearrange("p h t -> p (h t)"), SQ[:], ACT.Copy).then_inc(q_evac_a, 1)
                        if not back:
                            split_wo(range(4))
                        act.wait_ge(negs, i + 1)
                        for h in range(QH):
                            nc.scalar.activation(sm[:, h], sm[:, h], ACT.Exp, bias=neg[:, h:h + 1],
                                                 accum_out=sums[:, h:h + 1])
                        nc.scalar.activation(sink_e[:], sd[:], ACT.Exp).then_inc(exps, 1)
                        for n in range(4):
                            act.wait_ge(pTs, 4 * i + n + 1)
                            nc.scalar.activation(pT[:, n * 2:n * 2 + 2].rearrange("p h a q -> p (h a q)"), b[n][:],
                                                 ACT.Copy).then_inc(pT_in, 1)
                        if not back:
                            split_wo(range(4, KT))
                    if back:
                        for n in range(2):
                            act.wait_ge(hTs, 2 * i - 1 + n)
                            nc.scalar.activation(hT_hi[:, 4 * n:4 * n + 4, bass.ds((i - 1) * P, P)],
                                                 HT[n][:].rearrange("p (k t) -> p k t", k=4), ACT.Copy).then_inc(hT_his, 1)
                    if front:
                        for n in range(2):
                            act.wait_ge(yTs, 2 * i + n + 1)
                            nc.scalar.activation(yT_hi[:, 4 * n:4 * n + 4].rearrange("p k t -> p (k t)"), YT[n][:],
                                                 ACT.Copy).then_inc(yT_his, 1)

                turns(act, TB + 1, turn)

            @block.gpsimd
            def _(pool):
                def split_wo(ks):
                    for k in ks:
                        pool.wait_ge(wo_his, k + 1)
                        nc.gpsimd.tensor_tensor(wo_lo[:, k], wo_raw[k % 4][:], wo_hi[:, k].bitcast(F32),
                                                ALU.subtract).then_inc(wo_los, 1)

                def turn(i):
                    front, back = parts(i)
                    if front:
                        pool.wait_ge(qk_here, 32 * i + 32)
                        wait(pool, ret_kv, i)
                        nc.gpsimd.tensor_tensor(kz[:], pj[:, RW:2 * RW].rearrange("p (h c) -> p h c", h=RH),
                                                bc(zeta[:], 2, P), ALU.mult).then_inc(kz_in, 1)
                        pool.wait_ge(q_evac_a, 2 * i + 1)
                        nc.gpsimd.tensor_tensor(rqxT[:], rqT[:], xi[:], ALU.mult).then_inc(rqx_in, 1)
                        if not back:
                            pool.wait_ge(norm_here, 16)
                        pool.wait_ge(v_here, 32 * i + 32)
                        nc.gpsimd.tensor_tensor(pj[:, 3 * RW:4 * RW], pj[:, 3 * RW:4 * RW], gn_w[:],
                                                ALU.mult).then_inc(gate_in, 1)
                        if not back:
                            split_wo(range(4))
                    if back:
                        pool.wait_ge(lvar_here, i)
                        nc.gpsimd.tensor_tensor(l_rstd[:], l_var[:], minus_half[:, 0:1], ALU.pow).then_inc(lrstd_here, 1)
                    if front:
                        pool.wait_ge(var_here, i + 1)
                        nc.gpsimd.tensor_tensor(gn_rstd[:], gn_var[:], minus_half[:], ALU.pow).then_inc(rstd_here, 1)
                        if not back:
                            split_wo(range(4, KT))
                            pool.wait_ge(norm_here, 48)

                nc.gpsimd.memset(minus_half[:], -0.5).then_inc(own_pool, 1)
                pool.wait_ge(own_pool, 1)
                pool.wait_ge(const_here, 16 * 5)
                turns(pool, TB + 1, turn)

            @block.vector
            def _(v):
                chain = Chain(v, own)
                link = chain.link

                def turn(i):
                    front, back = parts(i)
                    if front:
                        wait(v, kept, i)
                        v.wait_ge(qkT, 4 * i + 2)
                        nc.vector.tensor_copy(rkT[:].rearrange("p h t -> p (h t)"), RK[:]).then_inc(q_evac_v, 1)
                        v.wait_ge(qkT, 4 * i + 4)
                        nc.vector.tensor_copy(skT[:, 1], SK[:, 0:P]).then_inc(q_evac_v, 1)
                        v.wait_ge(ret_s, i + 1)
                        nc.vector.tensor_tensor(retT[:], RS[:].rearrange("p (h t) -> p h t", h=RH), decayT[:],
                                                ALU.mult).then_inc(ret_sT, 1)
                        for done, n in enumerate((0, 2, 1, 3)):
                            v.wait_ge(swa_s, 4 * i + done + 1)
                            ins = nc.vector.scalar_tensor_tensor(
                                sm[:, 2 * n:2 * n + 2], b[n][:].rearrange("p (a k) -> p a k", a=2), SD ** -0.5,
                                bc(masks[:, 0], 1, 2), ALU.mult, ALU.add)
                        link(ins)
                        link(nc.vector.tensor_reduce(mx[:], sm[:], AX.X, ALU.max))
                        link(nc.vector.tensor_tensor(mx[:], mx[:], sinks[:], ALU.max))
                        nc.vector.tensor_tensor(sd[:], sinks[:], mx[:], ALU.subtract)
                        nc.vector.tensor_scalar(neg[:], mx[:], -1.0, None, ALU.mult).then_inc(negs, 1)
                    if back:
                        v.wait_ge(x_here, 16 * i)
                        for a in range(2):
                            c = slice(a * 512, (a + 1) * 512)
                            v.wait_ge(mixed, 2 * i - 1 + a)
                            link(nc.vector.scalar_tensor_tensor(hr[:, c], hr[:, c], ALPHA, MIX[a][:], ALU.mult, ALU.add))
                            link(nc.vector.bn_stats(lstats[:, a], hr[:, c]))
                        link(nc.vector.bn_aggr(lmv[:], lstats[:]))
                        nc.vector.tensor_scalar(l_var[:], lmv[:, 1:2], LN_EPS, None, ALU.add).then_inc(lvar_here, 1)
                    if front:
                        v.wait_ge(ret_y, i + 1)
                        for h in range(RH):
                            ins = nc.vector.bn_stats(stats[:, h], Y[:, h * P:(h + 1) * P])
                        link(ins)
                        for h in range(RH):
                            ins = nc.vector.bn_aggr(mv[:, h], stats[:, h])
                        link(ins)
                        nc.vector.tensor_scalar(gn_var[:], mv[:, :, 1], GN_EPS, None, ALU.add).then_inc(var_here, 1)
                        v.wait_ge(ret_kv, i + 1)
                        for h in range(RH):
                            g = float((1.0 - 2.0 ** (-5.0 - h)) ** P)
                            ins = nc.vector.scalar_tensor_tensor(state[:, h], state[:, h], g,
                                                                 KV[:, h * P:(h + 1) * P], ALU.mult, ALU.add)
                        link(ins)
                    if back:
                        link(nc.vector.scalar_tensor_tensor(hr[:], hr[:], lmv[:, 0:1], ln_w[:], ALU.subtract, ALU.mult))
                        v.wait_ge(lrstd_here, i)
                        nc.vector.scalar_tensor_tensor(hr[:], hr[:], l_rstd[:], ln_b[:], ALU.mult,
                                                       ALU.add).then_inc(h_ready, 1)
                    if front:
                        v.wait_ge(rstd_here, i + 1)
                        for h in range(RH):
                            ins = nc.vector.tensor_scalar(ycat[:, h * P:(h + 1) * P], Y[:, h * P:(h + 1) * P],
                                                          mv[:, h, 0:1], gn_rstd[:, h:h + 1], ALU.subtract, ALU.mult)
                        link(ins)
                        v.wait_ge(gate_in, i + 1)
                        nc.vector.tensor_tensor(ycat[:, 0:RW], ycat[:, 0:RW], pj[:, 3 * RW:4 * RW], ALU.mult)
                        v.wait_ge(exps, i + 1)
                        link(nc.vector.tensor_tensor(den[:], sums[:], sink_e[:], ALU.add))
                        link(nc.vector.reciprocal(rden[:], den[:]))
                        v.wait_ge(pv, i + 1)
                        nc.vector.tensor_tensor(ycat[:, RW:D].rearrange("p (h c) -> p h c", h=QH),
                                                PV[:].rearrange("p (h c) -> p h c", h=QH),
                                                bc(rden[:], 2, SD), ALU.mult).then_inc(y_ready, 1)
                        nc.vector.tensor_copy(v_prev[:], pj[:, COLS - SKV:COLS])
                        if not back:
                            nc.vector.tensor_copy(masks[:, 0], masks[:, 1])
                        nc.vector.tensor_copy(skT[:, 0], skT[:, 1]).then_inc(kept, 1)
                    if back:
                        for n in range(2):
                            v.wait_ge(hT_his, 2 * i - 1 + n)
                            c = bass.ds((i - 1) * P, P)
                            nc.vector.tensor_tensor(hT_lo[:, 4 * n:4 * n + 4, c], HT[n][:].rearrange("p (k t) -> p k t", k=4),
                                                    hT_hi[:, 4 * n:4 * n + 4, c].bitcast(F32),
                                                    ALU.subtract).then_inc(hT_los, 1)
                    if front:
                        for n in range(2):
                            v.wait_ge(yT_his, 2 * i + n + 1)
                            nc.vector.tensor_tensor(yT_lo[:, 4 * n:4 * n + 4].rearrange("p k t -> p (k t)"), YT[n][:],
                                                    yT_hi[:, 4 * n:4 * n + 4].rearrange("p k t -> p (k t)").bitcast(F32),
                                                    ALU.subtract).then_inc(yT_los, 1)
                    if not back:
                        v.wait_ge(norm_here, 48)
                    chain.restart()

                nc.vector.memset(state[:], 0.0)
                nc.vector.memset(v_prev[:], 0.0)
                nc.vector.memset(skT[:], 0.0).then_inc(ready, 1)
                v.wait_ge(ready, 1)
                v.wait_ge(const_here, 16 * 5)
                turns(v, TB + 1, turn)


class TopK:

    def __init__(self, nc, ctx):
        sb = memory(nc, ctx)[0]
        self.nc = nc
        self.places = sb("places", [P, TOPK])
        self.s_cp, self.s_left = sb("s_cp", [P, 2, NK]), sb("s_left", [P, 2, NK])
        self.top, self.top_f = sb("top", [P, 2, TOPK]), sb("top_f", [P, 2, TOPK])
        self.top_i = sb("top_i", [P, 2, TOPK], U32)
        self.cand, self.cand_left = sb("cand", [P, TOPK, TOPK]), sb("cand_left", [P, TOPK * TOPK])
        self.best, self.pos = sb("best", [P, TOPK]), sb("pos", [P, TOPK], U32)
        self.ab, self.ab_f = sb("ab", [P, 2, TOPK], U32), sb("ab_f", [P, 2, TOPK])
        self.pick = sb("pick", [P, 2, TOPK, TOPK])
        self.gap, self.gap_e = sb("gap", [P, TOPK]), sb("gap_e", [P, TOPK])
        self.gap_sum, self.gap_r = sb("gap_sum", [P, 1]), sb("gap_r", [P, 1])
        self.found = sb("found", [P, 3, PH, TOPK])

    def top16(self, link, values, left, out, index):
        nc = self.nc
        link(nc.vector.max(out[:, 0:8], values))
        nc.vector.max_index(index[:, 0:8], out[:, 0:8], values)
        link(nc.vector.match_replace(left, out[:, 0:8], values, LOWEST))
        link(nc.vector.max(out[:, 8:16], left))
        link(nc.vector.max_index(index[:, 8:16], out[:, 8:16], left))

    def side(self, link, p):
        self.top16(link, self.s_cp[:, p], self.s_left[:, p], self.top[:, p], self.top_i[:, p])

    def pairs(self, link):
        nc = self.nc
        link(nc.vector.tensor_tensor(self.cand[:], bc(self.top[:, 0], 2, TOPK), bc(self.top[:, 1], 1, TOPK), ALU.add))
        self.top16(link, self.cand[:].rearrange("p a b -> p (a b)"), self.cand_left[:], self.best, self.pos)

    def gaps(self):
        return self.nc.vector.tensor_scalar(self.gap[:], self.best[:], self.best[:, 0:1], None, ALU.subtract)

    def names(self, link, h):
        nc = self.nc
        nc.vector.tensor_copy(self.top_f[:], self.top_i[:])
        nc.vector.tensor_scalar(self.ab[:, 0], self.pos[:], 4, None, ALU.logical_shift_right)
        link(nc.vector.tensor_scalar(self.ab[:, 1], self.pos[:], 15, None, ALU.bitwise_and))
        link(nc.vector.tensor_copy(self.ab_f[:], self.ab[:]))
        link(nc.vector.tensor_tensor(self.pick[:], bc(self.ab_f[:], 3, TOPK),
                                     bc(bc(self.places[:], 1, TOPK), 1, 2), ALU.is_equal))
        link(nc.vector.tensor_tensor(self.pick[:], self.pick[:], bc(self.top_f[:], 2, TOPK), ALU.mult))
        link(nc.vector.tensor_reduce(self.found[:, 0:2, bass.ds(h, 1), :].rearrange("p a h k -> p a (h k)"),
                                     self.pick[:], AX.X, ALU.add))

    def exp(self):
        return self.nc.scalar.activation(self.gap_e[:], self.gap[:], ACT.Exp, accum_out=self.gap_sum[:])

    def gates(self, link, h):
        nc = self.nc
        link(nc.vector.reciprocal(self.gap_r[:], self.gap_sum[:]))
        link(nc.vector.tensor_scalar(self.found[:, 2, bass.ds(h, 1), :].rearrange("p h k -> p (h k)"),
                                     self.gap_e[:], self.gap_r[:], None, ALU.mult))


class ExpertTiles:

    def __init__(self, nc, ctx):
        sb, _, sem = memory(nc, ctx)
        self.ident, self.iota = sb("ident4", [P, P]), sb("iota", [P, P])
        self.u_raw = [sb(f"u_raw{e}", [P, KT, P]) for e in range(2)]
        self.u_hi = [sb(f"u_hi{e}", [P, KT, P], F32R) for e in range(2)]
        self.u_lo = [sb(f"u_lo{e}", [P, KT, P], F32R) for e in range(2)]
        self.const_here = sem("const4")
        self.u_here = [sem(f"u_here{e}") for e in range(2)]
        self.u_hi_in = [sem(f"u_hi_in{e}") for e in range(2)]
        self.u_lo_in = [sem(f"u_lo_in{e}") for e in range(2)]
        self.nc = nc

    def hi(self, e):
        self.nc.scalar.activation(self.u_hi[e][:], self.u_raw[e][:], ACT.Copy).then_inc(self.u_hi_in[e], 1)

    def lo(self, e):
        self.nc.gpsimd.tensor_tensor(self.u_lo[e][:], self.u_raw[e][:], self.u_hi[e][:].bitcast(F32),
                                     ALU.subtract).then_inc(self.u_lo_in[e], 1)


def score(nc, d, hT_hi, hT_lo, tk, tiles, ahead):
    HT = T // 2
    with ExitStack() as ctx:
        sb, bank, sem = memory(nc, ctx)
        keysT = sb("keysT", [P, PAIRS, NK])
        w_raw = ahead.wq_raw
        w_hi = [sb(f"wq_hi{p}", [P, KT, P], F32R) for p in range(2)]
        w_lo = [sb(f"wq_lo{p}", [P, KT, P], F32R) for p in range(2)]
        qT = [sb(f"qT{p}", [P, T]) for p in range(2)]
        s_out = sb("s_out", [P, TB, 2, NK])
        q_ps = [[bank(f"q_ps{p}{a}") for a in range(2)] for p in range(2)]
        s_ps = [[bank(f"s_ps{p}{a}") for a in range(2)] for p in range(2)]
        keys_here, places_here = sem("keys_here"), sem("places_here")
        w_here = ahead.wq_here
        w_his, w_los = sem("wq_his"), sem("wq_los")
        q_done, q_act, q_dve = sem("q_done"), sem("q_act"), sem("q_dve")
        s_done, s_act, s_dve = sem("s_done"), sem("s_act"), sem("s_dve")
        s_taken, s_stored = sem("s_taken3"), sem("s_stored")
        gaps, exps = sem("gaps3"), sem("exps3")
        own = sem("own_dve3")

        with nc.Block() as block:

            @block.sync
            def _(sp):
                def load(h):
                    for p in range(2):
                        wait(sp, w_los, 2 * h - 1 + p)
                        sp.dma_start(w_raw[p], d["w_pq"][2 * h + p]).then_inc(w_here[p], 16)

                sp.dma_start(keysT[:], d["keysT"]).then_inc(keys_here, 16)
                sp.dma_start(tk.places[:], d["iota"][:, 0:TOPK]).then_inc(places_here, 16)
                with sp.Fori(1, PH) as h:
                    load(h)
                sp.dma_start(tiles.ident[:], d["ident"]).then_inc(tiles.const_here, 16)
                sp.dma_start(tiles.iota[:], d["iota"]).then_inc(tiles.const_here, 16)
                for e in range(2):
                    sp.dma_start(tiles.u_raw[e][:], d["uT"][e]).then_inc(tiles.u_here[e], 16)

            @block.tensor
            def _(pe):
                def query(h, p, a):
                    if a == 0:
                        pe.wait_ge(w_los, 2 * h + p + 1)
                    c = slice(a * HT, (a + 1) * HT)
                    for k in range(KT):
                        nc.tensor.matmul(q_ps[p][a][:], w_hi[p][:, k], hT_hi[:, k, c], start=(k == 0), stop=False)
                        nc.tensor.matmul(q_ps[p][a][:], w_hi[p][:, k], hT_lo[:, k, c], start=False, stop=False)
                        last = nc.tensor.matmul(q_ps[p][a][:], w_lo[p][:, k], hT_hi[:, k, c],
                                                start=False, stop=(k == KT - 1))
                    last.then_inc(q_done, 1)

                def scores(h, p):
                    for a in range(2):
                        pe.wait_ge((q_act, q_dve)[a], 2 * h + p + 1)
                        wait(pe, (s_act, s_dve)[a], 2 * h)
                        for n in range(4):
                            tb = 4 * a + n
                            last = nc.tensor.matmul(s_ps[p][a][:, n * P:(n + 1) * P], qT[p][:, tb * P:(tb + 1) * P],
                                                    keysT[:, bass.ds(2 * h + p, 1), :].rearrange("p a k -> p (a k)"),
                                                    start=True, stop=True)
                        last.then_inc(s_done, 1)

                def turn(h):
                    query(h, 0, 0)
                    query(h, 0, 1)
                    query(h, 1, 0)
                    if isinstance(h, int) and h == 0:
                        pe.wait_ge(keys_here, 16)
                    scores(h, 0)
                    query(h, 1, 1)
                    scores(h, 1)

                turns(pe, PH, turn)

            @block.scalar
            def _(act):
                def split_w(h, p):
                    act.wait_ge(w_here[p], 16 * h + 16)
                    wait(act, q_done, 4 * h - 2 + 2 * p)
                    nc.scalar.activation(w_hi[p][:], w_raw[p], ACT.Copy).then_inc(w_his, 1)

                def query(h, p):
                    act.wait_ge(q_done, 4 * h + 2 * p + 1)
                    nc.scalar.activation(qT[p][:, 0:HT], q_ps[p][0][:], ACT.Copy).then_inc(q_act, 1)

                def scores(h, p):
                    act.wait_ge(s_done, 4 * h + 2 * p + 1)
                    wait(act, s_stored, 16 * h)
                    wait(act, s_taken, h)
                    nc.scalar.activation(s_out[:, 0:4, p], s_ps[p][0][:].rearrange("p (t k) -> p t k", k=NK),
                                         ACT.Copy).then_inc(s_act, 1)

                def turn(h):
                    last = isinstance(h, int) and h == PH - 1
                    query(h, 0)
                    if not (isinstance(h, int) and h == 0):
                        act.wait_ge(gaps, h)
                        tk.exp().then_inc(exps, 1)
                    if not last:
                        split_w(h + 1, 0)
                    query(h, 1)
                    scores(h, 0)
                    if not last:
                        split_w(h + 1, 1)
                    scores(h, 1)
                    act.wait_ge(s_act, 2 * h + 2)
                    act.wait_ge(s_dve, 2 * h + 2)
                    act.dma_start(d["scores"].rearrange("n h p k -> h p n k")[h][:, 1:TB],
                                  s_out[:, 1:TB].rearrange("p t a k -> p t (a k)")).then_inc(s_stored, 16)

                for p in range(2):
                    split_w(0, p)
                turns(act, PH, turn)
                act.wait_ge(tiles.u_here[0], 16)
                tiles.hi(0)
                act.wait_ge(gaps, PH)
                tk.exp().then_inc(exps, 1)
                act.wait_ge(s_stored, 16 * PH)

            @block.gpsimd
            def _(pool):
                pool.wait_ge(tiles.u_hi_in[0], 1)
                tiles.lo(0)

            @block.vector
            def _(v):
                chain = Chain(v, own)
                link = chain.link

                def split_w(h, p):
                    v.wait_ge(w_his, 2 * h + p + 1)
                    nc.vector.tensor_tensor(w_lo[p][:], w_raw[p], w_hi[p][:].bitcast(F32),
                                            ALU.subtract).then_inc(w_los, 1)

                def query(h, p):
                    v.wait_ge(q_done, 4 * h + 2 * p + 2)
                    nc.vector.tensor_copy(qT[p][:, HT:T], q_ps[p][1][:]).then_inc(q_dve, 1)

                def scores(h, p):
                    v.wait_ge(s_done, 4 * h + 2 * p + 2)
                    wait(v, s_stored, 16 * h)
                    nc.vector.tensor_copy(s_out[:, 4:8, p],
                                          s_ps[p][1][:].rearrange("p (t k) -> p t k", k=NK)).then_inc(s_dve, 1)

                def finish_top(h):
                    tk.names(link, h)
                    v.wait_ge(exps, h + 1)
                    tk.gates(link, h)

                def turn(h):
                    last = isinstance(h, int) and h == PH - 1
                    query(h, 0)
                    if not last:
                        split_w(h + 1, 0)
                    if not (isinstance(h, int) and h == 0):
                        finish_top(h - 1)
                    scores(h, 0)
                    query(h, 1)
                    if not last:
                        split_w(h + 1, 1)
                    scores(h, 1)
                    v.wait_ge(s_act, 2 * h + 2)
                    link(nc.vector.tensor_scalar(tk.s_cp[:], s_out[:, 0], 1.0, None, ALU.mult))
                    nc.vector.engine_nop().then_inc(s_taken, 1)
                    tk.side(link, 0)
                    tk.side(link, 1)
                    tk.pairs(link)
                    tk.gaps().then_inc(gaps, 1)
                    chain.restart()

                for p in range(2):
                    split_w(0, p)
                v.wait_ge(places_here, 16)
                turns(v, PH, turn)
                finish_top(PH - 1)


def experts_in(nc, d, hT_hi, hT_lo, tk, tiles, ahead):
    HT = T // 2
    Q = PH // 2
    with ExitStack() as ctx:
        sb, bank, sem = memory(nc, ctx)
        ident, iota = tiles.ident, tiles.iota
        u_raw, u_hi, u_lo = tiles.u_raw, tiles.u_hi, tiles.u_lo
        z_sb = [sb(f"z_sb{e}", [P, T]) for e in range(2)]
        s_in = [sb(f"s_in{j}", [P, 2, NK]) for j in range(2)]
        iT = sb("iT", [P, 2, P])
        gT_hi, gT_lo = sb("gT_hi", [P, P], F32R), sb("gT_lo", [P, P])
        cur = [sb(f"cur{b}", [P, 4, GT]) for b in range(2)]
        hot2 = [sb(f"hot2_{g}", [P, 4, NK], F32R) for g in range(2)]
        hot1 = [sb(f"hot1_{g}", [P, 4, NK]) for g in range(2)]
        hot1_g = [sb(f"hot1_g{g}", [P, 4, 2, NK], F32R) for g in range(2)]
        g_lo = [sb(f"g_lo{g}", [P, 4, NK]) for g in range(2)]
        g_sb = [sb(f"g_sb{b}", [P, NK, GT]) for b in range(2)]
        z_ps = [[bank(f"z_ps{e}{a}") for a in range(2)] for e in range(2)]
        g_ps = [ctx.enter_context(nc.psum_tensor(f"g_ps{g}", [P, 4, 2, NK], F32)) for g in range(2)]
        const_here, u_here, u_hi_in, u_lo_in = tiles.const_here, tiles.u_here, tiles.u_hi_in, tiles.u_lo_in
        z_done = [sem(f"z_done{e}") for e in range(2)]
        z_read = [sem(f"z_read{e}") for e in range(2)]
        z_stored = [sem(f"z_stored{e}") for e in range(2)]
        s_here = [sem(f"s_here{j}") for j in range(2)]
        s_taken = [sem(f"s_taken{j}") for j in range(2)]
        gaps, exps = sem("gaps"), sem("exps4")
        found_in, found_T = sem("found_in"), sem("found_T")
        hot_in = [sem(f"hot_in{g}") for g in range(2)]
        hot_g_in = [sem(f"hot_g_in{g}") for g in range(2)]
        g_done = [sem(f"g_done{g}") for g in range(2)]
        g_lo_in = [sem(f"g_lo_in{g}") for g in range(2)]
        g_read = [sem(f"g_read{g}") for g in range(2)]
        g_stored = [sem(f"g_stored{b}") for b in range(2)]
        own = sem("own_dve4")

        def is_(n, value):
            return isinstance(n, int) and n == value

        with nc.Block() as block:

            @block.sync
            def _(sp):
                scores = d["scores"].rearrange("n h p k -> (n h) p k")

                def load(m, heads):
                    for j in range(2):
                        if heads:
                            wait(sp, s_taken[j], m)
                            sp.dma_start(s_in[j][:], scores[2 * m + j + PH].rearrange(
                                "p (a k) -> p a k", a=2)).then_inc(s_here[j], 16)
                        for e in range(2):
                            if is_(2 * m + j, 0):
                                continue
                            sp.wait_ge(u_lo_in[e], 2 * m + j)
                            sp.dma_start(u_raw[e][:], d["uT"][4 * m + 2 * j + e]).then_inc(u_here[e], 16)

                load(0, True)
                with sp.Fori(1, Q * (TB - 1)) as m:
                    load(m, True)
                for m in range(Q * (TB - 1), Q * TB):
                    load(m, False)
                    n = m % Q
                    if n < 2:
                        for e in range(2):
                            sp.wait_ge(z_stored[e], 16 * 2)
                        sp.dma_start(ahead.z_in[:, 2 * n:2 * n + 2],
                                     d["z"].rearrange("n e t -> e n t")[:, 2 * n:2 * n + 2]).then_inc(ahead.z_here, 16)
                        sp.dma_start(ahead.v_raw[n][:], d["v"][n]).then_inc(ahead.v_here[n], 16)
                    else:
                        for b in range(2):
                            sp.wait_ge(g_stored[b], 16 * Q * (TB - 1) // 2)
                        half = ahead.GATES_AHEAD // GT // 2
                        c = slice((n - 2) * half, (n - 1) * half)
                        sp.dma_start(ahead.g_in[:, c], d["gates"].rearrange("c e i t -> e c (i t)")[:, c, 0:GROUP * GT]
                                     ).then_inc(ahead.z_here, 16)

            @block.tensor
            def _(pe):
                pe.wait_ge(const_here, 32)

                def z_half(m, n):
                    j, e, a = n // 4, n // 2 % 2, n % 2
                    if a == 0:
                        pe.wait_ge(u_lo_in[e], 2 * m + j + 1)
                        wait(pe, z_read[e], 2 * (2 * m + j))
                    cols = slice(a * HT, (a + 1) * HT)
                    for k in range(KT):
                        nc.tensor.matmul(z_ps[e][a][:], u_hi[e][:, k], hT_hi[:, k, cols], start=(k == 0), stop=False)
                        nc.tensor.matmul(z_ps[e][a][:], u_hi[e][:, k], hT_lo[:, k, cols], start=False, stop=False)
                        last = nc.tensor.matmul(z_ps[e][a][:], u_lo[e][:, k], hT_hi[:, k, cols],
                                                start=False, stop=(k == KT - 1))
                    last.then_inc(z_done[e], 1)

                def gates(m, n):
                    g = n % 2
                    pe.wait_ge(hot_g_in[g], 4 * m + n // 2 + 1)
                    wait(pe, g_read[g], 4 * m + n // 2)
                    for t in range(4):
                        last = nc.tensor.matmul(g_ps[g][:, t].rearrange("p w i -> p (w i)"), hot2[g][:, t],
                                                hot1_g[g][:, t].rearrange("p w i -> p (w i)"), start=True, stop=True)
                    last.then_inc(g_done[g], 1)

                def turn(tb):
                    for q in range(Q):
                        m = tb * Q + q
                        z_half(m, 0)
                        if q == 0:
                            wait(pe, found_in, tb)
                            wait(pe, g_read[0], 4 * m)
                            for n in range(3):
                                last = nc.tensor.transpose(g_ps[0][:, n, 0], tk.found[:, n].rearrange("p h k -> p (h k)"),
                                                           ident[:])
                            last.then_inc(found_T, 1)
                        for n in range(1, 8):
                            z_half(m, n)
                            gates(m, n - 1)
                        gates(m, 7)

                turns(pe, TB, turn)

            @block.scalar
            def _(act):
                def split_u(m, i):
                    e, j = i % 2, i // 2
                    act.wait_ge(u_here[e], 16 * (2 * m + j + 1))
                    wait(act, z_done[e], 2 * (2 * m + j))
                    tiles.hi(e)

                def store_gates(m, b):
                    act.wait_ge(g_read[0], 4 * m + 4)
                    act.wait_ge(g_read[1], 4 * m + 4)
                    act.dma_start(d["gates"][m], g_sb[b][:]).then_inc(g_stored[b], 16)

                def take_gates_lo(m, n):
                    g = n % 2
                    act.wait_ge(g_done[g], 4 * m + n // 2 + 1)
                    nc.scalar.activation(g_lo[g][:], g_ps[g][:, :, 1], ACT.Copy).then_inc(g_lo_in[g], 1)

                def turn(tb):
                    heads = not is_(tb, TB - 1)
                    for q in range(Q):
                        m = tb * Q + q
                        for n in range(8):
                            j, e, a = n // 4, n // 2 % 2, n % 2
                            if a == 0 and not is_(4 * m + n // 2, NK - 1):
                                split_u(m, n // 2 + 1)
                            if heads and n % 4 == 3:
                                act.wait_ge(gaps, 2 * m + j + 1)
                                tk.exp().then_inc(exps, 1)
                            act.wait_ge(z_done[e], 2 * (2 * m + j) + a + 1)
                            if a == 0:
                                wait(act, z_stored[e], 16 * (2 * m + j))
                            nc.scalar.activation(z_sb[e][:, a * HT:(a + 1) * HT], z_ps[e][a][:],
                                                 ACT.Copy).then_inc(z_read[e], 1)
                            if a == 1:
                                act.wait_ge(z_read[e], 2 * (2 * m + j) + 2)
                                act.dma_start(d["z"][4 * m + 2 * j + e], z_sb[e][:]).then_inc(z_stored[e], 16)
                            if n:
                                take_gates_lo(m, n - 1)
                            if n == 1 and not is_(m, 0):
                                store_gates(m - 1, (q + 1) % 2)
                        take_gates_lo(m, 7)

                turns(act, TB, turn)
                store_gates(Q * TB - 1, 1)
                for e in range(2):
                    act.wait_ge(z_stored[e], 16 * NK // 2)
                    act.wait_ge(g_stored[e], 16 * Q * TB // 2)

            @block.gpsimd
            def _(pool):
                def split_u(m, i):
                    e, j = i % 2, i // 2
                    pool.wait_ge(u_hi_in[e], 2 * m + j + 1)
                    tiles.lo(e)

                def turn(tb):
                    for q in range(Q):
                        m = tb * Q + q
                        for n in range(8):
                            if n % 2 == 0 and not is_(4 * m + n // 2, NK - 1):
                                split_u(m, n // 2 + 1)
                            g = n % 2
                            pool.wait_ge(hot_in[g], 4 * m + n // 2 + 1)
                            for w in range(2):
                                last = nc.gpsimd.tensor_tensor(hot1_g[g][:, :, w], hot1[g][:],
                                                               bc(cur[q % 2][:, 2 + w, 4 * n:4 * n + 4], 2, NK), ALU.mult)
                            last.then_inc(hot_g_in[g], 1)

                turns(pool, TB, turn)

            @block.vector
            def _(v):
                chain = Chain(v, own)
                link = chain.link
                v.wait_ge(const_here, 32)

                def top_piece(piece, m, j, h):
                    if piece == 0:
                        v.wait_ge(s_here[j], 16 * (m + 1))
                        link(nc.vector.tensor_copy(tk.s_cp[:], s_in[j][:]))
                        nc.vector.engine_nop().then_inc(s_taken[j], 1)
                        tk.side(link, 0)
                    elif piece == 1:
                        tk.side(link, 1)
                    elif piece == 2:
                        tk.pairs(link)
                        tk.gaps().then_inc(gaps, 1)
                    else:
                        tk.names(link, h)
                        v.wait_ge(exps, 2 * m + j + 1)
                        tk.gates(link, h)

                def add_gates(m, b, n):
                    g = n % 2
                    v.wait_ge(g_lo_in[g], 4 * m + n // 2 + 1)
                    nc.vector.tensor_tensor(g_sb[b][:, :, 4 * n:4 * n + 4].rearrange("p i t -> p t i"),
                                            g_ps[g][:, :, 0], g_lo[g][:], ALU.add).then_inc(g_read[g], 1)

                def turn(tb):
                    heads = not is_(tb, TB - 1)
                    v.wait_ge(found_T, tb + 1)
                    nc.vector.tensor_copy(iT[:], g_ps[0][:, 0:2, 0])
                    link(nc.vector.tensor_copy(gT_hi[:], g_ps[0][:, 2, 0]))
                    link(nc.vector.tensor_tensor(gT_lo[:], g_ps[0][:, 2, 0], gT_hi[:].bitcast(F32), ALU.subtract))
                    for q in range(Q):
                        m, b, t0 = tb * Q + q, q % 2, q * GT
                        for g in range(2):
                            wait(v, hot_g_in[g], 4 * (m - 1))
                        nc.vector.tensor_copy(cur[b][:, 0:2], iT[:, :, t0:t0 + GT])
                        nc.vector.tensor_copy(cur[b][:, 2], gT_hi[:, t0:t0 + GT].bitcast(F32))
                        link(nc.vector.tensor_copy(cur[b][:, 3], gT_lo[:, t0:t0 + GT]))
                        for n in range(8):
                            g = n % 2
                            wait(v, g_done[g], 4 * m + n // 2)
                            for hot, side in ((hot2, 1), (hot1, 0)):
                                last = nc.vector.tensor_tensor(hot[g][:], bc(iota[:], 1, 4),
                                                               bc(cur[b][:, side, 4 * n:4 * n + 4], 2, NK),
                                                               ALU.is_equal)
                            last.then_inc(hot_in[g], 1)
                            if heads:
                                top_piece(n % 4, m, n // 4, q * 2 + n // 4)
                            if n == 0:
                                wait(v, g_stored[b], 16 * (2 * tb + q // 2))
                            else:
                                add_gates(m, b, n - 1)
                        add_gates(m, b, 7)
                        chain.restart()
                    if heads:
                        nc.vector.engine_nop().then_inc(found_in, 1)

                turns(v, TB, turn)


def experts_out(nc, d, ahead):
    with ExitStack() as ctx:
        sb, bank, sem = memory(nc, ctx)
        z_in = [ahead.z_in, sb("z_in1", [P, GROUP, T])]
        g_in = [ahead.g_in, sb("g_in1", [P, T // GT, GROUP * GT])]
        v_raw = ahead.v_raw
        v_hi = [sb(f"v_hi{p}", [P, GROUP, D], F32R) for p in range(2)]
        v_lo = [sb(f"v_lo{p}", [P, GROUP, D], F32R) for p in range(2)]
        a_hi, a_lo = sb("a_hi", [P, GROUP, T], F32R), sb("a_lo", [P, GROUP, T], F32R)
        y = sb("y", [P, TB, D])
        st, mv = sb("st5", [P, 2, 6]), sb("mv5", [P, TB, 2])
        var, rstd, minus_half = sb("var5", [P, TB]), sb("rstd5", [P, TB]), sb("minus_half5", [P, 1])
        ln = z_in[0]
        y_ps = [bank(f"y_ps{n}") for n in range(8)]
        rest_here = sem("rest_here")
        z_here = [sem(f"z_here{p}") for p in range(2)]
        v_here = ahead.v_here
        v_hi_in = [sem(f"v_hi_in{e}") for e in range(2)]
        v_lo_in = [sem(f"v_lo_in{e}") for e in range(2)]
        h_here, h_scaled, ln_here = sem("h_here"), sem("h_scaled"), sem("ln_here")
        gelu_in, prod_in, a_hi_in, a_lo_in = sem("gelu_in"), sem("prod_in"), sem("a_hi_in"), sem("a_lo_in")
        y_done = sem("y_done")
        y_read = sem("y_read")
        var_in, rstd_in, y_in, stored = (
            sem("var_in"), sem("rstd_in"), sem("y_in"), sem("stored5"))
        own, own_pool = sem("own_dve5"), sem("own_pool5")

        def groups(step):
            def all_of(eng):
                step(0, 0, 0, True, False)
                step(1, 1, 0, True, True)
                step(2, 0, 1, True, True)
                with eng.Fori(1, NG // 2 - 1) as n:
                    step(2 * n + 1, 1, n, True, True)
                    step(2 * n + 2, 0, n + 1, True, True)
                step(NG - 1, 1, NG // 2 - 1, True, True)
                step(NG, 0, NG // 2, False, True)
            return all_of

        def tokens(s):
            return slice(s * P, (s + 1) * P)

        with nc.Block() as block:

            @block.sync
            def _(sp):
                def load_z(r, p):
                    sp.dma_start(z_in[p][:], d["z"].rearrange("(r i) e t -> r e i t", i=GROUP)[r]).then_inc(z_here[p], 16)
                    sp.dma_start(g_in[p][:], d["gates"].rearrange("c e (r i) t -> r e c (i t)", i=GROUP)[r]).then_inc(
                        z_here[p], 16)

                def load_v(r, first=0):
                    for i in range(first, GROUP):
                        wait(sp, v_lo_in[i % 2], 2 * r + i // 2)
                        sp.dma_start(v_raw[i % 2][:], d["v"][GROUP * r + i]).then_inc(v_here[i % 2], 16)

                c = slice(ahead.GATES_AHEAD // GT, T // GT)
                sp.dma_start(g_in[0][:, c], d["gates"].rearrange("c e i t -> e c (i t)")[:, c, 0:GROUP * GT]
                             ).then_inc(rest_here, 16)
                load_v(0, first=2)
                sp.dma_start(y[:], d["h"].rearrange("n p c -> p n c")).then_inc(h_here, 16)
                load_z(1, 1)
                load_v(1)
                with sp.Fori(0, NG // 2 - 1) as n:
                    for p in range(2):
                        sp.wait_ge(a_lo_in, TB * (2 * n + p + 1))
                        load_z(2 * n + 2 + p, p)
                        load_v(2 * n + 2 + p)
                sp.wait_ge(a_lo_in, TB * (NG - 1))
                sp.dma_start(ln[:, 0], d["ln2_w"]).then_inc(ln_here, 16)
                sp.dma_start(ln[:, 1], d["ln2_b"]).then_inc(ln_here, 16)
                for tb in range(TB):
                    sp.wait_ge(y_in, tb + 1)
                    sp.dma_start(d["out"][tokens(tb)], y[:, tb]).then_inc(stored, 16)
                sp.wait_ge(stored, 16 * TB)

            @block.tensor
            def _(pe):
                def turn(n):
                    for p in range(2):
                        r = 2 * n + p
                        for s in range(TB):
                            pe.wait_ge(a_lo_in, TB * r + s + 1)
                            for a in range(2):
                                bk = (2 * s + a) % 8
                                c = slice(a * 512, (a + 1) * 512)
                                wait(pe, y_read, 16 * r + 2 * s + a - 7)
                                for i in range(GROUP):
                                    if s == 0 and a == 0:
                                        pe.wait_ge(v_lo_in[i % 2], 2 * r + i // 2 + 1)
                                    ah, al = a_hi[:, i, tokens(s)], a_lo[:, i, tokens(s)]
                                    nc.tensor.matmul(y_ps[bk][:], ah, v_hi[p][:, i, c], start=(i == 0), stop=False)
                                    nc.tensor.matmul(y_ps[bk][:], ah, v_lo[p][:, i, c], start=False, stop=False)
                                    last = nc.tensor.matmul(y_ps[bk][:], al, v_hi[p][:, i, c],
                                                            start=False, stop=(i == GROUP - 1))
                                last.then_inc(y_done, 1)

                turns(pe, NG // 2, turn)

            @block.scalar
            def _(act):
                def step(r, p, use, prepare, add):
                    if not prepare:
                        return

                    def hi(s):
                        act.wait_ge(prod_in, TB * r + s + 1)
                        if add:
                            act.wait_ge(y_done, 16 * (r - 1) + 2 * s + 2)
                        nc.scalar.activation(a_hi[:, :, tokens(s)], z_in[p][:, :, tokens(s)],
                                             ACT.Copy).then_inc(a_hi_in, 1)

                    if add:
                        act.wait_ge(z_here[p], 32 * (use + p))
                    else:
                        act.wait_ge(ahead.z_here, 16 * ahead.Z_LOADS)
                        act.wait_ge(rest_here, 16)
                    if add:
                        wait(act, y_done, 16 * (r - 1))
                    for s in range(TB):
                        nc.scalar.activation(z_in[p][:, :, tokens(s)], z_in[p][:, :, tokens(s)],
                                             ACT.Gelu).then_inc(gelu_in, 1)
                        if s % 2 == 0:
                            i = s // 2
                            act.wait_ge(v_here[i % 2], 16 * (2 * r + i // 2 + 1))
                            nc.scalar.activation(v_hi[p][:, i], v_raw[i % 2][:], ACT.Copy).then_inc(v_hi_in[i % 2], 1)
                        if s:
                            hi(s - 1)
                    hi(TB - 1)

                groups(step)(act)

            @block.gpsimd
            def _(pool):
                nc.gpsimd.memset(minus_half[:], -0.5).then_inc(own_pool, 1)
                with pool.Fori(0, NG // 2) as n:
                    for p in range(2):
                        r = 2 * n + p
                        for i in range(GROUP):
                            pool.wait_ge(v_hi_in[i % 2], 2 * r + i // 2 + 1)
                            nc.gpsimd.tensor_tensor(v_lo[p][:, i], v_raw[i % 2][:], v_hi[p][:, i].bitcast(F32),
                                                    ALU.subtract).then_inc(v_lo_in[i % 2], 1)
                pool.wait_ge(own_pool, 1)
                for s in range(TB):
                    pool.wait_ge(var_in, s + 1)
                    nc.gpsimd.tensor_tensor(rstd[:, s:s + 1], var[:, s:s + 1], minus_half[:], ALU.pow
                                            ).then_inc(rstd_in, 1)

            @block.vector
            def _(v):
                chain = Chain(v, own)
                link = chain.link

                def norm(s):
                    link(nc.vector.scalar_tensor_tensor(y[:, s], y[:, s], mv[:, s, 0:1], ln[:, 0],
                                                        ALU.subtract, ALU.mult))
                    v.wait_ge(rstd_in, s + 1)
                    nc.vector.scalar_tensor_tensor(y[:, s], y[:, s], rstd[:, s:s + 1], ln[:, 1],
                                                   ALU.mult, ALU.add).then_inc(y_in, 1)

                def finish(s):
                    v.wait_ge(y_read, 16 * (NG - 1) + 2 * s + 2)
                    for a in range(2):
                        ins = nc.vector.bn_stats(st[:, a], y[:, s, a * 512:(a + 1) * 512])
                    link(ins)
                    link(nc.vector.bn_aggr(mv[:, s], st[:]))
                    nc.vector.tensor_scalar(var[:, s:s + 1], mv[:, s, 1:2], LN_EPS, None, ALU.add).then_inc(var_in, 1)
                    if s == 0:
                        v.wait_ge(ln_here, 32)
                    norm(s)

                def step(r, p, use, prepare, add):
                    def lo(s):
                        v.wait_ge(a_hi_in, TB * r + s + 1)
                        nc.vector.tensor_tensor(a_lo[:, :, tokens(s)], z_in[p][:, :, tokens(s)],
                                                a_hi[:, :, tokens(s)].bitcast(F32), ALU.subtract).then_inc(a_lo_in, 1)

                    for s in range(TB):
                        if prepare:
                            v.wait_ge(gelu_in, TB * r + s + 1)
                            zs = z_in[p][:, :, tokens(s)].rearrange("p i (c t) -> p i c t", t=GT)
                            gs = g_in[p][:, 4 * s:4 * s + 4].rearrange("p c (i t) -> p i c t", t=GT)
                            nc.vector.tensor_tensor(zs, zs, gs, ALU.mult).then_inc(prod_in, 1)
                        if add:
                            for a in range(2):
                                bk = (2 * s + a) % 8
                                c = slice(a * 512, (a + 1) * 512)
                                v.wait_ge(y_done, 16 * (r - 1) + 2 * s + a + 1)
                                nc.vector.tensor_tensor(y[:, s, c], y_ps[bk][:], y[:, s, c], ALU.add).then_inc(
                                    y_read, 1)
                        if prepare and s:
                            lo(s - 1)
                        if not prepare:
                            finish(s)
                    if prepare:
                        lo(TB - 1)
                    if not add:
                        v.wait_ge(h_here, 16)
                        nc.vector.tensor_scalar(y[:], y[:], ALPHA, None, ALU.mult).then_inc(h_scaled, 1)
                        v.wait_ge(h_scaled, 1)

                groups(step)(v)


def build(nc, d):
    project(nc, d)
    with ExitStack() as ctx:
        ahead = Ahead(nc, ctx)
        with ExitStack() as inner:
            hT_hi = inner.enter_context(nc.sbuf_tensor("hT_hi", [P, KT, T], F32R))
            hT_lo = inner.enter_context(nc.sbuf_tensor("hT_lo", [P, KT, T], F32R))
            attend(nc, d, hT_hi, hT_lo, ahead)
            tk = TopK(nc, inner)
            tiles = ExpertTiles(nc, inner)
            score(nc, d, hT_hi, hT_lo, tk, tiles, ahead)
            experts_in(nc, d, hT_hi, hT_lo, tk, tiles, ahead)
        experts_out(nc, d, ahead)


def tables():
    f = np.float32
    pos = np.arange(T, dtype=f)

    def rope(dim):
        inv = f(1.0) / (f(10000.0) ** (np.arange(0, dim, 2, dtype=f) / f(dim)))
        ang = pos[:, None] * inv[None, :]
        both = np.stack([np.cos(ang), np.sin(ang)], axis=1).astype(f)
        return np.ascontiguousarray(both.reshape(TB, P, 2, dim // 2).transpose(1, 0, 2, 3))

    idx = np.arange(P)
    log_g = np.log(1.0 - 2.0 ** (-5.0 - np.arange(RH)))
    diff = idx[:, None] - idx[None, :]
    decay = np.where(diff[None] >= 0, np.exp(np.maximum(diff, 0)[None] * log_g[:, None, None]), 0.0)
    scale = RD ** -0.5
    q, k = np.arange(P)[:, None] + P, np.arange(2 * P)[None, :]
    seen = (q - k >= 0) & (q - k < P)
    return {
        "rope": rope(RD), "rope64": rope(SD),
        "decayT": np.ascontiguousarray(decay.transpose(2, 0, 1) * scale).astype(f),
        "zeta": (np.exp((P - 1.0 - idx)[:, None] * log_g[None]) * scale).astype(f),
        "xi": rows(np.exp((idx + 1.0)[None] * log_g[:, None]).astype(f)),
        "masks": np.stack([np.where(seen & (k >= P), 0.0, NEG), np.where(seen, 0.0, NEG)], axis=1).astype(f),
        "ident": np.eye(P, dtype=f),
        "iota": np.broadcast_to(np.arange(P, dtype=f), (P, P)).copy(),
    }


def rows(a):
    return np.ascontiguousarray(np.broadcast_to(a, (P,) + a.shape))


def kernel(x, w_in, ret_gn_w, swa_sinks, w_out, ln1_w, ln1_b, w_pq, peer_sub_keys,
           peer_u, peer_v, ln2_w, ln2_b):
    import concourse.bacc as bacc
    from concourse.bass_utils import run_bass_kernel_spmd

    a = {k: np.asarray(v) for k, v in dict(
        x=x, w_in=w_in, ret_gn_w=ret_gn_w, swa_sinks=swa_sinks, w_out=w_out, ln1_w=ln1_w, ln1_b=ln1_b,
        w_pq=w_pq, keys=peer_sub_keys, u=peer_u, v=peer_v, ln2_w=ln2_w, ln2_b=ln2_b).items()}
    assert a["x"].shape == (1, T, D) and a["w_in"].shape == (1, D, COLS)

    def slices(w):
        return np.ascontiguousarray(w.reshape(KT, P, -1).transpose(1, 0, 2))

    heads = [g * G + n for n in range(G) for g in range(KVH)]
    cols = np.concatenate([np.arange(4 * RW)] + [4 * RW + h * SD + np.arange(SD) for h in heads]
                          + [np.arange(4 * RW + SW, COLS)])
    arrays = {
        "x": a["x"][0],
        "xT": slices(a["x"][0].T),
        "w_in": slices(a["w_in"][0][:, cols]),
        "w_out": slices(a["w_out"][0]),
        "w_pq": np.ascontiguousarray(a["w_pq"][0].reshape(KT, P, PAIRS, P).transpose(2, 1, 0, 3)),
        "keysT": np.ascontiguousarray(a["keys"][0].reshape(PAIRS, NK, P).transpose(2, 0, 1)),
        "uT": np.ascontiguousarray(a["u"][0].reshape(NK, NK, KT, P).transpose(0, 3, 2, 1)),
        "v": a["v"][0].reshape(NK, NK, D),
        "gn_w": rows(a["ret_gn_w"][0]), "sinks": rows(a["swa_sinks"][0]),
        "ln1_w": rows(a["ln1_w"][0]), "ln1_b": rows(a["ln1_b"][0]),
        "ln2_w": rows(a["ln2_w"][0]), "ln2_b": rows(a["ln2_b"][0]),
        **tables(),
    }
    nc = bacc.Bacc("TRN2", target_bir_lowering=False, num_devices=1)
    d = {n: nc.dram_tensor(f"in_{n}", t.shape, F32, kind="ExternalInput").ap() for n, t in arrays.items()}
    for n, shape in (("proj", (T, COLS)), ("h", (TB, P, D)), ("scores", (TB, PH, P, 2 * NK)),
                     ("z", (NK, P, T)), ("gates", (T // GT, P, NK, GT))):
        d[n] = nc.dram_tensor(n, shape, F32, kind="Internal").ap()
    d["out"] = nc.dram_tensor("out", (T, D), F32, kind="ExternalOutput").ap()
    build(nc, d)
    r = run_bass_kernel_spmd(nc, [{f"in_{n}": t for n, t in arrays.items()}], core_ids=[0])
    return r.results[0]["out"].reshape(1, T, D)
```
